# Optimizing a Trainium2 kernel written in Bass

```python
import math
import jax, jax.numpy as jnp
from jax import lax
import numpy as np

D_MODEL = 1024
BATCH = 1
SEQ = 2048
DEPTH = 1

N_MIXERS = 3
NORM_EPS = 1e-6

RW_HEAD = 64
RW_HEADS = D_MODEL // RW_HEAD
RW_WIDTH = RW_HEADS * RW_HEAD
RW_DECAY_RANK = 64
RW_AAA_RANK = 64
RW_VRES_RANK = 32
RW_GN_EPS = 64e-5

SSD_EXPAND = 2
SSD_WIDTH = SSD_EXPAND * D_MODEL
SSD_HEAD = 64
SSD_HEADS = SSD_WIDTH // SSD_HEAD
SSD_GROUPS = 8
SSD_STATE = 128
SSD_CONV = 4
SSD_CHUNK = 128
SSD_CONV_DIM = SSD_WIDTH + 2 * SSD_GROUPS * SSD_STATE

SB_HEAD = 64
SB_HEADS = D_MODEL // SB_HEAD
SB_WIDTH = SB_HEADS * SB_HEAD
SB_BLOCK = 128
SB_SCALE = 1.0 / math.sqrt(SB_HEAD)


def rms_norm(u, g, eps=NORM_EPS):
    u32 = u.astype(jnp.float32)
    y = u32 * lax.rsqrt(jnp.mean(u32 * u32, axis=-1, keepdims=True) + eps)
    return (y * g.astype(jnp.float32)).astype(u.dtype)

def token_shift(h):
    return jnp.pad(h, ((0, 0), (1, 0), (0, 0)))[:, :-1]

def rwkv7_mixer(h, p, v_first):
    mu, w_in, w_up, w0, a_up, a0, k_k, k_a, r_k, gn_w, gn_b, w_out = p[:12]
    Bsz, T, _ = h.shape
    W, H, N = RW_WIDTH, RW_HEADS, RW_HEAD
    dx = token_shift(h) - h
    x_r, x_w, x_k, x_v, x_a, x_g = (h + dx * mu[i] for i in range(6))
    c = np.cumsum([0, W, W, W, W, RW_DECAY_RANK, RW_AAA_RANK])
    r = x_r @ w_in[:, c[0]:c[1]]
    k = x_k @ w_in[:, c[1]:c[2]]
    v = x_v @ w_in[:, c[2]:c[3]]
    g = jax.nn.silu(x_g @ w_in[:, c[3]:c[4]])
    w_lo = jnp.tanh(x_w @ w_in[:, c[4]:c[5]])
    a_lo = x_a @ w_in[:, c[5]:c[6]]
    f32 = jnp.float32
    w_raw = (w0 + w_lo @ w_up).astype(f32)
    log_decay = -jnp.exp(-jax.nn.softplus(-w_raw) - 0.5)
    a = jax.nn.sigmoid((a0 + a_lo @ a_up).astype(f32))
    if v_first is None:
        v_first = v
    else:
        v_up, v0 = p[12:]
        v_lo = x_v @ w_in[:, c[6]:]
        v = v + (v_first - v) * jax.nn.sigmoid(v0 + v_lo @ v_up)

    def heads(t):
        return t.astype(f32).reshape(Bsz, T, H, N)

    kk = heads(k * k_k)
    kk = kk / jnp.maximum(jnp.sqrt(jnp.sum(kk * kk, axis=-1, keepdims=True)), 1e-12)
    k = k.astype(f32) * (1.0 + (a - 1.0) * k_a.astype(f32))
    r_h, k_h, v_h, a_h = heads(r), heads(k), heads(v), heads(a)
    decay_h = jnp.exp(heads(log_decay))

    def step(S, inp):
        r_t, w_t, k_t, v_t, kk_t, a_t = inp
        sa = jnp.einsum('bhvk,bhk->bhv', S, -kk_t)
        S = (S * w_t[:, :, None, :]
             + sa[..., None] * (kk_t * a_t)[:, :, None, :]
             + v_t[..., None] * k_t[:, :, None, :])
        y_t = jnp.einsum('bhvk,bhk->bhv', S, r_t)
        return S, y_t

    tm = lambda t: jnp.moveaxis(t, 1, 0)
    S0 = jnp.zeros((Bsz, H, N, N), f32)
    _, y = lax.scan(step, S0, (tm(r_h), tm(decay_h), tm(k_h), tm(v_h), tm(kk), tm(a_h)))
    y = jnp.moveaxis(y, 0, 1)
    mean = jnp.mean(y, axis=-1, keepdims=True)
    var = jnp.mean(jnp.square(y - mean), axis=-1, keepdims=True)
    y = (y - mean) * lax.rsqrt(var + RW_GN_EPS)
    y = y * gn_w.astype(f32).reshape(H, N) + gn_b.astype(f32).reshape(H, N)
    y = y + jnp.sum(r_h * k_h * r_k.astype(f32), axis=-1, keepdims=True) * v_h
    y = y.reshape(Bsz, T, W).astype(h.dtype) * g
    return y @ w_out, v_first

def causal_depthwise_conv(u, w, b):
    out = lax.conv_general_dilated(
        u, w[:, None, :].astype(u.dtype), window_strides=(1,),
        padding=[(w.shape[0] - 1, 0)], dimension_numbers=('NWC', 'WIO', 'NWC'),
        feature_group_count=u.shape[-1])
    return out + b

def ssd_chunked(x, a, Bm, Cm):
    Bsz, T, H, P = x.shape
    G, R, l = SSD_GROUPS, H // SSD_GROUPS, SSD_CHUNK
    nc = T // l
    x = x.reshape(Bsz, nc, l, G, R, P)
    Bm = Bm.reshape(Bsz, nc, l, G, SSD_STATE)
    Cm = Cm.reshape(Bsz, nc, l, G, SSD_STATE)
    ac = jnp.cumsum(jnp.moveaxis(a.reshape(Bsz, nc, l, G, R), 2, -1), axis=-1)
    causal = jnp.tril(jnp.ones((l, l), bool))
    seg = ac[..., :, None] - ac[..., None, :]
    decay_in = jnp.exp(jnp.where(causal, seg, -jnp.inf))
    cb = jnp.einsum('bclgn,bcsgn->bcgls', Cm, Bm)
    y_diag = jnp.einsum('bcgrls,bcsgrp->bclgrp', cb[:, :, :, None] * decay_in, x)
    decay_states = jnp.moveaxis(jnp.exp(ac[..., -1:] - ac), -1, 2)
    states = jnp.einsum('bclgn,bclgrp->bcgrpn', Bm, x * decay_states[..., None])
    chunk_decay = ac[..., -1]

    def chunk_step(h_prev, inp):
        st, dec = inp
        return h_prev * jnp.exp(dec)[..., None, None] + st, h_prev

    h0 = jnp.zeros((Bsz, G, R, P, SSD_STATE), x.dtype)
    _, h_in = lax.scan(chunk_step, h0, (jnp.moveaxis(states, 1, 0), jnp.moveaxis(chunk_decay, 1, 0)))
    h_in = jnp.moveaxis(h_in, 0, 1)
    decay_out = jnp.moveaxis(jnp.exp(ac), -1, 2)
    y_off = jnp.einsum('bclgn,bcgrpn->bclgrp', Cm, h_in) * decay_out[..., None]
    return (y_diag + y_off).reshape(Bsz, T, H, P)

def mamba2_mixer(h, p):
    w_in, conv_w, conv_b, dt_bias, a_log, d_skip, gnorm_w, w_out = p
    Bsz, T, _ = h.shape
    f32 = jnp.float32
    proj = h @ w_in
    z = proj[..., :SSD_WIDTH]
    xbc = proj[..., SSD_WIDTH:SSD_WIDTH + SSD_CONV_DIM]
    dt_raw = proj[..., SSD_WIDTH + SSD_CONV_DIM:]
    xbc = jax.nn.silu(causal_depthwise_conv(xbc, conv_w, conv_b)).astype(f32)
    gn = SSD_GROUPS * SSD_STATE
    xs = xbc[..., :SSD_WIDTH].reshape(Bsz, T, SSD_HEADS, SSD_HEAD)
    Bm = xbc[..., SSD_WIDTH:SSD_WIDTH + gn].reshape(Bsz, T, SSD_GROUPS, SSD_STATE)
    Cm = xbc[..., SSD_WIDTH + gn:].reshape(Bsz, T, SSD_GROUPS, SSD_STATE)
    dt = jax.nn.softplus((dt_raw + dt_bias).astype(f32))
    A = -jnp.exp(a_log.astype(f32))
    y = ssd_chunked(xs * dt[..., None], dt * A, Bm, Cm)
    y = y + xs * d_skip.astype(f32)[:, None]
    y = y.reshape(Bsz, T, SSD_WIDTH) * jax.nn.silu(z.astype(f32))
    y = y.reshape(Bsz, T, SSD_GROUPS, SSD_WIDTH // SSD_GROUPS)
    y = y * lax.rsqrt(jnp.mean(y * y, axis=-1, keepdims=True) + NORM_EPS)
    y = y.reshape(Bsz, T, SSD_WIDTH) * gnorm_w.astype(f32)
    return y.astype(h.dtype) @ w_out

def stick_breaking_mixer(h, p):
    w_in, q_norm, k_norm, w_out = p
    Bsz, T, _ = h.shape
    f32 = jnp.float32
    proj = h @ w_in
    W = SB_WIDTH
    q = rms_norm(proj[..., :W].reshape(Bsz, T, SB_HEADS, SB_HEAD), q_norm).astype(f32)
    k = rms_norm(proj[..., W:2 * W].reshape(Bsz, T, SB_HEADS, SB_HEAD), k_norm).astype(f32)
    v = proj[..., 2 * W:3 * W].reshape(Bsz, T, SB_HEADS, SB_HEAD).astype(f32)
    g = jax.nn.silu(proj[..., 3 * W:])
    outs = []
    for blk in range(T // SB_BLOCK):
        start, end = blk * SB_BLOCK, (blk + 1) * SB_BLOCK
        qb, kb, vb = q[:, start:end], k[:, :end], v[:, :end]
        z = jnp.einsum('bthd,bshd->bhts', qb, kb) * SB_SCALE
        t_idx = start + jnp.arange(SB_BLOCK)
        s_idx = jnp.arange(end)
        strict = s_idx[None, :] < t_idx[:, None]
        log_beta = jax.nn.log_sigmoid(z)
        log_1m_beta = jnp.where(strict, log_beta - z, 0.0)
        tail = lax.cumsum(log_1m_beta, axis=3, reverse=True) - log_1m_beta
        att = jnp.where(strict, jnp.exp(log_beta + tail), 0.0)
        outs.append(jnp.einsum('bhts,bshd->bthd', att, vb))
    o = jnp.concatenate(outs, axis=1).reshape(Bsz, T, W).astype(h.dtype)
    return (o * g) @ w_out

def _normal(key, shape, scale):
    return scale * jax.random.normal(key, shape, jnp.float32)

def _rwkv_params(key, prefix, value_residual):
    ks = jax.random.split(key, 16)
    W = RW_WIDTH
    n_cols = 4 * W + RW_DECAY_RANK + RW_AAA_RANK + (RW_VRES_RANK if value_residual else 0)
    p = {
        prefix + "norm": 1.0 + _normal(ks[0], (D_MODEL,), 0.05),
        prefix + "mu": jax.random.uniform(ks[1], (6, D_MODEL), jnp.float32),
        prefix + "w_in": _normal(ks[2], (D_MODEL, n_cols), D_MODEL ** -0.5),
        prefix + "w_up": _normal(ks[3], (RW_DECAY_RANK, W), 0.5 * RW_DECAY_RANK ** -0.5),
        prefix + "w0": jax.random.uniform(ks[4], (W,), jnp.float32, -6.0, 1.0),
        prefix + "a_up": _normal(ks[5], (RW_AAA_RANK, W), 0.5 * RW_AAA_RANK ** -0.5),
        prefix + "a0": _normal(ks[6], (W,), 0.5),
        prefix + "k_k": 0.85 + _normal(ks[7], (W,), 0.05),
        prefix + "k_a": 1.0 + _normal(ks[8], (W,), 0.05),
        prefix + "r_k": _normal(ks[9], (RW_HEADS, RW_HEAD), 0.1),
        prefix + "gn_w": 1.0 + _normal(ks[10], (W,), 0.05),
        prefix + "gn_b": _normal(ks[11], (W,), 0.01),
        prefix + "w_out": _normal(ks[12], (W, D_MODEL), W ** -0.5),
    }
    if value_residual:
        p[prefix + "v_up"] = _normal(ks[13], (RW_VRES_RANK, W), 0.5 * RW_VRES_RANK ** -0.5)
        p[prefix + "v0"] = _normal(ks[14], (W,), 0.5)
    return p

def _mamba2_params(key, prefix):
    ks = jax.random.split(key, 10)
    n_cols = SSD_WIDTH + SSD_CONV_DIM + SSD_HEADS
    dt = jnp.exp(jax.random.uniform(ks[4], (SSD_HEADS,), jnp.float32, math.log(1e-3), math.log(1e-1)))
    return {
        prefix + "norm": 1.0 + _normal(ks[0], (D_MODEL,), 0.05),
        prefix + "w_in": _normal(ks[1], (D_MODEL, n_cols), D_MODEL ** -0.5),
        prefix + "conv_w": _normal(ks[2], (SSD_CONV, SSD_CONV_DIM), SSD_CONV ** -0.5),
        prefix + "conv_b": _normal(ks[3], (SSD_CONV_DIM,), 0.01),
        prefix + "dt_bias": dt + jnp.log(-jnp.expm1(-dt)),
        prefix + "a_log": jnp.log(jax.random.uniform(ks[5], (SSD_HEADS,), jnp.float32, 1.0, 16.0)),
        prefix + "d_skip": 1.0 + _normal(ks[6], (SSD_HEADS,), 0.05),
        prefix + "gnorm_w": 1.0 + _normal(ks[7], (SSD_WIDTH,), 0.05),
        prefix + "w_out": _normal(ks[8], (SSD_WIDTH, D_MODEL), SSD_WIDTH ** -0.5),
    }

def _stickbreak_params(key, prefix):
    ks = jax.random.split(key, 5)
    return {
        prefix + "norm": 1.0 + _normal(ks[0], (D_MODEL,), 0.05),
        prefix + "w_in": _normal(ks[1], (D_MODEL, 4 * SB_WIDTH), D_MODEL ** -0.5),
        prefix + "q_norm": 1.0 + _normal(ks[2], (SB_HEAD,), 0.05),
        prefix + "k_norm": 1.0 + _normal(ks[3], (SB_HEAD,), 0.05),
        prefix + "w_out": _normal(ks[4], (SB_WIDTH, D_MODEL), SB_WIDTH ** -0.5),
    }

def first_inputs(seed: int = 0) -> dict:
    key = jax.random.key(seed)
    kx, k0, k1, k2, k3 = jax.random.split(key, 5)
    inputs = {"x": jax.random.normal(kx, (BATCH, SEQ, D_MODEL), jnp.float32)}
    inputs.update(_rwkv_params(k0, "l0_", value_residual=False))
    inputs.update(_mamba2_params(k1, "l1_"))
    inputs.update(_stickbreak_params(k2, "l2_"))
    inputs.update(_rwkv_params(k3, "l3_", value_residual=True))
    return inputs

def first_block(x,
              l0_norm, l0_mu, l0_w_in, l0_w_up, l0_w0, l0_a_up, l0_a0, l0_k_k, l0_k_a, l0_r_k,
              l0_gn_w, l0_gn_b, l0_w_out,
              l1_norm, l1_w_in, l1_conv_w, l1_conv_b, l1_dt_bias, l1_a_log, l1_d_skip, l1_gnorm_w,
              l1_w_out,
              l2_norm, l2_w_in, l2_q_norm, l2_k_norm, l2_w_out,
              l3_norm, l3_mu, l3_w_in, l3_w_up, l3_w0, l3_a_up, l3_a0, l3_k_k, l3_k_a, l3_r_k,
              l3_gn_w, l3_gn_b, l3_w_out, l3_v_up, l3_v0):
    layer_params = [
        (l0_norm, (l0_mu, l0_w_in, l0_w_up, l0_w0, l0_a_up, l0_a0, l0_k_k, l0_k_a, l0_r_k,
                   l0_gn_w, l0_gn_b, l0_w_out)),
        (l1_norm, (l1_w_in, l1_conv_w, l1_conv_b, l1_dt_bias, l1_a_log, l1_d_skip, l1_gnorm_w,
                   l1_w_out)),
        (l2_norm, (l2_w_in, l2_q_norm, l2_k_norm, l2_w_out)),
        (l3_norm, (l3_mu, l3_w_in, l3_w_up, l3_w0, l3_a_up, l3_a0, l3_k_k, l3_k_a, l3_r_k,
                   l3_gn_w, l3_gn_b, l3_w_out, l3_v_up, l3_v0)),
    ]
    v_first = None
    for i in range(DEPTH):
        norm_g, p = layer_params[i]
        h = rms_norm(x, norm_g)
        kind = i % N_MIXERS
        if kind == 0:
            y, v_first = rwkv7_mixer(h, p, v_first)
        elif kind == 1:
            y = mamba2_mixer(h, p)
        else:
            y = stick_breaking_mixer(h, p)
        x = x + y.astype(x.dtype)
    return x


MIX_WIDTH = D_MODEL
CONV_WIDTH = MIX_WIDTH // 2
ATTN_HEADS = 8
HEAD_DIM = (MIX_WIDTH - CONV_WIDTH) // ATTN_HEADS
ATTN_WIDTH = ATTN_HEADS * HEAD_DIM
CONV_K = 3
DILATED_CONFIGS = ((128, 1), (512, 4), (2048, 16))
Q_BLOCK = 128
NUM_BUCKETS = 32
MAX_DISTANCE = 1024
EPS = 1e-6
NEG = -1e30


def rmsnorm(x, w):
    xf = x.astype(jnp.float32)
    y = xf * lax.rsqrt(jnp.mean(xf * xf, axis=-1, keepdims=True) + EPS)
    return (y * w.astype(jnp.float32)).astype(x.dtype)

def t5_bucket(rel):
    half_b = NUM_BUCKETS // 2
    max_exact = half_b // 2
    ret = jnp.where(rel > 0, half_b, 0)
    n = jnp.abs(rel)
    nf = jnp.maximum(n, 1).astype(jnp.float32)
    large = max_exact + (jnp.log(nf / max_exact) / math.log(MAX_DISTANCE / max_exact)
                         * (half_b - max_exact)).astype(jnp.int32)
    large = jnp.minimum(large, half_b - 1)
    return ret + jnp.where(n < max_exact, n, large)

def dilated_window_attention(q, k, v, rel_bias, window, dilation):
    b, s, nh, dh = q.shape
    half = window // (2 * dilation)
    length = s // dilation
    n_blk = -(-length // Q_BLOCK)
    padded = n_blk * Q_BLOCK
    kb_len = Q_BLOCK + 2 * half
    bd = b * dilation

    def to_residue(t):
        t = t.reshape(b, length, dilation, nh, dh)
        return t.transpose(0, 2, 3, 1, 4).reshape(bd, nh, length, dh)

    qr = jnp.pad(to_residue(q), ((0, 0), (0, 0), (0, padded - length), (0, 0)))
    qr = qr.reshape(bd, nh, n_blk, Q_BLOCK, dh)
    pad_kv = ((0, 0), (0, 0), (half, padded - length + half), (0, 0))
    kr = jnp.pad(to_residue(k), pad_kv)
    vr = jnp.pad(to_residue(v), pad_kv)

    key_idx = jnp.arange(n_blk)[:, None] * Q_BLOCK + jnp.arange(kb_len)[None, :]
    kblk = kr[:, :, key_idx]
    vblk = vr[:, :, key_idx]

    logits = jnp.einsum('bhnqd,bhnkd->bhnqk', qr, kblk,
                        preferred_element_type=jnp.float32) * (dh ** -0.5)

    rel = jnp.arange(kb_len)[None, :] - half - jnp.arange(Q_BLOCK)[:, None]
    band = jnp.abs(rel) <= half
    buckets = t5_bucket(jnp.clip(rel, -half, half) * dilation)
    bias = rel_bias[buckets].astype(jnp.float32).transpose(2, 0, 1)
    key_pos = key_idx - half
    key_ok = (key_pos >= 0) & (key_pos < length)
    mask = band[None, :, :] & key_ok[:, None, :]
    logits = jnp.where(mask[None, None], logits + bias[None, :, None], NEG)

    m = jnp.max(logits, axis=-1, keepdims=True)
    p = jnp.exp(logits - m)
    denom = jnp.sum(p, axis=-1, keepdims=True)
    o = jnp.einsum('bhnqk,bhnkd->bhnqd', p, vblk.astype(jnp.float32)) / denom
    lse = (m + jnp.log(denom))[..., 0]

    o = o.reshape(bd, nh, padded, dh)[:, :, :length]
    o = o.reshape(b, dilation, nh, length, dh).transpose(0, 3, 1, 2, 4).reshape(b, s, nh, dh)
    lse = lse.reshape(bd, nh, padded)[:, :, :length]
    lse = lse.reshape(b, dilation, nh, length).transpose(0, 3, 1, 2).reshape(b, s, nh)
    return o, lse

def short_gated_conv(u, gate_b, gate_c, conv_w, conv_b):
    pad = (CONV_K - 1) // 2
    z = lax.conv_general_dilated(gate_c * u, conv_w[:, None, :].astype(u.dtype),
                                 window_strides=(1,), padding=((pad, pad),),
                                 dimension_numbers=('NWC', 'WIO', 'NWC'),
                                 feature_group_count=CONV_WIDTH)
    return gate_b * (z + conv_b.astype(u.dtype))

def second_inputs(seed: int = 0) -> dict:
    key = jax.random.key(seed)
    ks = jax.random.split(key, 9)
    proj_cols = 4 * CONV_WIDTH + 4 * ATTN_WIDTH
    x = jax.random.normal(ks[0], (BATCH, SEQ, D_MODEL), jnp.float32)
    norm_w = 1.0 + 0.05 * jax.random.normal(ks[1], (D_MODEL,), jnp.float32)
    w_in = jax.random.normal(ks[2], (D_MODEL, proj_cols), jnp.float32) * D_MODEL ** -0.5
    conv_w = jax.random.normal(ks[3], (CONV_K, CONV_WIDTH), jnp.float32) * CONV_K ** -0.5
    conv_b = 0.01 * jax.random.normal(ks[4], (CONV_WIDTH,), jnp.float32)
    q_norm_w = 1.0 + 0.05 * jax.random.normal(ks[5], (HEAD_DIM,), jnp.float32)
    k_norm_w = 1.0 + 0.05 * jax.random.normal(ks[6], (HEAD_DIM,), jnp.float32)
    rel_bias = 0.5 * jax.random.normal(ks[7], (NUM_BUCKETS, ATTN_HEADS), jnp.float32)
    w_out = jax.random.normal(ks[8], (MIX_WIDTH, D_MODEL), jnp.float32) * MIX_WIDTH ** -0.5
    return {"x": x, "norm_w": norm_w, "w_in": w_in, "conv_w": conv_w, "conv_b": conv_b,
            "q_norm_w": q_norm_w, "k_norm_w": k_norm_w, "rel_bias": rel_bias, "w_out": w_out}

def second_block(x, norm_w, w_in, conv_w, conv_b, q_norm_w, k_norm_w, rel_bias, w_out):
    b, s, _ = x.shape
    for _layer in range(DEPTH):
        h = rmsnorm(x, norm_w)
        proj = jnp.einsum('bsd,de->bse', h, w_in)
        c, a = CONV_WIDTH, ATTN_WIDTH
        splits = [c, 2 * c, 3 * c, 4 * c, 4 * c + a, 4 * c + 2 * a, 4 * c + 3 * a]
        u, g_b, g_c, z_conv, q, k, v, z_attn = jnp.split(proj, splits, axis=-1)

        y_conv = short_gated_conv(u, g_b, g_c, conv_w, conv_b) * jax.nn.silu(z_conv)

        q = rmsnorm(q.reshape(b, s, ATTN_HEADS, HEAD_DIM), q_norm_w)
        k = rmsnorm(k.reshape(b, s, ATTN_HEADS, HEAD_DIM), k_norm_w)
        v = v.reshape(b, s, ATTN_HEADS, HEAD_DIM)
        outs, lses = [], []
        for window, dilation in DILATED_CONFIGS:
            o_i, lse_i = dilated_window_attention(q, k, v, rel_bias, window, dilation)
            outs.append(o_i)
            lses.append(lse_i)
        mix = jax.nn.softmax(jnp.stack(lses, axis=0), axis=0)
        o = jnp.einsum('gbsh,gbshd->bshd', mix, jnp.stack(outs, axis=0))
        y_attn = o.reshape(b, s, ATTN_WIDTH).astype(x.dtype) * jax.nn.silu(z_attn)

        y = jnp.concatenate([y_conv, y_attn], axis=-1)
        x = x + jnp.einsum('bse,ed->bsd', y, w_out)
    return x


def setup_inputs(seed=0):
    out = dict(first_inputs(seed))
    for name, value in second_inputs(seed + 1).items():
        if name != "x":
            out[name + "_2"] = value
    return out


def reference(
    x, l0_norm, l0_mu, l0_w_in, l0_w_up, l0_w0, l0_a_up, l0_a0, l0_k_k, l0_k_a, l0_r_k, l0_gn_w,
    l0_gn_b, l0_w_out, l1_norm, l1_w_in, l1_conv_w, l1_conv_b, l1_dt_bias, l1_a_log, l1_d_skip,
    l1_gnorm_w, l1_w_out, l2_norm, l2_w_in, l2_q_norm, l2_k_norm, l2_w_out, l3_norm, l3_mu,
    l3_w_in, l3_w_up, l3_w0, l3_a_up, l3_a0, l3_k_k, l3_k_a, l3_r_k, l3_gn_w, l3_gn_b, l3_w_out,
    l3_v_up, l3_v0, norm_w_2, w_in_2, conv_w_2, conv_b_2, q_norm_w_2, k_norm_w_2, rel_bias_2,
    w_out_2,
):
    x = first_block(
        x, l0_norm, l0_mu, l0_w_in, l0_w_up, l0_w0, l0_a_up, l0_a0, l0_k_k, l0_k_a, l0_r_k,
        l0_gn_w, l0_gn_b, l0_w_out, l1_norm, l1_w_in, l1_conv_w, l1_conv_b, l1_dt_bias,
        l1_a_log, l1_d_skip, l1_gnorm_w, l1_w_out, l2_norm, l2_w_in, l2_q_norm, l2_k_norm,
        l2_w_out, l3_norm, l3_mu, l3_w_in, l3_w_up, l3_w0, l3_a_up, l3_a0, l3_k_k, l3_k_a,
        l3_r_k, l3_gn_w, l3_gn_b, l3_w_out, l3_v_up, l3_v0,
    )
    return second_block(
        x, norm_w_2, w_in_2, conv_w_2, conv_b_2, q_norm_w_2, k_norm_w_2, rel_bias_2, w_out_2,
    )


_drawn_inputs = setup_inputs


def setup_inputs(seed=0):
    import zlib

    import numpy as np

    out = dict(_drawn_inputs(seed))
    spreads = {}
    factors = {'l0_w_up': 4.522,
     'l0_gn_b': 8.0,
     'conv_b_2': 8.0,
     'q_norm_w_2': 8.0,
     'k_norm_w_2': 8.0,
     'rel_bias_2': 3.568}
    for name, (base, spread) in spreads.items():
        noise = np.random.default_rng([zlib.crc32(name.encode()), seed]).standard_normal(out[name].shape)
        drawn = base * np.exp(spread * noise) if base else spread * noise
        out[name] = __import__('jax').numpy.asarray(drawn.astype(out[name].dtype))
    for name, factor in factors.items():
        out[name] = (out[name] * factor).astype(out[name].dtype)
    return out
```

```python
import math
from contextlib import ExitStack

import numpy as np
import concourse.bass as bass
from concourse import mybir

F32 = mybir.dt.float32
F16 = mybir.dt.float16
ALU = mybir.AluOpType
ACT = mybir.ActivationFunctionType
AX = mybir.AxisListType
ds = bass.ds

T = 2048
D = 1024
KT = D // 128
HALF = T // 2
HB = HALF // 512
RANK = 64
EPS = 1e-6

VEC_NAMES = ["norm1", "mu_r", "mu_k", "mu_v", "mu_g", "mu_w", "mu_a", "w0", "a0", "k_k", "k_a", "r_k",
             "gn_w", "gn_b", "norm2"]
V = {n: KT * i for i, n in enumerate(VEC_NAMES)}
NVEC = KT * len(VEC_NAMES)


class Semaphores:

    def __init__(self, nc, scope):
        self.nc, self.made = nc, []
        scope.callback(self.clear)

    def new(self, name):
        self.made.append(self.nc.alloc_semaphore(name))
        return self.made[-1]

    def clear(self):
        self.nc.clear_and_free_semaphores(self.made)
        self.nc.all_engine_barrier()


def firm_wait(eng, sem, value, passed):
    eng.wait_ge(sem, value)
    eng.sem_inc(passed, 1)


class Place:

    def __init__(self, eng, sems, per, t, ahead=1):
        self.eng, self.sems, self.per, self.t, self.ahead, self.sent = eng, sems, per, t, ahead, {}
        self.firm = False

    def settle(self):
        self.firm = True

    def back(self, steps, name, k):
        per = self.per[name]
        value = self.t * per + ((self.ahead - steps) * per + (per if k is None else k))
        if self.firm and not isinstance(value, int):
            firm_wait(self.eng, self.sems[name], value, self.sems["passed"])
        else:
            self.eng.wait_ge(self.sems[name], value)

    def need(self, name, k=None):
        self.back(0, name, k)

    def prev1(self, name, k=None):
        self.back(1, name, k)

    def prev(self, name, k=None):
        self.back(self.ahead, name, k)

    def did(self, ins, name, by=1):
        ins.then_inc(self.sems[name], by)
        self.firm = False
        self.sent[name] = self.sent.get(name, 0) + by

    def end(self):
        for n, k in self.sent.items():
            assert k == self.per[n], (n, k)


def norm_phase(nc, name, src, h, gain, ones):
    NB = T // 512
    with ExitStack() as c:
        sems = Semaphores(nc, c)
        sq = [c.enter_context(nc.sbuf_tensor(f"{name}_sq{i}", [128, 512], F32)) for i in range(4)]
        var = c.enter_context(nc.sbuf_tensor(f"{name}_var", [128, T], F32))
        rstd = c.enter_context(nc.sbuf_tensor(f"{name}_rstd", [128, T], F32))
        total = [c.enter_context(nc.psum_tensor(f"{name}_total{i}", [128, 512], F32)) for i in range(NB)]
        loaded = [sems.new(f"{name}_loaded{k}") for k in range(KT)]
        squared = sems.new(f"{name}_squared")
        summed = sems.new(f"{name}_summed")
        meaned = sems.new(f"{name}_meaned")
        rooted = sems.new(f"{name}_rooted")
        inverted = sems.new(f"{name}_inverted")
        block = c.enter_context(nc.Block())

        @block.sync
        def _(sp):
            for k in range(KT):
                if src is not None:
                    sp.dma_start(h[:, k, :], src[:, k, :]).then_inc(loaded[k], 16)

        @block.scalar
        def _(act):
            for b in range(NB):
                for k in range(KT):
                    n = b * KT + k
                    if src is not None:
                        act.wait_ge(loaded[k], 16)
                    if n >= 4:
                        act.wait_ge(summed, n - 3)
                    act.activation(sq[n % 4][:], h[:, k, 512 * b:512 * b + 512], ACT.Square).then_inc(squared, 1)
            for b in range(NB):
                act.wait_ge(meaned, b + 1)
                act.activation(rstd[:, 512 * b:512 * b + 512], var[:, 512 * b:512 * b + 512],
                               ACT.Sqrt).then_inc(rooted, 1)

        @block.tensor
        def _(pe):
            for b in range(NB):
                for k in range(KT):
                    pe.wait_ge(squared, b * KT + k + 1)
                    pe.matmul(total[b][:], ones[:], sq[(b * KT + k) % 4][:],
                              start=k == 0, stop=k == KT - 1).then_inc(summed, 1)

        @block.vector
        def _(dve):
            for b in range(NB):
                dve.wait_ge(summed, KT * (b + 1))
                dve.tensor_scalar(var[:, 512 * b:512 * b + 512], total[b][:], 1.0 / D, EPS,
                                  ALU.mult, ALU.add).then_inc(meaned, 1)
            for b in range(NB):
                col = slice(512 * b, 512 * b + 512)
                dve.wait_ge(rooted, b + 1)
                dve.reciprocal(var[:, col], rstd[:, col]).then_inc(inverted, 1)
                dve.wait_ge(inverted, b + 1)
                for k in range(KT):
                    dve.scalar_tensor_tensor(h[:, k, col], h[:, k, col], gain[:, k:k + 1], var[:, col],
                                             ALU.mult, ALU.mult)


def rwkv_projections(nc, h, vec, w_in, w_up, a_up, proj):
    with ExitStack() as c:
        sems = Semaphores(nc, c)
        def sb(n, shape, dt=F32):
            return c.enter_context(nc.sbuf_tensor(f"pj_{n}", shape, dt))

        def sem(n):
            return sems.new(f"pj_{n}")

        xs = [sb(f"xs{i}", [128, KT, HALF]) for i in range(2)]
        diff = [sb(f"diff{i}", [128, HALF]) for i in range(2)]
        w = [sb(f"w{i}", [128, KT, 128]) for i in range(2)]
        out_sb = [sb(f"out{i}", [128, HALF]) for i in range(2)]
        lo_w = sb("lo_w", [128, KT, 2 * RANK])
        lo = [sb(f"lo{i}", [RANK, T]) for i in range(2)]
        up = [sb(f"up{i}", [RANK, D]) for i in range(2)]
        ps = [c.enter_context(nc.psum_tensor(f"pj_ps{i}", [128, HALF], F32)) for i in range(2)]
        s_diff, s_xs = sem("diff"), sem("xs")
        s_w = [sem(f"w{i}") for i in range(2)]
        s_mm, s_ps_free = sem("mm"), sem("ps_free")
        s_out = [sem(f"out{i}") for i in range(2)]
        s_small, s_passed = sem("small"), sem("passed")
        block = c.enter_context(nc.Block())
        MAIN = 4 * 2 * KT
        w_cols = w_in.rearrange("(k p) n -> p k n", p=128)
        proj_rows = proj.rearrange("q (j p) t -> q p j t", p=128)

        def uses(q, hv):
            return (2 * q + hv + 1) * KT if q < 4 else MAIN + 2 * (q - 4) + hv + 1

        @block.gpsimd
        def _(pool):
            for q in range(6):
                for hv in range(2):
                    for k in range(KT):
                        n = (2 * q + hv) * KT + k
                        if n >= 2:
                            pool.wait_ge(s_xs, n - 1)
                        pool.tensor_tensor(diff[n % 2][:], h[:, k, hv * HALF:hv * HALF + HALF],
                                           h[:, k, hv * HALF + 1:hv * HALF + HALF + 1],
                                           ALU.subtract).then_inc(s_diff, 1)

        @block.vector
        def _(dve):
            for q in range(6):
                for hv in range(2):
                    if q > 0:
                        dve.wait_ge(s_mm, uses(q - 1, hv))
                    for k in range(KT):
                        n = (2 * q + hv) * KT + k
                        m = V["mu_r"] + q * KT + k
                        dve.wait_ge(s_diff, n + 1)
                        dve.scalar_tensor_tensor(xs[hv][:, k, :], diff[n % 2][:], vec[:, m:m + 1],
                                                 h[:, k, hv * HALF + 1:hv * HALF + HALF + 1],
                                                 ALU.mult, ALU.add).then_inc(s_xs, 1)

        @block.sync
        def _(sp):
            def load(i, n2):
                col = (n2 // KT) * D + ((n2 * 2 + i) % KT) * 128
                sp.dma_start(w[i][:], w_cols[:, :, ds(col, 128)]).then_inc(s_w[i], 16)

            for i in range(2):
                load(i, 0)
            sp.dma_start(lo_w[:], w_cols[:, :, 4 * D:4 * D + 2 * RANK]).then_inc(s_small, 16)
            sp.dma_start(up[0][:], w_up).then_inc(s_small, 16)
            sp.dma_start(up[1][:], a_up).then_inc(s_small, 16)
            with sp.Fori(1, MAIN // 2) as n2:
                for i in range(2):
                    sp.wait_ge(s_mm, n2 * 2 + i - 1)
                    load(i, n2)

        @block.tensor
        def _(pe):
            with pe.Fori(0, 4) as q:
                for hv in range(2):
                    firm_wait(pe, s_xs, q * (2 * KT) + (hv + 1) * KT, s_passed)
                    with pe.Fori(0, KT // 2) as c2:
                        for i in range(2):
                            n = q * (2 * KT) + c2 * 2 + (hv * KT + i)
                            pe.wait_ge(s_w[i], q * (16 * KT) + c2 * 16 + (hv * 8 * KT + 16))
                            pe.wait_ge(s_ps_free, n + 1)
                            for k in range(KT):
                                for b in range(HB):
                                    last = pe.matmul(ps[i][:, 512 * b:512 * b + 512], w[i][:, k, :],
                                                     xs[hv][:, k, 512 * b:512 * b + 512],
                                                     start=k == 0, stop=k == KT - 1)
                            last.then_inc(s_mm, 1)
            pe.wait_ge(s_small, 48)
            n = MAIN
            for r in range(2):
                for hv in range(2):
                    pe.wait_ge(s_xs, ((4 + r) * 2 + hv + 1) * KT)
                    pe.wait_ge(s_ps_free, n + 1)
                    for k in range(KT):
                        for b in range(HB):
                            last = pe.matmul(ps[n % 2][0:RANK, 512 * b:512 * b + 512],
                                             lo_w[:, k, r * RANK:(r + 1) * RANK],
                                             xs[hv][:, k, 512 * b:512 * b + 512],
                                             start=k == 0, stop=k == KT - 1)
                    last.then_inc(s_mm, 1)
                    n += 1
            for r in range(2):
                for j in range(KT):
                    for hv in range(2):
                        pe.wait_ge(s_ps_free, MAIN + 2 * r + hv + 3)
                        pe.wait_ge(s_ps_free, n + 1)
                        for b in range(HB):
                            t0 = hv * HALF + 512 * b
                            last = pe.matmul(ps[n % 2][:, 512 * b:512 * b + 512], up[r][:, 128 * j:128 * j + 128],
                                             lo[r][:, t0:t0 + 512], start=True, stop=True)
                        last.then_inc(s_mm, 1)
                        n += 1

        @block.scalar
        def _(act):
            act.sem_inc(s_ps_free, 2)
            act.sem_inc(s_out[0], 16)
            act.sem_inc(s_out[1], 16)

            with act.Fori(0, 4) as q:
                for hv in range(2):
                    with act.Fori(0, KT // 2) as c2:
                        for i in range(2):
                            n = q * (2 * KT) + c2 * 2 + (hv * KT + i)
                            use = q * KT + c2 + hv * (KT // 2)
                            act.wait_ge(s_mm, n + 1)
                            act.wait_ge(s_out[i], use * 16 + 16)
                            act.copy(out_sb[i][:], ps[i][:]).then_inc(s_ps_free, 1)
                            act.wait_ge(s_ps_free, n + 3)
                            act.dma_start(proj_rows[ds(q, 1), :, ds(c2 * 2 + i, 1), hv * HALF:(hv + 1) * HALF]
                                          .rearrange("q p j t -> p (q j t)"), out_sb[i][:]).then_inc(s_out[i], 16)
            n = MAIN
            for r in range(2):
                for hv in range(2):
                    act.wait_ge(s_mm, n + 1)
                    act.activation(lo[r][:, hv * HALF:(hv + 1) * HALF], ps[n % 2][0:RANK, :],
                                   ACT.Tanh if r == 0 else ACT.Copy).then_inc(s_ps_free, 1)
                    n += 1
            use = MAIN // 2
            for r in range(2):
                for j in range(KT):
                    for hv in range(2):
                        v = V["w0" if r == 0 else "a0"] + j
                        act.wait_ge(s_mm, n + 1)
                        act.wait_ge(s_out[n % 2], use * 16 + 16)
                        act.activation(out_sb[n % 2][:], ps[n % 2][:], ACT.Sigmoid,
                                       bias=vec[:, v:v + 1]).then_inc(s_ps_free, 1)
                        act.wait_ge(s_ps_free, n + 3)
                        act.dma_start(proj_rows[4 + r, :, j, hv * HALF:(hv + 1) * HALF],
                                      out_sb[n % 2][:]).then_inc(s_out[n % 2], 16)
                        n += 1
                        use += hv
            for i in range(2):
                act.wait_ge(s_out[i], (use + 1) * 16)



CHUNK = 64
NCH = 128 // CHUNK
RW_HEADS = 16
RW_N = 64
DECAY = math.exp(-0.5)
GN_EPS = 64e-5
LEVELS = [1, 2, 4, 8, 16, 32]

C_WIDTHS = {"maskA": 512, "maskL": 128, "merge": 128 * len(LEVELS), "mergeT": 128, "ident": 128, "headsum": 128,
            "restart": 1024}
C_AT, _at = {}, 0
for _n, _w in C_WIDTHS.items():
    C_AT[_n] = _at
    _at += _w
C_TOTAL = _at


def shape_constants():
    s = np.arange(128)[:, None]
    t = np.arange(128)[None, :]
    same = s // CHUNK == t // CHUNK
    strict, incl = same & (s < t), same & (s <= t)
    out = np.zeros((128, C_TOTAL), np.float32)

    def put(name, a):
        out[:, C_AT[name]:C_AT[name] + C_WIDTHS[name]] = a

    put("maskA", np.concatenate([strict, incl, strict, incl], 1))
    put("maskL", same & (s > t))
    merge = [(s // (2 * b) == t // (2 * b)) & (s // b % 2 == 1) & (t // b % 2 == 0) for b in LEVELS]
    put("merge", np.concatenate(merge, 1))
    put("mergeT", merge[0].T)
    put("ident", s == t)
    put("headsum", s // RW_N == t // RW_N)
    put("restart", np.broadcast_to(np.arange(1024)[None, :] % CHUNK != 0, (128, 1024)))
    return out


RW_PER = dict(
    in_r=16, in_k=16, in_v=16, in_g=16, in_sw=16, in_a=16,
    scan=1, exps=2, kkr=1, ksq=1, ksum=1, kroot=1, kclamp=1, kinv=1, kk=1, am=1, kp=1, at=1, rt=1, b=1, bt=1, kt=1,
    rk=1, trans=8, tok=8, amat=16, amat_sb=16, lmat=4, lmat_sb=4, l_hi=4, x_tmp=4, y_tmp=4, xy1=4,
    w=20, w_sb=20, xy=20, xy_sb=20, e=4, e_sb=4, yt=4, yt_sb=4,
    t1=2, t1_sb=2, u0=2, u0_sb=2, wt=2, wt_sb=2, u=2, u_sb=2, m=2, m_add=2, m_sb=2, m_copy=1,
    y=1, y_sb=1, mean=1, yc=1, ysq=1, var=1, yroot=1, yinv=1, yn=1, yw=1, yb=1, bonus=1, bv=1, ysum=1,
    gsig=1, gs=1, yout=1, stored=16,
)


def rwkv_recurrence(nc, proj, yT, vec, cst):
    with ExitStack() as c:
        sems = Semaphores(nc, c)
        def sb(n, shape, dt=F32):
            return c.enter_context(nc.sbuf_tensor(f"rw_{n}", shape, dt))

        S = {n: sems.new(f"rw_{n}") for n in (*RW_PER, "passed")}
        s_init = sems.new("rw_init")
        tile = [128, KT, 128]
        r_in, k_in, v_in, g_in, sw_in, a_in = (sb(n, tile) for n in ("r", "k", "v", "g", "sw", "a"))
        inputs = dict(r=r_in, k=k_in, v=v_in, g=g_in, sw=sw_in, a=a_in)
        csum = sb("csum", tile)
        pe1 = sb("pe1", [128, KT, NCH, CHUNK + 1])
        pinv = sb("pinv", tile)
        kkr, tmp, root, am = (sb(n, tile) for n in ("kkr", "tmp", "root", "am"))
        ar = sb("ar", [128, KT, 256])
        bt, kt, rk, ybuf = (sb(n, tile) for n in ("bt", "kt", "rk", "ybuf"))
        tok = [sb(f"tok{i}", tile) for i in range(4)]
        v_tok, b_tok, k_tok, a_tok = tok
        amat = sb("amat", [128, 2, KT, 512])
        four = [128, 4, 128]
        lmat = [sb(f"lmat{g}", four) for g in range(2)]
        l_hi, l_lo, lt16, x16, y16, w16 = ([sb(f"{n}{g}", four, F16) for g in range(2)]
                                           for n in ("l_hi", "l_lo", "lt16", "x16", "y16", "w16"))
        ident16, negid16 = sb("ident16", [128, 128], F16), sb("negid16", [128, 128], F16)
        xt32 = sb("xt32", [128, 2, KT, 128])
        t1, u0, utok = (sb(n, [128, 2, KT, RW_N]) for n in ("t1", "u0", "utok"))
        wt = sb("wt", tile)
        mst = [sb(f"m{i}", [128, KT, RW_N]) for i in range(NCH + 1)]
        mtmp = sb("mtmp", [128, KT, RW_N])
        rkbd = sb("rkbd", tile)
        gneps = sb("gneps", [128, 1])
        PS = c.enter_context(nc.psum_tensor("rw_ps", [128, 8, 512], F32))

        def bc(v):
            return vec[:, V[v]:V[v] + KT].unsqueeze(2).to_broadcast(tile)

        def const(name, i=0):
            at = C_AT[name] + 128 * i
            return cst[:, at:at + 128]

        def four_of(a):
            return a.unsqueeze(1).to_broadcast(four)

        def rows(g):
            return slice(RW_N * g, RW_N * (g + 1))

        def bank(b, w=128):
            return PS[:, b, :].rearrange("p (j w) -> p j w", w=w)

        def two(b, w=128):
            return PS[:, b:b + 2, :].rearrange("p b (j w) -> p (b j) w", w=w)

        WB, XB, YB = (2, 5), (3, 6), (4, 7)
        TRB = (2, 3, 5, 6)

        def level(hf, l, g):
            return hf * 10 + (l - 1) * 2 + g + 1

        block = c.enter_context(nc.Block())
        p_view = proj.rearrange("q (j p) t -> q p j t", p=128)
        y_view = yT.rearrange("(j p) t -> p j t", p=128)
        TILES = T // 128

        @block.sync
        def _(sp):
            for n in RW_PER:
                sp.sem_inc(S[n], RW_PER[n])
            with sp.Fori(0, TILES) as t:
                at = Place(sp, S, RW_PER, t)
                for n, q, freed in (("sw", 4, ["scan"]), ("k", 1, ["kkr", "kp"]), ("a", 5, ["am", "b"]),
                                    ("r", 0, ["rt", "rk"]), ("v", 2, ["bv", "trans"]), ("g", 3, ["gs"])):
                    at.settle()
                    for f in freed:
                        at.prev(f)
                    at.did(sp.dma_start(inputs[n][:], p_view[q, :, :, ds(t * 128, 128)]), f"in_{n}", 16)
                at.need("yout")
                at.did(sp.dma_start(y_view[:, :, ds(t * 128, 128)], ybuf[:]), "stored", 16)
                at.end()
            sp.wait_ge(S["stored"], 16 * (TILES + 1))

        @block.gpsimd
        def _(pool):
            pool.memset(pe1[:, :, :, 0:1], 1.0).then_inc(s_init, 1)
            pool.memset(mst[0][:], 0.0).then_inc(s_init, 1)
            pool.memset(gneps[:], GN_EPS).then_inc(s_init, 1)
            pool.tensor_copy(ident16[:], const("ident")).then_inc(s_init, 1)
            pool.tensor_scalar(negid16[:], const("ident"), -1.0, None, ALU.mult).then_inc(s_init, 1)
            for j in range(KT):
                pool.tensor_scalar(rkbd[:, j, :], const("headsum"), vec[:, V["r_k"] + j:V["r_k"] + j + 1], None,
                                   ALU.mult).then_inc(s_init, 1)
            with pool.Fori(0, TILES) as t:
                at = Place(pool, S, RW_PER, t)
                at.need("in_k")
                at.prev("at")
                at.did(pool.tensor_tensor(kkr[:], k_in[:], bc("k_k"), ALU.mult), "kkr")
                at.need("kk")
                at.need("in_a")
                at.prev("lmat")
                at.did(pool.tensor_tensor(bt[:], kkr[:], a_in[:], ALU.mult), "b")
                at.need("kp")
                at.need("in_r")
                at.prev("bonus")
                at.did(pool.tensor_tensor(rk[:], r_in[:], am[:], ALU.mult), "rk")
                for hf in range(2):
                    for g in range(2):
                        G = 2 * hf + g
                        a_ab = amat[:, g, 4 * hf:4 * hf + 4, 0:128]
                        at.settle()
                        at.need("lmat_sb", G + 1)
                        at.did(pool.tensor_copy(l_hi[g][:], lmat[g][:]), "l_hi")
                        at.settle()
                        at.need("amat_sb", 8 * hf + 8)
                        pool.tensor_copy(lt16[g][:], a_ab)
                        at.did(pool.tensor_tensor(x16[g][:], lmat[g][:], four_of(const("merge")), ALU.mult), "x_tmp")
                        at.did(pool.tensor_tensor(y16[g][:], a_ab, four_of(const("mergeT")), ALU.mult), "y_tmp")
                        at.need("l_hi", G + 1)
                        pool.tensor_tensor(l_lo[g][:], lmat[g][:], l_hi[g][:], ALU.subtract)
                        at.need("x_tmp", G + 1)
                        pool.tensor_tensor(x16[g][:], x16[g][:], four_of(const("ident")), ALU.add)
                        at.need("y_tmp", G + 1)
                        at.did(pool.tensor_tensor(y16[g][:], y16[g][:], four_of(const("ident")), ALU.add), "xy1")
                at.need("gsig")
                at.did(pool.tensor_tensor(am[:], g_in[:], am[:], ALU.mult), "gs")
                at.need("yn")
                at.did(pool.tensor_tensor(tmp[:], tmp[:], bc("gn_w"), ALU.mult), "yw")
                at.need("yw")
                at.did(pool.tensor_tensor(tmp[:], tmp[:], bc("gn_b"), ALU.add), "yb")
                at.end()

        @block.scalar
        def _(act):
            act.wait_ge(s_init, 5 + KT)
            with act.Fori(0, TILES) as t:
                at = Place(act, S, RW_PER, t)
                at.need("scan")
                flat = csum[:].rearrange("p j (c s) -> p j c s", s=CHUNK)
                at.did(act.activation(pe1[:, :, :, 1:CHUNK + 1], flat, ACT.Exp, scale=-DECAY), "exps")
                at.did(act.activation(pinv[:], csum[:], ACT.Exp, scale=DECAY), "exps")
                at.need("kkr")
                at.prev("yout")
                at.did(act.activation(tmp[:], kkr[:], ACT.Square), "ksq")
                at.need("ksum")
                at.did(act.activation(root[:], two(0), ACT.Sqrt), "kroot")
                for i in range(8):
                    at.need("trans", i + 1)
                    at.did(act.copy(tok[i // 2][:, 4 * (i % 2):4 * (i % 2) + 4, :], bank(TRB[i % 4])), "tok")
                for hf in range(2):
                    col = slice(4 * hf, 4 * hf + 4)
                    for l in range(1, 6):
                        for g in range(2):
                            at.need("xy", level(hf, l, g))
                            act.copy(x16[g][:], bank(XB[g]))
                            at.did(act.copy(y16[g][:], bank(YB[g])), "xy_sb")
                    for g in range(2):
                        at.need("yt", 2 * hf + g + 1)
                        at.did(act.copy(xt32[:, g, col, :], bank(YB[g])), "yt_sb")
                    at.need("t1", hf + 1)
                    at.did(act.copy(t1[:, :, col, :], PS[:, 0, :].rearrange("p (g j w) -> p g j w", g=2, w=RW_N)),
                           "t1_sb")
                    at.need("u0", hf + 1)
                    at.did(act.copy(u0[:, :, col, :], PS[:, 1, :].rearrange("p (g j w) -> p g j w", g=2, w=RW_N)),
                           "u0_sb")
                    at.need("wt", hf + 1)
                    at.did(act.copy(wt[:, col, :], bank(2)), "wt_sb")
                at.need("y")
                at.need("m_sb")
                at.did(act.copy(mst[0][:], mst[2][:]), "m_copy")
                at.did(act.copy(csum[:], two(3)), "y_sb")
                at.need("yc")
                at.did(act.activation(root[:], tmp[:], ACT.Square), "ysq")
                at.need("var")
                at.did(act.activation(csum[:], two(0), ACT.Sqrt, bias=gneps[:], scale=1.0 / RW_N), "yroot")
                at.need("in_g")
                at.need("rk")
                at.need("kt")
                at.did(act.activation(am[:], g_in[:], ACT.Sigmoid), "gsig")
                at.end()

        @block.vector
        def _(dve):
            dve.wait_ge(s_init, 5 + KT)
            with dve.Fori(0, TILES) as t:
                at = Place(dve, S, RW_PER, t)
                at.need("in_sw")
                flat = slice(C_AT["restart"], C_AT["restart"] + 1024)
                at.did(dve.tensor_tensor_scan(csum[:].rearrange("p j s -> p (j s)"), cst[:, flat],
                                              sw_in[:].rearrange("p j s -> p (j s)"), 0.0, ALU.mult, ALU.add), "scan")
                at.need("in_a")
                at.did(dve.scalar_tensor_tensor(am[:], a_in[:], -1.0, bc("k_a"), ALU.add, ALU.mult), "am")
                at.need("am")
                at.need("in_k")
                at.did(dve.scalar_tensor_tensor(am[:], am[:], 1.0, k_in[:], ALU.add, ALU.mult), "kp")
                at.need("kroot")
                at.did(dve.tensor_scalar(root[:], root[:], 1e-12, None, ALU.max), "kclamp")
                at.need("kclamp")
                at.did(dve.reciprocal(tmp[:], root[:]), "kinv")
                at.need("kinv")
                at.did(dve.tensor_tensor(kkr[:], kkr[:], tmp[:], ALU.mult), "kk")
                at.need("exps")
                at.prev("y")
                at.need("in_r")
                split = "p j (c s) -> p j c s"
                at.did(dve.tensor_tensor(ar[:, :, 128:256].rearrange(split, s=CHUNK),
                                         r_in[:].rearrange(split, s=CHUNK), pe1[:, :, :, 1:CHUNK + 1],
                                         ALU.mult), "rt")
                at.need("kp")
                at.did(dve.tensor_tensor(kt[:], am[:], pinv[:], ALU.mult), "kt")
                at.need("kk")
                at.did(dve.scalar_tensor_tensor(ar[:, :, 0:128].rearrange(split, s=CHUNK),
                                                kkr[:].rearrange(split, s=CHUNK), -1.0, pe1[:, :, :, 0:CHUNK],
                                                ALU.mult, ALU.mult), "at")
                at.need("b")
                at.did(dve.tensor_tensor(bt[:], bt[:], pinv[:], ALU.mult), "bt")
                for hf in range(2):
                    col = slice(4 * hf, 4 * hf + 4)
                    for n in range(8):
                        jj, g = n // 2, n % 2
                        at.need("amat", 8 * hf + n + 1)
                        at.did(dve.tensor_tensor(amat[:, g, 4 * hf + jj, :], PS[:, g, :],
                                                 cst[:, C_AT["maskA"]:C_AT["maskA"] + 512], ALU.mult), "amat_sb")
                    for g in range(2):
                        at.need("lmat", 2 * hf + g + 1)
                        at.did(dve.tensor_tensor(lmat[g][:], bank(WB[g]), four_of(const("maskL")), ALU.mult),
                               "lmat_sb")
                    for l in range(1, 6):
                        for g in range(2):
                            at.need("w", level(hf, l, g))
                            at.did(dve.tensor_tensor(w16[g][:], bank(WB[g]), four_of(const("merge", l)), ALU.mult),
                                   "w_sb")
                    for g in range(2):
                        at.need("e", 2 * hf + g + 1)
                        at.did(dve.tensor_copy(w16[g][:], bank(WB[g])), "e_sb")
                at.need("u0_sb")
                for ci in range(NCH):
                    s = slice(CHUNK * ci, CHUNK * (ci + 1))
                    at.need("u", ci + 1)
                    at.did(dve.tensor_tensor(utok[s].rearrange("p g j v -> p g (j v)"), PS[s, 0:2, :],
                                             u0[s].rearrange("p g j v -> p g (j v)"), ALU.add), "u_sb")
                    if ci == 0:
                        at.prev("m_copy")
                    else:
                        at.need("m_sb", ci)
                    at.need("m", ci + 1)
                    at.did(dve.tensor_tensor(mtmp[:], bank(2, RW_N), mst[ci][:], ALU.add), "m_add")
                    at.need("m_add", ci + 1)
                    at.did(dve.tensor_tensor(mst[ci + 1][:], mtmp[:],
                                             pe1[:, :, ci, CHUNK:CHUNK + 1].to_broadcast([128, KT, RW_N]),
                                             ALU.mult), "m_sb")
                at.need("mean")
                at.did(dve.scalar_tensor_tensor(tmp[:], two(5), -1.0 / RW_N, csum[:], ALU.mult, ALU.add), "yc")
                at.need("yroot")
                at.did(dve.reciprocal(root[:], csum[:]), "yinv")
                at.need("yinv")
                at.did(dve.tensor_tensor(tmp[:], tmp[:], root[:], ALU.mult), "yn")
                at.need("bonus")
                at.did(dve.tensor_tensor(csum[:], two(5), v_in[:], ALU.mult), "bv")
                at.need("bv")
                at.need("yb")
                at.did(dve.tensor_tensor(tmp[:], tmp[:], csum[:], ALU.add), "ysum")
                at.need("ysum")
                at.need("gs")
                at.prev("stored")
                at.did(dve.tensor_tensor(ybuf[:], tmp[:], am[:], ALU.mult), "yout")
                at.end()

        @block.tensor
        def _(pe):
            pe.wait_ge(s_init, 5 + KT)
            with pe.Fori(0, TILES) as t:
                at = Place(pe, S, RW_PER, t)
                at.need("ksq")
                at.prev("yroot")
                for i in range(2):
                    last = pe.matmul(PS[:, i, :], const("headsum"),
                                     tmp[:, 4 * i:4 * i + 4, :].rearrange("p j s -> p (j s)"), start=True, stop=True)
                at.did(last, "ksum")
                at.prev("m_add")
                at.prev("y_sb")
                at.prev("bv")
                for i, (src, made) in enumerate((s, m) for s, m in ((v_in, "in_v"), (bt, "bt"), (kt, "kt"),
                                                                    (ar, "at")) for _ in range(2)):
                    at.need(made)
                    if i >= 4:
                        at.need("tok", i - 3)
                    for jj in range(4):
                        last = pe.transpose(bank(TRB[i % 4])[:, jj, :], src[:, 4 * (i % 2) + jj, 0:128],
                                            const("ident"))
                    at.did(last, "trans")
                at.need("rt")
                at.need("kroot")
                at.need("tok")
                for hf in range(2):
                    for n in range(8):
                        jj, g = n // 2, n % 2
                        j, R = 4 * hf + jj, rows(g)
                        if hf and n < 2:
                            at.need(("t1_sb", "u0_sb")[n], 1)
                        if n >= 2:
                            at.need("amat_sb", 8 * hf + n - 1)
                        pe.matmul(PS[:, g, 0:256], bt[R, j, :], ar[R, j, :], start=True, stop=True)
                        at.did(pe.matmul(PS[:, g, 256:512], kt[R, j, :], ar[R, j, :], start=True, stop=True), "amat")
                    for g in range(2):
                        R = rows(g)
                        if hf and g == 0:
                            at.need("wt_sb", 1)
                        for jj in range(4):
                            last = pe.matmul(bank(WB[g])[:, jj, :], ar[R, 4 * hf + jj, 0:128], bt[R, 4 * hf + jj, :],
                                             start=True, stop=True)
                        at.did(last, "lmat")
                    for l in range(1, 6):
                        for g in range(2):
                            if l == 1:
                                at.need("xy1", 2 * hf + g + 1)
                            else:
                                at.need("xy_sb", level(hf, l - 1, g))
                            for jj in range(4):
                                last = pe.matmul(bank(WB[g])[:, jj, :], lt16[g][:, jj, :], x16[g][:, jj, :],
                                                 start=True, stop=True)
                            at.did(last, "w")
                        for g in range(2):
                            at.need("w_sb", level(hf, l, g))
                            for jj in range(4):
                                X, Y, W = x16[g][:, jj, :], y16[g][:, jj, :], w16[g][:, jj, :]
                                pe.matmul(bank(XB[g])[:, jj, :], Y, W, start=True, stop=False)
                                pe.matmul(bank(XB[g])[:, jj, :], ident16[:], X, start=False, stop=True)
                                pe.matmul(bank(YB[g])[:, jj, :], W, Y, start=True, stop=False)
                                last = pe.matmul(bank(YB[g])[:, jj, :], ident16[:], Y, start=False, stop=True)
                            at.did(last, "xy")
                    for g in range(2):
                        at.need("xy_sb", level(hf, 5, g))
                        for jj in range(4):
                            Y = y16[g][:, jj, :]
                            pe.matmul(bank(WB[g])[:, jj, :], l_hi[g][:, jj, :], Y, start=True, stop=False)
                            pe.matmul(bank(WB[g])[:, jj, :], l_lo[g][:, jj, :], Y, start=False, stop=False)
                            pe.matmul(bank(WB[g])[:, jj, :], negid16[:], Y, start=False, stop=False)
                            last = pe.matmul(bank(WB[g])[:, jj, :], ident16[:], ident16[:], start=False, stop=True)
                        at.did(last, "e")
                    for g in range(2):
                        at.need("e_sb", 2 * hf + g + 1)
                        for jj in range(4):
                            pe.matmul(bank(YB[g])[:, jj, :], x16[g][:, jj, :], w16[g][:, jj, :],
                                      start=True, stop=False)
                            last = pe.matmul(bank(YB[g])[:, jj, :], ident16[:], y16[g][:, jj, :],
                                             start=False, stop=True)
                        at.did(last, "yt")
                    at.need("amat_sb", 8 * hf + 8)
                    for g in range(2):
                        for jj in range(4):
                            j = 4 * hf + jj
                            q = (4 * g + jj) * RW_N
                            last = pe.matmul(PS[:, 0, q:q + RW_N], amat[:, g, j, 256:384], v_tok[:, j, rows(g)],
                                             start=True, stop=True)
                    at.did(last, "t1")
                    at.need("t1_sb", hf + 1)
                    at.need("yt_sb", 2 * hf + 2)
                    for g in range(2):
                        for jj in range(4):
                            q = (4 * g + jj) * RW_N
                            last = pe.matmul(PS[:, 1, q:q + RW_N], xt32[:, g, 4 * hf + jj, :],
                                             t1[:, g, 4 * hf + jj, :], start=True, stop=True)
                    at.did(last, "u0")
                    for g in range(2):
                        for jj in range(4):
                            j = 4 * hf + jj
                            last = pe.matmul(bank(2)[rows(g), jj, :], a_tok[:, j, rows(g)], xt32[:, g, j, :],
                                             start=True, stop=True)
                    at.did(last, "wt")
                at.need("t1_sb")
                at.need("u0_sb")
                at.need("wt_sb")
                for ci in range(NCH):
                    s = slice(CHUNK * ci, CHUNK * (ci + 1))
                    at.settle()
                    if ci == 0:
                        at.prev("m_copy")
                    else:
                        at.need("m_sb", ci)
                    for g in range(2):
                        for j in range(KT):
                            last = pe.matmul(PS[s, g, RW_N * j:RW_N * (j + 1)], wt[rows(g), j, s],
                                             mst[ci][rows(g), j, :], start=True, stop=True)
                    at.did(last, "u")
                    at.settle()
                    at.need("u_sb", ci + 1)
                    if ci:
                        at.need("m_add", ci)
                    for g in range(2):
                        for j in range(KT):
                            o = bank(2, RW_N)[rows(g), j, :]
                            pe.matmul(o, k_tok[s, j, rows(g)], v_tok[s, j, rows(g)], start=True, stop=False)
                            last = pe.matmul(o, b_tok[s, j, rows(g)], utok[s, g, j, :], start=False, stop=True)
                    at.did(last, "m")
                at.need("yt_sb")
                for g in range(2):
                    R = rows(g)
                    for j in range(KT):
                        o = two(3)[R, j, :]
                        pe.matmul(o, utok[:, g, j, :], amat[:, g, j, 128:256], start=True, stop=False)
                        pe.matmul(o, v_tok[:, j, R], amat[:, g, j, 384:512], start=False, stop=True)
                        for ci in range(NCH):
                            s = slice(CHUNK * ci, CHUNK * (ci + 1))
                            last = pe.matmul(o[:, s], mst[ci][R, j, :], ar[R, j, 128 + CHUNK * ci:192 + CHUNK * ci],
                                             start=False, stop=True, skip_group_check=True)
                at.did(last, "y")
                at.need("y_sb")
                for i in range(2):
                    last = pe.matmul(PS[:, 5 + i, :], const("headsum"),
                                     csum[:, 4 * i:4 * i + 4, :].rearrange("p j s -> p (j s)"), start=True, stop=True)
                at.did(last, "mean")
                at.need("ysq")
                for i in range(2):
                    last = pe.matmul(PS[:, i, :], const("headsum"),
                                     root[:, 4 * i:4 * i + 4, :].rearrange("p j s -> p (j s)"), start=True, stop=True)
                at.did(last, "var")
                at.need("rk")
                for j in range(KT):
                    last = pe.matmul(two(5)[:, j, :], rkbd[:, j, :], rk[:, j, :], start=True, stop=True)
                at.did(last, "bonus")
                at.end()



def output_projection(nc, name, src, y, w_out, residual, dst):
    per = dict(w0=16, w1=16, res0=32, res1=32, out0=32, out1=32, mm=4, sum=4)
    with ExitStack() as c:
        sems = Semaphores(nc, c)
        def sb(n, shape, dt=F32):
            return c.enter_context(nc.sbuf_tensor(f"{name}_{n}", shape, dt))

        S = {n: sems.new(f"{name}_{n}") for n in per}
        s_y = sems.new(f"{name}_y")
        w = [sb(f"w{i}", [128, KT, 128]) for i in range(2)]
        res = [sb(f"res{i}", [128, HALF]) for i in range(2)]
        out = [sb(f"out{i}", [128, HALF]) for i in range(2)]
        ps = [c.enter_context(nc.psum_tensor(f"{name}_ps{i}", [128, HALF], F32)) for i in range(2)]
        block = c.enter_context(nc.Block())
        w_cols = w_out.rearrange("(k p) n -> p k n", p=128)
        res_v = residual.rearrange("(j p) t -> j p t", p=128)
        dst_v = dst.rearrange("(j p) t -> j p t", p=128)

        def part(dram, c2, i, hv):
            return dram[ds(c2 * 2 + i, 1), :, HALF * hv:HALF * hv + HALF].rearrange("j p t -> p (j t)")

        @block.sync
        def _(sp):
            for n in per:
                sp.sem_inc(S[n], per[n])
            if src is not None:
                for k in range(KT):
                    sp.dma_start(y[:, k, :], src[128 * k:128 * k + 128, :]).then_inc(s_y, 16)
            with sp.Fori(0, KT // 2) as c2:
                at = Place(sp, S, per, c2)
                for i in range(2):
                    at.prev("mm", 2 * i + 2)
                    at.did(sp.dma_start(w[i][:], w_cols[:, :, ds(c2 * 256 + 128 * i, 128)]), f"w{i}", 16)
                    for hv in range(2):
                        if i:
                            at.need("sum", hv + 1)
                        else:
                            at.prev("sum", 3 + hv)
                        at.did(sp.dma_start(res[hv][:], part(res_v, c2, i, hv)), f"res{hv}", 16)
                at.end()

        @block.scalar
        def _(act):
            with act.Fori(0, KT // 2) as c2:
                at = Place(act, S, per, c2)
                for i in range(2):
                    for hv in range(2):
                        at.need("sum", 2 * i + hv + 1)
                        at.did(act.dma_start(part(dst_v, c2, i, hv), out[hv][:]), f"out{hv}", 16)
                at.end()
            for hv in range(2):
                act.wait_ge(S[f"out{hv}"], 32 * (KT // 2 + 1))

        @block.tensor
        def _(pe):
            if src is not None:
                pe.wait_ge(s_y, 16 * KT)
            with pe.Fori(0, KT // 2) as c2:
                at = Place(pe, S, per, c2)
                for i in range(2):
                    at.need(f"w{i}")
                    for hv in range(2):
                        if i:
                            at.need("sum", hv + 1)
                        else:
                            at.prev("sum", 3 + hv)
                        for k in range(KT):
                            for b in range(HB):
                                t0 = HALF * hv + 512 * b
                                last = pe.matmul(ps[hv][:, 512 * b:512 * b + 512], w[i][:, k, :], y[:, k, t0:t0 + 512],
                                                 start=k == 0, stop=k == KT - 1)
                        at.did(last, "mm")
                at.end()

        @block.vector
        def _(dve):
            with dve.Fori(0, KT // 2) as c2:
                at = Place(dve, S, per, c2)
                for i in range(2):
                    for hv in range(2):
                        at.need("mm", 2 * i + hv + 1)
                        at.need(f"res{hv}", 16 * (i + 1))
                        if i:
                            at.need(f"out{hv}", 16)
                        else:
                            at.prev(f"out{hv}", 32)
                        at.did(dve.tensor_tensor(out[hv][:], ps[hv][:], res[hv][:], ALU.add), "sum")
                at.end()



CW = D // 2
CB = CW // 128
HEADS = 8
DH = 64


def conv_branch(nc, h2, w_in, cvec, y2):
    order = (2, 0, 1, 3)
    per = dict(w0=32, w1=32, mm=8, gc=2, zu=2, tap0=1, tap1=1, tap2=1, gb=2, sig=2, sil=2, yc=1, out=16)
    with ExitStack() as c:
        sems = Semaphores(nc, c)
        def sb(n, shape, dt=F32):
            return c.enter_context(nc.sbuf_tensor(f"cv_{n}", shape, dt))

        S = {n: sems.new(f"cv_{n}") for n in (*per, "passed")}
        s_zero = sems.new("cv_zero")
        w = [sb(f"w{i}", [128, KT, 128]) for i in range(2)]
        gc, conv = sb("gc", [128, T]), sb("conv", [128, T])
        sig = gc
        zu = sb("zu", [128, T + 2])
        vec = sb("vec", [128, 4, CB])
        ps = [c.enter_context(nc.psum_tensor(f"cv_ps{i}", [128, HALF], F32)) for i in range(4)]
        block = c.enter_context(nc.Block())
        w_cols = w_in.rearrange("(k p) n -> p k n", p=128)

        def half(hv, shift=0):
            return slice(HALF * hv + shift, HALF * hv + HALF + shift)

        READ = {0: ("gc", 0), 1: ("zu", 0), 2: ("gb", 0), 3: ("sil", 0)}

        @block.sync
        def _(sp):
            for n in per:
                sp.sem_inc(S[n], per[n])
            with sp.Fori(0, CB) as g:
                at = Place(sp, S, per, g)
                for m in range(4):
                    at.settle()
                    if m < 2:
                        at.prev("mm", 2 * m + 6)
                    else:
                        at.need("mm", 2 * m - 2)
                    at.did(sp.dma_start(w[m % 2][:], w_cols[:, :, ds(g * 128 + order[m] * CW, 128)]), f"w{m % 2}", 16)
                at.end()

        @block.tensor
        def _(pe):
            with pe.Fori(0, CB) as g:
                at = Place(pe, S, per, g)
                for m in range(4):
                    at.need(f"w{m % 2}", 16 * (m // 2 + 1))
                    for hv in range(2):
                        if m < 2:
                            at.prev(READ[m + 2][0], hv + 1)
                        else:
                            at.need(READ[m - 2][0], hv + 1)
                        for k in range(KT):
                            for b in range(HB):
                                t0 = HALF * hv + 512 * b
                                last = pe.matmul(ps[2 * (m % 2) + hv][:, 512 * b:512 * b + 512], w[m % 2][:, k, :],
                                                 h2[:, k, t0:t0 + 512], start=k == 0, stop=k == KT - 1)
                        at.did(last, "mm")
                at.end()

        @block.scalar
        def _(act):
            act.dma_start(vec[:], cvec).then_inc(s_zero, 16)
            with act.Fori(0, CB) as g:
                at = Place(act, S, per, g)
                at.prev("yc")
                for hv in range(2):
                    at.need("mm", hv + 1)
                    at.did(act.copy(gc[:, half(hv)], ps[hv][:]), "gc")
                at.need("zu")
                for hv in range(2):
                    at.need("mm", 7 + hv)
                    at.did(act.activation(sig[:, half(hv)], ps[2 + hv][:], ACT.Sigmoid), "sig")
                at.need("yc")
                at.did(act.dma_start(y2[ds(g * 128, 128), :], conv[:]), "out", 16)
                at.end()
            act.wait_ge(S["out"], 16 * (CB + 1))

        @block.gpsimd
        def _(pool):
            pool.memset(zu[:, 0:1], 0.0).then_inc(s_zero, 1)
            pool.memset(zu[:, T + 1:T + 2], 0.0).then_inc(s_zero, 1)

        @block.vector
        def _(dve):
            dve.wait_ge(s_zero, 18)
            with dve.Fori(0, CB) as g:
                at = Place(dve, S, per, g)

                def tap(i):
                    return vec[:, i, ds(g, 1)]

                for hv in range(2):
                    at.need("mm", 3 + hv)
                    at.need("gc", hv + 1)
                    at.did(dve.tensor_tensor(zu[:, half(hv, 1)], ps[2 + hv][:], gc[:, half(hv)], ALU.mult), "zu")
                at.need("zu")
                at.prev("out")
                at.did(dve.tensor_scalar(conv[:], zu[:, 0:T], tap(0), tap(3), ALU.mult, ALU.add), "tap0")
                at.need("tap0")
                at.did(dve.scalar_tensor_tensor(conv[:], zu[:, 1:T + 1], tap(1), conv[:], ALU.mult, ALU.add), "tap1")
                at.need("tap1")
                at.did(dve.scalar_tensor_tensor(conv[:], zu[:, 2:T + 2], tap(2), conv[:], ALU.mult, ALU.add), "tap2")
                at.need("tap2")
                for hv in range(2):
                    at.need("mm", 5 + hv)
                    at.did(dve.tensor_tensor(conv[:, half(hv)], ps[hv][:], conv[:, half(hv)], ALU.mult), "gb")
                for hv in range(2):
                    at.need("sig", hv + 1)
                    at.did(dve.tensor_tensor(sig[:, half(hv)], ps[2 + hv][:], sig[:, half(hv)], ALU.mult), "sil")
                at.need("sil")
                at.need("gb")
                at.did(dve.tensor_tensor(conv[:], conv[:], sig[:], ALU.mult), "yc")
                at.end()


def attention_projections(nc, h2, w_in, qkv, gains, headsum, z_gate):
    per = dict(w0=16, w1=16, mm=4, sq=4, raw=4, ms=4, var=4, root=4, inv=4, norm=4)
    zper = dict(sig=4, out0=32, out1=32)
    with ExitStack() as c:
        sems = Semaphores(nc, c)
        def sb(n, shape, dt=F32):
            return c.enter_context(nc.sbuf_tensor(f"at_{n}", shape, dt))

        S = {n: sems.new(f"at_{n}") for n in (*per, *zper)}
        s_gain = sems.new("at_gain")
        w = [sb(f"w{i}", [128, KT, 128]) for i in range(2)]
        sq, root = ([sb(f"{n}{i}", [128, HALF]) for i in range(2)] for n in ("sq", "root"))
        gain = sb("gain", [128, 2])
        ps = [c.enter_context(nc.psum_tensor(f"at_ps{i}", [128, HALF], F32)) for i in range(2)]
        ms = [c.enter_context(nc.psum_tensor(f"at_ms{i}", [128, HALF], F32)) for i in range(2)]
        block = c.enter_context(nc.Block())
        w_cols = w_in.rearrange("(k p) n -> p k n", p=128)
        z_rows = z_gate.rearrange("(j p) t -> j p t", p=128)
        PAIRS = CB // 2

        def half(hv):
            return slice(HALF * hv, HALF * hv + HALF)

        def n_of(i, hv):
            return 2 * i + hv + 1

        def dest(kind, c2, i, hv):
            return qkv[kind][:, ds(c2 * 2 + i, 1), half(hv)].rearrange("p j t -> p (j t)")

        def pairs(eng):
            for kind in range(4):
                with eng.Fori(0, PAIRS) as c2:
                    at = Place(eng, S, per, c2 + kind * PAIRS)
                    yield kind, c2, at

        @block.sync
        def _(sp):
            for n in per:
                sp.sem_inc(S[n], per[n])
            for n in zper:
                sp.sem_inc(S[n], zper[n])
            for kind, c2, at in pairs(sp):
                for i in range(2):
                    at.prev("mm", n_of(i, 1))
                    at.did(sp.dma_start(w[i][:], w_cols[:, :, ds(c2 * 256 + ((4 + kind) * CW + 128 * i), 128)]),
                           f"w{i}", 16)
                if kind == 3:
                    zat = Place(sp, S, zper, c2)
                    for i in range(2):
                        for hv in range(2):
                            at.need("raw", n_of(i, hv))
                            zat.did(sp.dma_start(z_rows[ds(c2 * 2 + i, 1), :, half(hv)]
                                                 .rearrange("j p t -> p (j t)"), root[hv][:]), f"out{hv}", 16)
            for hv in range(2):
                sp.wait_ge(S[f"out{hv}"], 32 * (PAIRS + 1))

        @block.tensor
        def _(pe):
            for kind, c2, at in pairs(pe):
                for i in range(2):
                    at.need(f"w{i}")
                    for hv in range(2):
                        last_read = at.need if i else at.prev
                        last_read("raw", 2 * (1 - i) + hv + 1)
                        for kt in range(KT):
                            for b in range(HB):
                                t0 = HALF * hv + 512 * b
                                last = pe.matmul(ps[hv][:, 512 * b:512 * b + 512], w[i][:, kt, :],
                                                 h2[:, kt, t0:t0 + 512], start=kt == 0, stop=kt == KT - 1)
                        at.did(last, "mm")
                    if kind < 2:
                        for hv in range(2):
                            at.need("sq", n_of(i, hv))
                            (at.need if i else at.prev)("var", 2 * (1 - i) + hv + 1)
                            for b in range(HB):
                                last = pe.matmul(ms[hv][:, 512 * b:512 * b + 512], headsum,
                                                 sq[hv][:, 512 * b:512 * b + 512], start=True, stop=True)
                            at.did(last, "ms")

        @block.scalar
        def _(act):
            act.dma_start(gain[:], gains).then_inc(s_gain, 16)
            for kind, c2, at in pairs(act):
                zat = Place(act, S, zper, c2)
                for i in range(2):
                    for hv in range(2):
                        at.need("mm", n_of(i, hv))
                        if kind < 2:
                            (at.need if i else at.prev)("ms", 2 * (1 - i) + hv + 1)
                            at.did(act.activation(sq[hv][:], ps[hv][:], ACT.Square), "sq")
                        if kind < 3:
                            at.did(act.copy(dest(kind, c2, i, hv), ps[hv][:]), "raw")
                        else:
                            (at.need if i else at.prev)("raw", 2 * (1 - i) + hv + 1)
                            zat.did(act.activation(sq[hv][:], ps[hv][:], ACT.Sigmoid), "sig")
                    if kind < 2:
                        for hv in range(2):
                            at.need("var", n_of(i, hv))
                            at.did(act.activation(root[hv][:], root[hv][:], ACT.Sqrt), "root")

        @block.vector
        def _(dve):
            dve.wait_ge(s_gain, 16)
            dve.tensor_scalar(gain[:, 0:1], gain[:, 0:1], DH ** -0.5, None, ALU.mult).then_inc(s_gain, 1)
            dve.wait_ge(s_gain, 17)
            for kind, c2, at in pairs(dve):
                zat = Place(dve, S, zper, c2)
                for i in range(2):
                    for hv in range(2):
                        n = n_of(i, hv)
                        if kind < 2:
                            at.need("ms", n)
                            (at.need if i else at.prev)("norm", 2 * (1 - i) + hv + 1)
                            at.did(dve.tensor_scalar(root[hv][:], ms[hv][:], 1.0 / DH, EPS, ALU.mult, ALU.add), "var")
                        if kind == 3:
                            dve.wait_ge(S["norm"], 4 * (2 * PAIRS + 1))
                            at.need("mm", n)
                            zat.need("sig", n)
                            if i:
                                zat.need(f"out{hv}", 16)
                            else:
                                zat.prev(f"out{hv}", 32)
                            at.did(dve.tensor_tensor(root[hv][:], ps[hv][:], sq[hv][:], ALU.mult), "raw")
                    if kind < 2:
                        for hv in range(2):
                            n = n_of(i, hv)
                            at.need("root", n)
                            at.did(dve.reciprocal(root[hv][:], root[hv][:]), "inv")
                            at.need("inv", n)
                            at.need("raw", n)
                            d = dest(kind, c2, i, hv)
                            at.did(dve.scalar_tensor_tensor(d, d, gain[:, kind:kind + 1], root[hv][:],
                                                            ALU.mult, ALU.mult), "norm")
            dve.wait_ge(S["norm"], 4 * (2 * PAIRS + 1))



DILATIONS = (1, 4, 16)
WINDOW_HALF = 64
QB = 128
BUCKETS = 32
MAX_DISTANCE = 1024
NEG = -1e30
SKEW = 383
OROW = HEADS * (DH + 2)


def bucket_constants():
    half_b = BUCKETS // 2
    exact = half_b // 2
    out = np.zeros((BUCKETS + 1, len(DILATIONS), SKEW), np.float32)
    for g, dil in enumerate(DILATIONS):
        for x in range(SKEW):
            rel = x - (SKEW // 2)
            if abs(rel) > WINDOW_HALF:
                out[BUCKETS, g, x] = 1.0
                continue
            n = abs(rel) * dil
            far = exact + int(np.float32(np.log(np.float32(max(n, 1)) / np.float32(exact)))
                              / np.float32(math.log(MAX_DISTANCE / exact)) * np.float32(half_b - exact))
            out[(half_b if rel > 0 else 0) + (n if n < exact else min(far, half_b - 1)), g, x] = 1.0
    return out


def bias_tables(nc, rel_bias, onehot, skew, table):
    NG = len(DILATIONS)
    with ExitStack() as c:
        sems = Semaphores(nc, c)
        rb = c.enter_context(nc.sbuf_tensor("bt_rb", [BUCKETS + 1, HEADS], F32))
        rb_q = c.enter_context(nc.sbuf_tensor("bt_rb_q", [BUCKETS + 1, HEADS, 128], F32))
        hot = c.enter_context(nc.sbuf_tensor("bt_hot", [BUCKETS + 1, NG, SKEW], F32))
        flat = c.enter_context(nc.sbuf_tensor("bt_flat", [128, NG * HEADS, SKEW], F32))
        ps = [c.enter_context(nc.psum_tensor(f"bt_ps{i}", [128, 512], F32)) for i in range(2)]
        s_set, s_in, s_spread, s_mm, s_flat, s_skew, s_table = (
            sems.new(f"bt_{n}") for n in ("set", "in", "spread", "mm", "flat", "skew", "table"))
        block = c.enter_context(nc.Block())

        @block.gpsimd
        def _(pool):
            pool.memset(rb[:], NEG).then_inc(s_set, 1)
            pool.wait_ge(s_in, 32)
            pool.tensor_copy(rb_q[:], rb[:].unsqueeze(2).to_broadcast([BUCKETS + 1, HEADS, 128])).then_inc(s_spread, 1)

        @block.sync
        def _(sp):
            sp.dma_start(hot[:], onehot).then_inc(s_in, 16)
            sp.wait_ge(s_set, 1)
            sp.dma_start(rb[0:BUCKETS, :], rel_bias).then_inc(s_in, 16)
            for n in range(NG * HEADS):
                sp.wait_ge(s_flat, n + 1)
                sp.dma_start(skew[n].rearrange("(p x) -> p x", x=SKEW), flat[:, n, :]).then_inc(s_skew, 16)
            sp.wait_ge(s_skew, 16 * NG * HEADS)
            for n in range(NG * HEADS):
                diag = skew[n, QB - 1:QB - 1 + 128 * (SKEW - 1)].rearrange("(p x) -> p x", x=SKEW - 1)[:, 0:256]
                sp.dma_start(table[:, n // HEADS, n % HEADS, :], diag).then_inc(s_table, 16)
            sp.wait_ge(s_table, 16 * NG * HEADS)

        @block.tensor
        def _(pe):
            pe.wait_ge(s_spread, 1)
            for n in range(NG * HEADS):
                if n >= 2:
                    pe.wait_ge(s_flat, n - 1)
                pe.matmul(ps[n % 2][:, 0:SKEW], rb_q[:, n % HEADS, :], hot[:, n // HEADS, :],
                          start=True, stop=True).then_inc(s_mm, 1)

        @block.scalar
        def _(act):
            for n in range(NG * HEADS):
                act.wait_ge(s_mm, n + 1)
                act.copy(flat[:, n, :], ps[n % 2][:, 0:SKEW]).then_inc(s_flat, 1)


AT_PER = dict(stage=1, vtr=1, v_sb=1, s=4, s_red=4, neg=4, exps=4, ptr=4, p_sb=4, o=1, o_sb=1, out=16)


def window_attention(nc, qkv, table, ident, partial):
    with ExitStack() as c:
        sems = Semaphores(nc, c)
        def sb(n, shape, dt=F32):
            return c.enter_context(nc.sbuf_tensor(f"wa_{n}", shape, dt))

        S = {n: sems.new(f"wa_{n}") for n in (*AT_PER, "passed")}
        qs = [sb(f"qs{i}", [128, 4, QB]) for i in range(2)]
        ks, vs = ([sb(f"{n}{i}", [128, 4, 256]) for i in range(2)] for n in ("ks", "vs"))
        v_tok = [sb(f"v_tok{i}", [128, 2, CW]) for i in range(2)]
        sc = [sb(f"sc{i}", [128, 2, 256]) for i in range(2)]
        p = [sb(f"p{i}", [128, 2, 256]) for i in range(2)]
        pt = [sb(f"pt{i}", [128, 2, 2, 128]) for i in range(2)]
        neg = [sb(f"neg{i}", [128, HEADS]) for i in range(2)]
        ob = [sb(f"ob{i}", [128, HEADS, DH + 2]) for i in range(2)]
        V_PS = [c.enter_context(nc.psum_tensor(f"wa_vps{i}", [128, 4, 128], F32)) for i in range(2)]
        S_PS = [c.enter_context(nc.psum_tensor(f"wa_sps{i}", [128, 2, 256], F32)) for i in range(2)]
        P_PS = [c.enter_context(nc.psum_tensor(f"wa_pps{i}", [128, 2, 2, 128], F32)) for i in range(2)]
        O_PS = [c.enter_context(nc.psum_tensor(f"wa_ops{i}", [128, HEADS, DH], F32)) for i in range(2)]
        block = c.enter_context(nc.Block())
        AHEAD = 2

        def steps(eng):
            def step(t, par, g, w, col, q0, k0):
                return Place(eng, S, AT_PER, t, AHEAD), par, g, w, col, q0, k0

            yield step(0, 0, 0, 192, 64, 0, 0)
            with eng.Fori(0, 7) as i:
                for par in range(2):
                    q0 = i * 256 + (128 + 128 * par)
                    yield step(i * 2 + (1 + par), 1 - par, 0, 256, 0, q0, i * 256 + (64 + 128 * par))
            yield step(15, 1, 0, 192, 0, T - QB, T - 192)
            with eng.Fori(0, 4) as r:
                for n in range(4):
                    w, col, k0 = ((192, 64, 0), (256, 0, 64), (256, 0, 192), (192, 0, 320))[n]
                    yield step(r * 4 + (16 + n), n % 2, 1, w, col, r + 4 * QB * n, r + 4 * k0)
            with eng.Fori(0, 8) as i:
                for par in range(2):
                    yield step(i * 2 + (32 + par), par, 2, 128, 64, i * 2 + par, i * 2 + par)

        def chunks(w):
            return [(k, min(128, w - 128 * k)) for k in range(-(-w // 128))]

        def group(gi):
            return [(2 * (gi // 2) + jj, gi % 2) for jj in range(2)]

        @block.gpsimd
        def _(pool):
            for at, par, g, w, col, q0, k0 in steps(pool):
                at.settle()
                at.prev("s", 4)
                at.prev("vtr")
                pool.tensor_copy(qs[par][:], qkv[0][:, :, ds(q0, QB, step=DILATIONS[g])])
                pool.tensor_copy(ks[par][:, :, 0:w], qkv[1][:, :, ds(k0, w, step=DILATIONS[g])])
                at.did(pool.tensor_copy(vs[par][:, :, 0:w], qkv[2][:, :, ds(k0, w, step=DILATIONS[g])]), "stage")

        @block.tensor
        def _(pe):
            for at, par, g, w, col, q0, k0 in steps(pe):
                at.need("stage")
                at.prev1("v_sb")
                for k, n in chunks(w):
                    for j in range(4):
                        last = pe.transpose(V_PS[k][0:n, j, :], vs[par][:, j, 128 * k:128 * k + n], ident)
                at.did(last, "vtr")

                def scores(gi):
                    at.need("s_red", gi - 1) if gi >= 2 else at.prev1("s_red", gi + 3)
                    for jj, (j, m) in enumerate(group(gi)):
                        R = slice(DH * m, DH * m + DH)
                        last = pe.matmul(S_PS[gi % 2][:, jj, 0:w], qs[par][R, j, :], ks[par][R, j, 0:w],
                                         start=True, stop=True)
                    at.did(last, "s")

                def values(gi):
                    at.need("exps", gi + 1)
                    at.need("p_sb", gi - 1) if gi >= 2 else at.prev1("p_sb", gi + 3)
                    for jj in range(2):
                        for k, n in chunks(w):
                            last = pe.transpose(P_PS[gi % 2][0:n, jj, k, :], p[gi % 2][:, jj, 128 * k:128 * k + n],
                                                ident)
                    at.did(last, "ptr")

                def outputs(gi):
                    at.need("p_sb", gi + 1)
                    if gi == 0:
                        at.need("v_sb")
                        at.prev("o_sb")
                    for jj, (j, m) in enumerate(group(gi)):
                        for k, n in chunks(w):
                            h = 2 * j + m
                            last = pe.matmul(O_PS[par][:, h, :], pt[gi % 2][0:n, jj, k, :],
                                             v_tok[par][0:n, k, DH * h:DH * h + DH],
                                             start=k == 0, stop=k == len(chunks(w)) - 1)
                    return last

                scores(0)
                scores(1)
                for gi in range(4):
                    values(gi)
                    if gi + 2 < 4:
                        scores(gi + 2)
                    last = outputs(gi)
                at.did(last, "o")

        @block.vector
        def _(dve):
            for at, par, g, w, col, q0, k0 in steps(dve):
                def reduce(gi):
                    at.settle()
                    at.need("s", gi + 1)
                    at.need("exps", gi - 1) if gi >= 2 else at.prev1("exps", gi + 3)
                    if gi == 0:
                        at.prev("out")
                    for jj, (j, m) in enumerate(group(gi)):
                        h = 2 * j + m
                        last = dve.tensor_tensor_reduce(sc[gi % 2][:, jj, 0:w], S_PS[gi % 2][:, jj, 0:w],
                                                        table[:, g, h, col:col + w], 1.0, -3e38, ALU.add, ALU.max,
                                                        ob[par][:, h, DH:DH + 1])
                    at.did(last, "s_red")
                    at.need("s_red", gi + 1)
                    h = 2 * group(gi)[0][0] + gi % 2
                    at.did(dve.tensor_scalar(neg[par][:, h:h + 3:2], ob[par][:, h:h + 3:2, DH], -1.0, None,
                                             ALU.mult), "neg")

                def weights(gi):
                    at.need("ptr", gi + 1)
                    for k, n in chunks(w):
                        last = dve.tensor_copy(pt[gi % 2][0:n, :, k, :], P_PS[gi % 2][0:n, :, k, :])
                    at.did(last, "p_sb")

                reduce(0)
                reduce(1)
                weights(0)
                reduce(2)
                weights(1)
                reduce(3)
                weights(2)
                weights(3)

        @block.scalar
        def _(act):
            for at, par, g, w, col, q0, k0 in steps(act):
                at.need("vtr")
                for k, n in chunks(w):
                    last = act.copy(v_tok[par][0:n, k, :], V_PS[k][0:n].rearrange("p j c -> p (j c)"))
                at.did(last, "v_sb")
                for gi in range(4):
                    at.need("neg", gi + 1)
                    at.need("ptr", gi - 1) if gi >= 2 else at.prev1("ptr", gi + 3)
                    for jj, (j, m) in enumerate(group(gi)):
                        h = 2 * j + m
                        last = act.activation(p[gi % 2][:, jj, 0:w], sc[gi % 2][:, jj, 0:w], ACT.Exp,
                                              bias=neg[par][:, h:h + 1], accum_out=ob[par][:, h, DH + 1:DH + 2])
                    at.did(last, "exps")
                at.need("o")
                at.did(act.copy(ob[par][:, :, 0:DH], O_PS[par][:]), "o_sb")

        @block.sync
        def _(sp):
            for n in AT_PER:
                sp.sem_inc(S[n], AHEAD * AT_PER[n])
            for at, par, g, w, col, q0, k0 in steps(sp):
                at.need("o_sb")
                at.prev1("out")
                at.did(sp.dma_start(partial[g, ds(q0, QB, step=DILATIONS[g]), :],
                                    ob[par][:].rearrange("p h e -> p (h e)")), "out", 16)
            sp.wait_ge(S["out"], 16 * (48 + AHEAD))


MG_PER = dict(top=1, top2=1, low=1, e=1, ed=1, s1=1, s2=1, inv=1, wg=1, prod=1, o1=1, o2=1, tr=1, gated=1)


def merge_attention(nc, partial, z_gate, y2_dram, y2, ident):
    NG = len(DILATIONS)
    with ExitStack() as c:
        sems = Semaphores(nc, c)
        def sb(n, shape, dt=F32):
            return c.enter_context(nc.sbuf_tensor(f"mg_{n}", shape, dt))

        S = {n: sems.new(f"mg_{n}") for n in (*MG_PER, "passed")}
        in_per = dict(in0=16, in1=16, z0=16, z1=16)
        SI = {n: sems.new(f"mg_{n}") for n in in_per}
        SI["passed"] = S["passed"]
        s_y = sems.new("mg_y")
        part = [sb(f"part{i}", [128, NG, HEADS, DH + 2]) for i in range(2)]
        z = [sb(f"z{i}", [128, CB, 128]) for i in range(2)]
        prod = [sb(f"prod{i}", [128, NG, HEADS, DH]) for i in range(2)]
        top, tot, inv = sb("top", [128, HEADS]), sb("tot", [128, HEADS]), sb("inv", [128, HEADS])
        e, ed = sb("e", [128, NG, HEADS]), sb("ed", [128, NG, HEADS])
        ps = [c.enter_context(nc.psum_tensor(f"mg_ps{i}", [128, CB, 128], F32)) for i in range(2)]
        block = c.enter_context(nc.Block())
        z_view = z_gate.rearrange("(j p) t -> p j t", p=128)
        AHEAD = 2

        def tiles(eng):
            with eng.Fori(0, T // 256) as i:
                for par in range(2):
                    yield Place(eng, S, MG_PER, i * 2 + par, AHEAD), Place(eng, SI, in_per, i), par, i * 256 + 128 * par

        def spread(a, g=NG):
            return a.unsqueeze(1).to_broadcast([128, g, HEADS])

        @block.sync
        def _(sp):
            for n in MG_PER:
                sp.sem_inc(S[n], AHEAD * MG_PER[n])
            for n in in_per:
                sp.sem_inc(SI[n], in_per[n])
            for at, pin, par, t0 in tiles(sp):
                at.prev("prod")
                at.prev("ed")
                pin.did(sp.dma_start(part[par][:].rearrange("p g h e -> p g (h e)"),
                                     partial[:, ds(t0, 128), :].rearrange("g p e -> p g e")), f"in{par}", 16)
                at.settle()
                at.prev("gated")
                pin.did(sp.dma_start(z[par][:], z_view[:, :, ds(t0, 128)]), f"z{par}", 16)

        @block.scalar
        def _(act):
            act.dma_start(y2[:, 0:CB, :], y2_dram.rearrange("(k p) t -> p k t", p=128)).then_inc(s_y, 16)
            for at, pin, par, t0 in tiles(act):
                at.need("low")
                at.prev1("wg")
                at.did(act.activation(e[:], ed[:], ACT.Exp), "e")
            act.wait_ge(s_y, 16)

        @block.vector
        def _(dve):
            for at, pin, par, t0 in tiles(dve):
                m, d = part[par][:, :, :, DH], part[par][:, :, :, DH + 1]
                pin.need(f"in{par}")
                at.did(dve.tensor_tensor(top[:], m[:, 0, :], m[:, 1, :], ALU.max), "top")
                at.need("top")
                at.did(dve.tensor_tensor(top[:], top[:], m[:, 2, :], ALU.max), "top2")
                at.need("top2")
                at.did(dve.tensor_tensor(ed[:], m, spread(top[:]), ALU.subtract), "low")
                at.need("e")
                at.did(dve.tensor_tensor(ed[:], e[:], d, ALU.mult), "ed")
                at.need("ed")
                at.did(dve.tensor_tensor(tot[:], ed[:, 0, :], ed[:, 1, :], ALU.add), "s1")
                at.need("s1")
                at.did(dve.tensor_tensor(tot[:], tot[:], ed[:, 2, :], ALU.add), "s2")
                at.need("s2")
                at.did(dve.reciprocal(inv[:], tot[:]), "inv")
                at.need("inv")
                at.did(dve.tensor_tensor(e[:], e[:], spread(inv[:]), ALU.mult), "wg")
                at.need("wg")
                at.prev("tr")
                at.did(dve.tensor_tensor(prod[par][:], part[par][:, :, :, 0:DH],
                                         e[:].unsqueeze(3).to_broadcast([128, NG, HEADS, DH]), ALU.mult), "prod")
                at.need("tr")
                pin.need(f"z{par}")
                at.did(dve.tensor_tensor(y2[:, CB:2 * CB, ds(t0, 128)], ps[par][:], z[par][:], ALU.mult), "gated")

        @block.gpsimd
        def _(pool):
            for at, pin, par, t0 in tiles(pool):
                at.need("prod")
                at.did(pool.tensor_tensor(prod[par][:, 0], prod[par][:, 0], prod[par][:, 1], ALU.add), "o1")
                at.need("o1")
                at.did(pool.tensor_tensor(prod[par][:, 0], prod[par][:, 0], prod[par][:, 2], ALU.add), "o2")

        @block.tensor
        def _(pe):
            for at, pin, par, t0 in tiles(pe):
                at.need("o2")
                at.prev("gated")
                for j in range(CB):
                    last = pe.transpose(ps[par][:, j, :], prod[par][:, 0, 2 * j:2 * j + 2, :]
                                        .rearrange("p h d -> p (h d)"), ident)
                at.did(last, "tr")


def build(nc, xT, vecs, consts, w_in, w_up, a_up, w_out, w_in2, cvec, gains, rel_bias, onehot, w_out2, outT,
          dbg=None):
    NG = len(DILATIONS)

    def dram(n, shape):
        if dbg and n in dbg:
            return dbg[n]
        return nc.dram_tensor(n, shape, F32, kind="Internal").ap()

    proj, yT, x2T = dram("proj", (6, D, T)), dram("yT", (D, T)), dram("x2T", (D, T))
    y_conv, z_gate = dram("y_conv", (CW, T)), dram("z_gate", (CW, T))
    skew, partial = dram("skew", (NG * HEADS, 128 * SKEW)), dram("partial", (NG, T, OROW))
    with ExitStack() as c:
        sems = Semaphores(nc, c)
        vec = c.enter_context(nc.sbuf_tensor("vec", [128, NVEC], F32))
        cst = c.enter_context(nc.sbuf_tensor("cst", [128, C_TOTAL], F32))
        ones = c.enter_context(nc.sbuf_tensor("ones", [128, 128], F32))
        s_const = sems.new("s_const")
        with nc.Block() as block:
            @block.sync
            def _(sp):
                sp.dma_start(vec[:], vecs).then_inc(s_const, 16)
                sp.dma_start(cst[:], consts).then_inc(s_const, 16)
                sp.wait_ge(s_const, 33)

            @block.gpsimd
            def _(pool):
                pool.memset(ones[:], 1.0).then_inc(s_const, 1)
        ident, headsum = (cst[:, C_AT[n]:C_AT[n] + 128] for n in ("ident", "headsum"))
        with ExitStack() as c1:
            h = c1.enter_context(nc.sbuf_tensor("h", [128, KT, T + 1], F32))
            s_zero = Semaphores(nc, c1).new("s_zero")
            with nc.Block() as block:
                @block.gpsimd
                def _(pool):
                    pool.memset(h[:, :, 0:1], 0.0).then_inc(s_zero, 1)
                    pool.wait_ge(s_zero, 1)
            norm_phase(nc, "n1", xT.rearrange("(k p) t -> p k t", p=128), h[:, :, 1:T + 1],
                       vec[:, V["norm1"]:V["norm1"] + KT], ones)
            rwkv_projections(nc, h, vec, w_in, w_up, a_up, proj)
        rwkv_recurrence(nc, proj, yT, vec, cst)
        with ExitStack() as c2:
            y = c2.enter_context(nc.sbuf_tensor("y", [128, KT, T], F32))
            output_projection(nc, "o1", yT, y, w_out, xT, x2T)
        with ExitStack() as c3:
            qkv = [c3.enter_context(nc.sbuf_tensor(f"qkv{i}", [128, CB, T], F32)) for i in range(3)]
            with ExitStack() as c4:
                h2 = c4.enter_context(nc.sbuf_tensor("h2", [128, KT, T], F32))
                norm_phase(nc, "n2", x2T.rearrange("(k p) t -> p k t", p=128), h2,
                           vec[:, V["norm2"]:V["norm2"] + KT], ones)
                conv_branch(nc, h2, w_in2, cvec, y_conv)
                attention_projections(nc, h2, w_in2, qkv, gains, headsum, z_gate)
            table = c3.enter_context(nc.sbuf_tensor("table", [128, NG, HEADS, 256], F32))
            bias_tables(nc, rel_bias, onehot, skew, table)
            window_attention(nc, qkv, table, ident, partial)
        with ExitStack() as c4:
            y2 = c4.enter_context(nc.sbuf_tensor("y2", [128, KT, T], F32))
            merge_attention(nc, partial, z_gate, y_conv, y2, ident)
            output_projection(nc, "o2", None, y2, w_out2, x2T, outT)


def kernel(**inputs):
    import concourse.bacc as bacc
    from concourse.bass_utils import run_bass_kernel_spmd

    a = {k: np.asarray(v) for k, v in inputs.items()}
    order = [a["l0_norm"], *(a["l0_mu"][i] for i in (0, 2, 3, 5, 1, 4)), a["l0_w0"], a["l0_a0"], a["l0_k_k"],
             a["l0_k_a"], a["l0_r_k"].reshape(-1), a["l0_gn_w"], a["l0_gn_b"], a["norm_w_2"]]
    conv = np.concatenate([a["conv_w_2"], a["conv_b_2"][None]])
    arrays = dict(
        xT=a["x"][0].T,
        vecs=np.stack(order).reshape(-1, KT, 128).transpose(2, 0, 1).reshape(128, -1),
        consts=shape_constants(),
        w_in=a["l0_w_in"], w_up=a["l0_w_up"], a_up=a["l0_a_up"], w_out=a["l0_w_out"], w_in2=a["w_in_2"],
        cvec=conv.reshape(4, CB, 128).transpose(2, 0, 1),
        gains=np.stack([np.tile(a["q_norm_w_2"], 2), np.tile(a["k_norm_w_2"], 2)], 1),
        rel_bias=a["rel_bias_2"], onehot=bucket_constants(), w_out2=a["w_out_2"],
    )
    arrays = {k: np.ascontiguousarray(v) for k, v in arrays.items()}
    nc = bacc.Bacc("TRN2", target_bir_lowering=False, num_devices=1)
    aps = {k: nc.dram_tensor(k, v.shape, F32, kind="ExternalInput").ap() for k, v in arrays.items()}
    outT = nc.dram_tensor("outT", (D, T), F32, kind="ExternalOutput").ap()
    build(nc, **aps, outT=outT)
    r = run_bass_kernel_spmd(nc, [arrays], core_ids=[0])
    return np.ascontiguousarray(r.results[0]["outT"].T)[None]
```

```python
import math
from contextlib import ExitStack

import numpy as np
import concourse.bass as bass
from concourse import mybir

F32 = mybir.dt.float32
F16 = mybir.dt.float16
ALU = mybir.AluOpType
ACT = mybir.ActivationFunctionType
AX = mybir.AxisListType
ds = bass.ds

T = 2048
D = 1024
KT = D // 128
HALF = T // 2
HB = HALF // 512
RANK = 64
EPS = 1e-6

VEC_NAMES = ["norm1", "mu_r", "mu_k", "mu_v", "mu_g", "mu_w", "mu_a", "w0", "a0", "k_k", "k_a", "r_k",
             "gn_w", "gn_b", "norm2"]
V = {n: KT * i for i, n in enumerate(VEC_NAMES)}
NVEC = KT * len(VEC_NAMES)


class Semaphores:

    def __init__(self, nc, scope):
        self.nc, self.made = nc, []
        scope.callback(self.clear)

    def new(self, name):
        self.made.append(self.nc.alloc_semaphore(name))
        return self.made[-1]

    def clear(self):
        self.nc.clear_and_free_semaphores(self.made)
        self.nc.all_engine_barrier()


def firm_wait(eng, sem, value, passed):
    eng.wait_ge(sem, value)
    eng.sem_inc(passed, 1)


class Place:

    def __init__(self, eng, sems, per, t, ahead=1, lag=0):
        self.eng, self.sems, self.per, self.t, self.ahead, self.sent = eng, sems, per, t, ahead, {}
        self.lag = lag
        self.firm = False

    def settle(self):
        self.firm = True

    def back(self, steps, name, k):
        per = self.per[name]
        value = self.t * per + ((self.ahead - steps - self.lag) * per + (per if k is None else k))
        if self.firm and not isinstance(value, int):
            firm_wait(self.eng, self.sems[name], value, self.sems["passed"])
        else:
            self.eng.wait_ge(self.sems[name], value)

    def need(self, name, k=None):
        self.back(0, name, k)

    def prev1(self, name, k=None):
        self.back(1, name, k)

    def prev(self, name, k=None):
        self.back(self.ahead, name, k)

    def did(self, ins, name, by=1):
        ins.then_inc(self.sems[name], by)
        self.firm = False
        self.sent[name] = self.sent.get(name, 0) + by

    def end(self):
        for n, k in self.sent.items():
            assert k == self.per[n], (n, k)


def norm_phase(nc, name, src, h, gain, ones):
    NB = T // 512
    with ExitStack() as c:
        sems = Semaphores(nc, c)
        sq = [c.enter_context(nc.sbuf_tensor(f"{name}_sq{i}", [128, 512], F32)) for i in range(4)]
        var = c.enter_context(nc.sbuf_tensor(f"{name}_var", [128, T], F32))
        rstd = c.enter_context(nc.sbuf_tensor(f"{name}_rstd", [128, T], F32))
        total = [c.enter_context(nc.psum_tensor(f"{name}_total{i}", [128, 512], F32)) for i in range(NB)]
        loaded = [sems.new(f"{name}_loaded{k}") for k in range(KT)]
        squared = sems.new(f"{name}_squared")
        summed = sems.new(f"{name}_summed")
        meaned = sems.new(f"{name}_meaned")
        rooted = sems.new(f"{name}_rooted")
        inverted = sems.new(f"{name}_inverted")
        block = c.enter_context(nc.Block())

        @block.sync
        def _(sp):
            for k in range(KT):
                if src is not None:
                    sp.dma_start(h[:, k, :], src[:, k, :]).then_inc(loaded[k], 16)

        @block.scalar
        def _(act):
            for b in range(NB):
                for k in range(KT):
                    n = b * KT + k
                    if src is not None:
                        act.wait_ge(loaded[k], 16)
                    if n >= 4:
                        act.wait_ge(summed, n - 3)
                    act.activation(sq[n % 4][:], h[:, k, 512 * b:512 * b + 512], ACT.Square).then_inc(squared, 1)
            for b in range(NB):
                act.wait_ge(meaned, b + 1)
                act.activation(rstd[:, 512 * b:512 * b + 512], var[:, 512 * b:512 * b + 512],
                               ACT.Sqrt).then_inc(rooted, 1)

        @block.tensor
        def _(pe):
            for b in range(NB):
                for k in range(KT):
                    pe.wait_ge(squared, b * KT + k + 1)
                    pe.matmul(total[b][:], ones[:], sq[(b * KT + k) % 4][:],
                              start=k == 0, stop=k == KT - 1).then_inc(summed, 1)

        @block.vector
        def _(dve):
            for b in range(NB):
                dve.wait_ge(summed, KT * (b + 1))
                dve.tensor_scalar(var[:, 512 * b:512 * b + 512], total[b][:], 1.0 / D, EPS,
                                  ALU.mult, ALU.add).then_inc(meaned, 1)
            for b in range(NB):
                col = slice(512 * b, 512 * b + 512)
                dve.wait_ge(rooted, b + 1)
                dve.reciprocal(var[:, col], rstd[:, col]).then_inc(inverted, 1)
                dve.wait_ge(inverted, b + 1)
                for k in range(KT):
                    dve.scalar_tensor_tensor(h[:, k, col], h[:, k, col], gain[:, k:k + 1], var[:, col],
                                             ALU.mult, ALU.mult)


def rwkv_projections(nc, h, vec, w_in, w_up, a_up, proj):
    with ExitStack() as c:
        sems = Semaphores(nc, c)
        def sb(n, shape, dt=F32):
            return c.enter_context(nc.sbuf_tensor(f"pj_{n}", shape, dt))

        def sem(n):
            return sems.new(f"pj_{n}")

        xs = [sb(f"xs{i}", [128, KT, HALF]) for i in range(2)]
        diff = [sb(f"diff{i}", [128, HALF]) for i in range(2)]
        w = [sb(f"w{i}", [128, KT, 128]) for i in range(2)]
        out_sb = [sb(f"out{i}", [128, HALF]) for i in range(2)]
        lo_w = sb("lo_w", [128, KT, 2 * RANK])
        lo = [sb(f"lo{i}", [RANK, T]) for i in range(2)]
        up = [sb(f"up{i}", [RANK, D]) for i in range(2)]
        ps = [c.enter_context(nc.psum_tensor(f"pj_ps{i}", [128, HALF], F32)) for i in range(2)]
        s_diff, s_xs = sem("diff"), sem("xs")
        s_w = [sem(f"w{i}") for i in range(2)]
        s_mm, s_ps_free = sem("mm"), sem("ps_free")
        s_out = [sem(f"out{i}") for i in range(2)]
        s_small, s_passed = sem("small"), sem("passed")
        block = c.enter_context(nc.Block())
        MAIN = 4 * 2 * KT
        w_cols = w_in.rearrange("(k p) n -> p k n", p=128)
        proj_rows = proj.rearrange("q (j p) t -> q p j t", p=128)

        def uses(q, hv):
            return (2 * q + hv + 1) * KT if q < 4 else MAIN + 2 * (q - 4) + hv + 1

        @block.gpsimd
        def _(pool):
            for q in range(6):
                for hv in range(2):
                    for k in range(KT):
                        n = (2 * q + hv) * KT + k
                        if n >= 2:
                            pool.wait_ge(s_xs, n - 1)
                        pool.tensor_tensor(diff[n % 2][:], h[:, k, hv * HALF:hv * HALF + HALF],
                                           h[:, k, hv * HALF + 1:hv * HALF + HALF + 1],
                                           ALU.subtract).then_inc(s_diff, 1)

        @block.vector
        def _(dve):
            for q in range(6):
                for hv in range(2):
                    if q > 0:
                        dve.wait_ge(s_mm, uses(q - 1, hv))
                    for k in range(KT):
                        n = (2 * q + hv) * KT + k
                        m = V["mu_r"] + q * KT + k
                        dve.wait_ge(s_diff, n + 1)
                        dve.scalar_tensor_tensor(xs[hv][:, k, :], diff[n % 2][:], vec[:, m:m + 1],
                                                 h[:, k, hv * HALF + 1:hv * HALF + HALF + 1],
                                                 ALU.mult, ALU.add).then_inc(s_xs, 1)

        @block.sync
        def _(sp):
            def load(i, n2):
                col = (n2 // KT) * D + ((n2 * 2 + i) % KT) * 128
                sp.dma_start(w[i][:], w_cols[:, :, ds(col, 128)]).then_inc(s_w[i], 16)

            for i in range(2):
                load(i, 0)
            sp.dma_start(lo_w[:], w_cols[:, :, 4 * D:4 * D + 2 * RANK]).then_inc(s_small, 16)
            sp.dma_start(up[0][:], w_up).then_inc(s_small, 16)
            sp.dma_start(up[1][:], a_up).then_inc(s_small, 16)
            with sp.Fori(1, MAIN // 2) as n2:
                for i in range(2):
                    sp.wait_ge(s_mm, n2 * 2 + i - 1)
                    load(i, n2)

        @block.tensor
        def _(pe):
            with pe.Fori(0, 4) as q:
                for hv in range(2):
                    firm_wait(pe, s_xs, q * (2 * KT) + (hv + 1) * KT, s_passed)
                    with pe.Fori(0, KT // 2) as c2:
                        for i in range(2):
                            n = q * (2 * KT) + c2 * 2 + (hv * KT + i)
                            pe.wait_ge(s_w[i], q * (16 * KT) + c2 * 16 + (hv * 8 * KT + 16))
                            pe.wait_ge(s_ps_free, n + 1)
                            for k in range(KT):
                                for b in range(HB):
                                    last = pe.matmul(ps[i][:, 512 * b:512 * b + 512], w[i][:, k, :],
                                                     xs[hv][:, k, 512 * b:512 * b + 512],
                                                     start=k == 0, stop=k == KT - 1)
                            last.then_inc(s_mm, 1)
            pe.wait_ge(s_small, 48)
            n = MAIN
            for r in range(2):
                for hv in range(2):
                    pe.wait_ge(s_xs, ((4 + r) * 2 + hv + 1) * KT)
                    pe.wait_ge(s_ps_free, n + 1)
                    for k in range(KT):
                        for b in range(HB):
                            last = pe.matmul(ps[n % 2][0:RANK, 512 * b:512 * b + 512],
                                             lo_w[:, k, r * RANK:(r + 1) * RANK],
                                             xs[hv][:, k, 512 * b:512 * b + 512],
                                             start=k == 0, stop=k == KT - 1)
                    last.then_inc(s_mm, 1)
                    n += 1
            for r in range(2):
                for j in range(KT):
                    for hv in range(2):
                        pe.wait_ge(s_ps_free, MAIN + 2 * r + hv + 3)
                        pe.wait_ge(s_ps_free, n + 1)
                        for b in range(HB):
                            t0 = hv * HALF + 512 * b
                            last = pe.matmul(ps[n % 2][:, 512 * b:512 * b + 512], up[r][:, 128 * j:128 * j + 128],
                                             lo[r][:, t0:t0 + 512], start=True, stop=True)
                        last.then_inc(s_mm, 1)
                        n += 1

        @block.scalar
        def _(act):
            act.sem_inc(s_ps_free, 2)
            act.sem_inc(s_out[0], 16)
            act.sem_inc(s_out[1], 16)

            with act.Fori(0, 4) as q:
                for hv in range(2):
                    with act.Fori(0, KT // 2) as c2:
                        for i in range(2):
                            n = q * (2 * KT) + c2 * 2 + (hv * KT + i)
                            use = q * KT + c2 + hv * (KT // 2)
                            act.wait_ge(s_mm, n + 1)
                            act.wait_ge(s_out[i], use * 16 + 16)
                            act.copy(out_sb[i][:], ps[i][:]).then_inc(s_ps_free, 1)
                            act.wait_ge(s_ps_free, n + 3)
                            act.dma_start(proj_rows[ds(q, 1), :, ds(c2 * 2 + i, 1), hv * HALF:(hv + 1) * HALF]
                                          .rearrange("q p j t -> p (q j t)"), out_sb[i][:]).then_inc(s_out[i], 16)
            n = MAIN
            for r in range(2):
                for hv in range(2):
                    act.wait_ge(s_mm, n + 1)
                    act.activation(lo[r][:, hv * HALF:(hv + 1) * HALF], ps[n % 2][0:RANK, :],
                                   ACT.Tanh if r == 0 else ACT.Copy).then_inc(s_ps_free, 1)
                    n += 1
            use = MAIN // 2
            for r in range(2):
                for j in range(KT):
                    for hv in range(2):
                        v = V["w0" if r == 0 else "a0"] + j
                        act.wait_ge(s_mm, n + 1)
                        act.wait_ge(s_out[n % 2], use * 16 + 16)
                        act.activation(out_sb[n % 2][:], ps[n % 2][:], ACT.Sigmoid,
                                       bias=vec[:, v:v + 1]).then_inc(s_ps_free, 1)
                        act.wait_ge(s_ps_free, n + 3)
                        act.dma_start(proj_rows[4 + r, :, j, hv * HALF:(hv + 1) * HALF],
                                      out_sb[n % 2][:]).then_inc(s_out[n % 2], 16)
                        n += 1
                        use += hv
            for i in range(2):
                act.wait_ge(s_out[i], (use + 1) * 16)



CHUNK = 64
NCH = 128 // CHUNK
RW_HEADS = 16
RW_N = 64
DECAY = math.exp(-0.5)
GN_EPS = 64e-5
LEVELS = [1, 2, 4, 8, 16, 32]

C_WIDTHS = {"ident": 128, "headsum": 128, "maskA": 512, "maskL": 128, "merge": 128 * len(LEVELS), "select": 32 * KT, "selectT": 128 * KT,
            "restart": 1024}
C_AT, _at = {}, 0
for _n, _w in C_WIDTHS.items():
    C_AT[_n] = _at
    _at += _w
C_TOTAL = _at


def shape_constants():
    s = np.arange(128)[:, None]
    t = np.arange(128)[None, :]
    same = s // CHUNK == t // CHUNK
    strict, incl = same & (s < t), same & (s <= t)
    out = np.zeros((128, C_TOTAL), np.float32)

    def put(name, a):
        out[:, C_AT[name]:C_AT[name] + C_WIDTHS[name]] = a

    put("maskA", np.concatenate([strict, incl, strict, incl], 1))
    put("maskL", same & (s > t))
    merge = [(s // (2 * b) == t // (2 * b)) & (s // b % 2 == 1) & (t // b % 2 == 0) for b in LEVELS]
    put("merge", np.concatenate(merge, 1))
    put("ident", s == t)
    put("headsum", s // RW_N == t // RW_N)
    pairs = np.arange(KT)
    put("select", (np.arange(32) == 2 * pairs[:, None] + s[:, :, None] // RW_N).reshape(128, KT * 32))
    head = np.arange(32)[:, None]
    spread = np.concatenate([head == 2 * j + t // RW_N for j in range(KT)], 1)
    put("selectT", np.concatenate([spread, np.zeros((96, 128 * KT))]))
    put("restart", np.broadcast_to(np.arange(1024)[None, :] % CHUNK != 0, (128, 1024)))
    return out


RW_PER = dict(
    in_r=16, in_k=16, in_v=16, in_g=16, in_sw=16, in_a=16,
    scan=1, exps=2, dec=1, kkr=1, ksq=1, ksum=1, kroot=1, kclamp=1, kinv=1, kspread=1, kk=1, am=1, kp=1, at=1, rt=1, b=1, bt=1, kt=1,
    rk=1, trans=8, tok=8, amat=16, amat_sb=16, lmat=4, lmat_sb=4, l_hi=4, l_lo=4, lt16=4,
    w=20, w_sb=24, xy=24, xy_sb=24, e=4, e_sb=4, yt=4, yt_sb=4,
    t1=2, t1_sb=2, u0=2, u0_sb=2, wt=2, wt_sb=2, u=2, u_sb=2, m=2, m_add=2, m_sb=2, m_copy=1,
    y=1, y_sb=1, mean=1, yc=1, ysq=1, var=1, ystd=1, yinv=1, yspread=1, yn=1, yw=1, yb=1, bonus=1, bv=1, ysum=1,
    gsig=1, gs=1, yout=1, stored=16,
)


def rwkv_recurrence(nc, proj, yT, vec, consts):
    with ExitStack() as c:
        sems = Semaphores(nc, c)
        def sb(n, shape, dt=F32):
            return c.enter_context(nc.sbuf_tensor(f"rw_{n}", shape, dt))

        S = {n: sems.new(f"rw_{n}") for n in (*RW_PER, "passed")}
        s_init, s_const = sems.new("rw_init"), sems.new("rw_const")
        cst = sb("cst", [128, C_TOTAL])
        tile = [128, KT, 128]
        r_in, k_in, v_in, g_in, sw_in, a_in = (sb(n, tile) for n in ("r", "k", "v", "g", "sw", "a"))
        inputs = dict(r=r_in, k=k_in, v=v_in, g=g_in, sw=sw_in, a=a_in)
        csum = sb("csum", tile)
        pe1 = sb("pe1", [128, KT, NCH, CHUNK + 1])
        dec = sb("dec", [128, KT, NCH])
        pinv = sb("pinv", tile)
        kkr, tmp, am = (sb(n, tile) for n in ("kkr", "tmp", "am"))
        yraw, yn, ysq, bv = (sb(n, tile) for n in ("yraw", "yn", "ysq", "bv"))
        ar = sb("ar", [128, KT, 256])
        bt, kt, rk, ybuf = (sb(n, tile) for n in ("bt", "kt", "rk", "ybuf"))
        tok = [sb(f"tok{i}", tile) for i in range(4)]
        v_tok, b_tok, k_tok, a_tok = tok
        amat = sb("amat", [128, 2, KT, 512])
        four = [128, 4, 128]
        lmat = [sb(f"lmat{g}", four) for g in range(2)]
        l_hi, l_lo, lt16, x16, y16, w16 = ([sb(f"{n}{g}", four, F16) for g in range(2)]
                                           for n in ("l_hi", "l_lo", "lt16", "x16", "y16", "w16"))
        ident16, negid16 = sb("ident16", [128, 128], F16), sb("negid16", [128, 128], F16)
        xt32 = sb("xt32", [128, 2, KT, 128])
        t1, u0, utok = (sb(n, [128, 2, KT, RW_N]) for n in ("t1", "u0", "utok"))
        wt = sb("wt", tile)
        mst = [sb(f"m{i}", [128, KT, RW_N]) for i in range(NCH + 1)]
        mtmp = sb("mtmp", [128, KT, RW_N])
        rkbd = sb("rkbd", tile)
        gneps = sb("gneps", [32, 1])
        kinv, yinv = (sb(n, [32, 128]) for n in ("kinv", "yinv"))
        PS = c.enter_context(nc.psum_tensor("rw_ps", [128, 8, 512], F32))

        def bc(v):
            return vec[:, V[v]:V[v] + KT].unsqueeze(2).to_broadcast(tile)

        def const(name, i=0):
            at = C_AT[name] + 128 * i
            return cst[:, at:at + 128]

        def sel(j):
            at = C_AT["select"] + 32 * j
            return cst[:, at:at + 32]

        def sel_t(j):
            at = C_AT["selectT"] + 128 * j
            return cst[0:32, at:at + 128]

        def four_of(a):
            return a.unsqueeze(1).to_broadcast(four)

        def rows(g):
            return slice(RW_N * g, RW_N * (g + 1))

        def bank(b, w=128):
            return PS[:, b, :].rearrange("p (j w) -> p j w", w=w)

        def two(b, w=128):
            return PS[:, b:b + 2, :].rearrange("p b (j w) -> p (b j) w", w=w)

        XB, YB = (2, 4), (3, 5)
        TRB = (0, 1, 6, 7)

        def level(hf, l, g):
            return hf * 12 + l * 2 + g + 1

        def product(hf, l, g):
            return hf * 10 + (l - 1) * 2 + g + 1

        block = c.enter_context(nc.Block())
        p_view = proj.rearrange("q (j p) t -> q p j t", p=128)
        y_view = yT.rearrange("(j p) t -> p j t", p=128)
        TILES = T // 128

        def run(eng, step):
            step(Place(eng, S, RW_PER, 0), None)
            with eng.Fori(1, TILES) as t:
                f, b = Place(eng, S, RW_PER, t), Place(eng, S, RW_PER, t, lag=1)
                step(f, b)
                for place in (f, b):
                    place.end()
                assert not set(f.sent) & set(b.sent)
            step(None, Place(eng, S, RW_PER, TILES - 1))

        @block.sync
        def _(sp):
            def load(f, name, q, freed):
                f.settle()
                for n in freed:
                    f.prev(n)
                at = f.t * 128
                f.did(sp.dma_start(inputs[name][:], p_view[q, :, :, ds(at, 128)]), f"in_{name}", 16)

            def step(f, b):
                if f:
                    load(f, "sw", 4, ["scan"])
                    load(f, "k", 1, ["kkr", "kp"])
                    load(f, "a", 5, ["am", "b"])
                    load(f, "r", 0, ["rt", "rk"])
                    load(f, "v", 2, ["bv", "trans"])
                    load(f, "g", 3, ["gs"])
                if b:
                    b.need("yout")
                    at = (b.t - b.lag) * 128 if isinstance(b.t, int) else b.t * 128 - 128 * b.lag
                    b.did(sp.dma_start(y_view[:, :, ds(at, 128)], ybuf[:]), "stored", 16)

            sp.dma_start(cst[:], consts).then_inc(s_const, 16)
            for n in RW_PER:
                sp.sem_inc(S[n], RW_PER[n])
            run(sp, step)
            sp.wait_ge(S["stored"], 16 * (TILES + 1))

        @block.gpsimd
        def _(pool):
            pool.wait_ge(s_const, 16)
            pool.memset(pe1[:, :, :, 0:1], 1.0).then_inc(s_init, 1)
            pool.memset(mst[0][:], 0.0).then_inc(s_init, 1)
            pool.memset(gneps[:], GN_EPS).then_inc(s_init, 1)
            pool.tensor_copy(ident16[:], const("ident")).then_inc(s_init, 1)
            pool.tensor_scalar(negid16[:], const("ident"), -1.0, None, ALU.mult).then_inc(s_init, 1)
            for j in range(KT):
                pool.tensor_scalar(rkbd[:, j, :], const("headsum"), vec[:, V["r_k"] + j:V["r_k"] + j + 1], None,
                                   ALU.mult).then_inc(s_init, 1)

            def split_l(f, hf):
                for g in range(2):
                    G = 2 * hf + g + 1
                    f.settle()
                    f.need("lmat_sb", G)
                    f.did(pool.tensor_copy(l_hi[g][:], lmat[g][:]), "l_hi")
                    f.need("l_hi", G)
                    f.did(pool.tensor_tensor(l_lo[g][:], lmat[g][:], l_hi[g][:], ALU.subtract), "l_lo")

            def step(f, b):
                if f:
                    f.need("in_k")
                    f.prev("at")
                    f.did(pool.tensor_tensor(kkr[:], k_in[:], bc("k_k"), ALU.mult), "kkr")
                    f.need("kk")
                    f.need("in_a")
                    f.prev("lmat")
                    f.did(pool.tensor_tensor(bt[:], kkr[:], a_in[:], ALU.mult), "b")
                    split_l(f, 0)
                    f.need("kp")
                    f.need("in_r")
                    f.prev("bonus")
                    f.did(pool.tensor_tensor(rk[:], r_in[:], am[:], ALU.mult), "rk")
                if b:
                    b.need("gsig")
                    b.did(pool.tensor_tensor(ybuf[:], g_in[:], ybuf[:], ALU.mult), "gs")
                    b.need("yn")
                    b.did(pool.tensor_tensor(yn[:], yn[:], bc("gn_w"), ALU.mult), "yw")
                    b.need("yw")
                    b.did(pool.tensor_tensor(yn[:], yn[:], bc("gn_b"), ALU.add), "yb")
                if f:
                    split_l(f, 1)

            run(pool, step)

        @block.scalar
        def _(act):
            act.wait_ge(s_const, 16)
            act.wait_ge(s_init, 5 + KT)
            heads_of = "p (g j w) -> p g j w"

            def inverse(f, b, hf):
                for g in range(2):
                    f.need("amat_sb", 8 * hf + 8)
                    f.did(act.copy(lt16[g][:], amat[:, g, 4 * hf:4 * hf + 4, 0:128]), "lt16")
                for l in range(6):
                    for g in range(2):
                        f.need("xy", level(hf, l, g))
                        act.copy(x16[g][:], bank(XB[g]))
                        f.did(act.copy(y16[g][:], bank(YB[g])), "xy_sb")
                    if hf == 0 and l == 1 and b:
                        b.need("yc")
                        b.did(act.activation(ysq[:], yn[:], ACT.Square), "ysq")
                    if hf == 0 and l == 3 and b:
                        std(b)
                    if hf == 1 and l == 0:
                        t1_copy(f, 0)
                    if hf == 1 and l == 1:
                        u0_copy(f, 0)
                    if hf == 1 and l == 2:
                        wt_copy(f, 0)
                    if hf == 1 and l == 4:
                        t1_copy(f, 1)
                for g in range(2):
                    f.need("yt", 2 * hf + g + 1)
                    f.did(act.copy(xt32[:, g, 4 * hf:4 * hf + 4, :], bank(YB[g])), "yt_sb")

            def std(b):
                b.need("var")
                b.prev("yspread")
                b.did(act.activation(yinv[:], PS[0:32, 6, 0:128], ACT.Sqrt, bias=gneps[:], scale=1.0 / RW_N), "ystd")

            def t1_copy(f, hf):
                f.need("t1", hf + 1)
                f.did(act.copy(t1[:, :, 4 * hf:4 * hf + 4, :], PS[:, 0, :].rearrange(heads_of, g=2, w=RW_N)), "t1_sb")

            def u0_copy(f, hf):
                f.need("u0", hf + 1)
                f.did(act.copy(u0[:, :, 4 * hf:4 * hf + 4, :], PS[:, 1, :].rearrange(heads_of, g=2, w=RW_N)), "u0_sb")

            def wt_copy(f, hf):
                f.need("wt", hf + 1)
                f.did(act.copy(wt[:, 4 * hf:4 * hf + 4, :], bank(0)), "wt_sb")

            def step(f, b):
                if f:
                    f.need("scan")
                    f.prev("at")
                    f.prev("bt")
                    f.prev("dec")
                    flat = csum[:].rearrange("p j (c s) -> p j c s", s=CHUNK)
                    f.did(act.activation(pe1[:, :, :, 1:CHUNK + 1], flat, ACT.Exp, scale=-DECAY), "exps")
                    f.did(act.activation(pinv[:], csum[:], ACT.Exp, scale=DECAY), "exps")
                    f.need("kkr")
                    f.did(act.activation(tmp[:], kkr[:], ACT.Square), "ksq")
                    f.need("ksum")
                    f.prev("kspread")
                    f.did(act.activation(kinv[:], PS[0:32, 6, 0:128], ACT.Sqrt), "kroot")
                if b:
                    b.need("y")
                    b.prev("mean")
                    b.prev("yc")
                    b.did(act.copy(yraw[:], two(4)), "y_sb")
                    b.need("m_sb")
                    b.did(act.copy(mst[0][:], mst[2][:]), "m_copy")
                if f:
                    for i in range(8):
                        f.need("trans", i + 1)
                        f.did(act.copy(tok[i // 2][:, 4 * (i % 2):4 * (i % 2) + 4, :], bank(TRB[i % 4])), "tok")
                    f.need("exps")
                    f.prev("m_sb")
                    f.did(act.copy(dec[:], pe1[:, :, :, CHUNK]), "dec")
                    inverse(f, b, 0)
                elif b:
                    b.need("yc")
                    b.did(act.activation(ysq[:], yn[:], ACT.Square), "ysq")
                    std(b)
                if b:
                    b.need("in_g")
                    b.prev("stored")
                    b.did(act.activation(ybuf[:], g_in[:], ACT.Sigmoid), "gsig")
                if f:
                    inverse(f, b, 1)
                    u0_copy(f, 1)
                    wt_copy(f, 1)

            run(act, step)

        @block.vector
        def _(dve):
            dve.wait_ge(s_const, 16)
            dve.wait_ge(s_init, 5 + KT)
            split = "p j (c s) -> p j c s"

            def masked(f, n):
                f.need("amat", n + 1)
                f.did(dve.tensor_tensor(amat[:, n % 2, n // 2, :], PS[:, n % 2, :],
                                        cst[:, C_AT["maskA"]:C_AT["maskA"] + 512], ALU.mult), "amat_sb")

            def u_sum(b, ci):
                s = slice(CHUNK * ci, CHUNK * (ci + 1))
                b.need("u0_sb")
                b.need("u", ci + 1)
                b.did(dve.tensor_tensor(utok[s].rearrange("p g j v -> p g (j v)"), PS[s, 6:8, :],
                                        u0[s].rearrange("p g j v -> p g (j v)"), ALU.add), "u_sb")

            def m_next(b, ci):
                if ci == 0:
                    b.prev("m_copy")
                else:
                    b.need("m_sb", ci)
                b.need("m", ci + 1)
                b.did(dve.tensor_tensor(mtmp[:], bank(2 + ci, RW_N), mst[ci][:], ALU.add), "m_add")
                b.need("m_add", ci + 1)
                b.need("dec")
                b.did(dve.tensor_tensor(mst[ci + 1][:], mtmp[:], dec[:, :, ci:ci + 1].to_broadcast([128, KT, RW_N]),
                                        ALU.mult), "m_sb")

            def centre(b):
                b.need("mean")
                b.need("y_sb")
                b.prev("yout")
                b.did(dve.scalar_tensor_tensor(yn[:], two(6), -1.0 / RW_N, yraw[:], ALU.mult, ALU.add), "yc")

            def inverse_std(b):
                b.need("ystd")
                b.did(dve.reciprocal(yinv[:], yinv[:]), "yinv")

            def scale(b):
                b.need("yspread")
                b.did(dve.tensor_tensor(yn[:], yn[:], two(6), ALU.mult), "yn")

            def finish(b):
                b.need("yb")
                b.need("bv")
                b.did(dve.tensor_tensor(yn[:], yn[:], bv[:], ALU.add), "ysum")
                b.need("ysum")
                b.need("gs")
                b.did(dve.tensor_tensor(ybuf[:], yn[:], ybuf[:], ALU.mult), "yout")

            def inverse(f, b, hf):
                for g in range(2):
                    f.need("lmat", 2 * hf + g + 1)
                    f.did(dve.tensor_tensor(w16[g][:], bank(XB[g]), four_of(const("merge")), ALU.mult), "w_sb")
                    f.did(dve.tensor_tensor(lmat[g][:], bank(XB[g]), four_of(const("maskL")), ALU.mult), "lmat_sb")
                for l in range(1, 6):
                    for g in range(2):
                        f.need("w", product(hf, l, g))
                        f.did(dve.tensor_tensor(w16[g][:], bank(XB[g]), four_of(const("merge", l)), ALU.mult), "w_sb")
                    if hf == 0 and l == 1 and b:
                        centre(b)
                    if hf == 0 and l < 5:
                        masked(f, 8 + 2 * (l - 1))
                        masked(f, 9 + 2 * (l - 1))
                    if hf == 0 and l == 4 and b:
                        inverse_std(b)
                    if hf == 1 and l == 3 and b:
                        finish(b)
                    if hf == 1 and l == 4:
                        f.need("bonus")
                        f.prev("ysum")
                        f.did(dve.tensor_tensor(bv[:], two(6), v_in[:], ALU.mult), "bv")
                for g in range(2):
                    f.need("e", 2 * hf + g + 1)
                    f.did(dve.tensor_copy(w16[g][:], bank(XB[g])), "e_sb")

            def step(f, b):
                if f:
                    f.need("in_sw")
                    f.prev("exps")
                    at = C_AT["restart"]
                    f.did(dve.tensor_tensor_scan(csum[:].rearrange("p j s -> p (j s)"), cst[:, at:at + 1024],
                                                 sw_in[:].rearrange("p j s -> p (j s)"), 0.0, ALU.mult, ALU.add),
                          "scan")
                    f.need("in_a")
                    f.prev("kt")
                    f.prev("rk")
                    f.did(dve.scalar_tensor_tensor(am[:], a_in[:], -1.0, bc("k_a"), ALU.add, ALU.mult), "am")
                    f.need("am")
                    f.need("in_k")
                    f.did(dve.scalar_tensor_tensor(am[:], am[:], 1.0, k_in[:], ALU.add, ALU.mult), "kp")
                    f.need("kroot")
                    f.prev("kspread")
                    f.did(dve.tensor_scalar(kinv[:], kinv[:], 1e-12, None, ALU.max), "kclamp")
                    f.need("kclamp")
                    f.did(dve.reciprocal(kinv[:], kinv[:]), "kinv")
                if b:
                    b.prev("y")
                    u_sum(b, 0)
                if f:
                    f.need("kspread")
                    f.did(dve.tensor_tensor(kkr[:], kkr[:], two(0), ALU.mult), "kk")
                if b:
                    m_next(b, 0)
                if f:
                    f.need("exps")
                    f.need("kp")
                    f.prev("lmat")
                    f.did(dve.tensor_tensor(kt[:], am[:], pinv[:], ALU.mult), "kt")
                if b:
                    u_sum(b, 1)
                if f:
                    f.need("b")
                    f.did(dve.tensor_tensor(bt[:], bt[:], pinv[:], ALU.mult), "bt")
                if b:
                    m_next(b, 1)
                if f:
                    f.need("kk")
                    f.need("in_r")
                    f.prev("y")
                    f.did(dve.scalar_tensor_tensor(ar[:, :, 0:128].rearrange(split, s=CHUNK),
                                                   kkr[:].rearrange(split, s=CHUNK), -1.0, pe1[:, :, :, 0:CHUNK],
                                                   ALU.mult, ALU.mult), "at")
                    f.did(dve.tensor_tensor(ar[:, :, 128:256].rearrange(split, s=CHUNK),
                                            r_in[:].rearrange(split, s=CHUNK), pe1[:, :, :, 1:CHUNK + 1],
                                            ALU.mult), "rt")
                    for n in range(8):
                        masked(f, n)
                    inverse(f, b, 0)
                elif b:
                    centre(b)
                    inverse_std(b)
                if b:
                    scale(b)
                if f:
                    inverse(f, b, 1)
                elif b:
                    finish(b)

            run(dve, step)

        @block.tensor
        def _(pe):
            pe.wait_ge(s_const, 16)
            pe.wait_ge(s_init, 5 + KT)

            def sums_by_head(src):
                for j in range(KT):
                    last = pe.matmul(PS[0:32, 6, 0:128], sel(j), src[:, j, :], start=j == 0, stop=j == KT - 1)
                return last

            def spread(src, at):
                for j in range(KT):
                    last = pe.matmul(two(at)[:, j, :], sel_t(j), src[:], start=True, stop=True)
                return last

            def head_sums(src, at):
                for i in range(2):
                    last = pe.matmul(PS[:, at + i, :], const("headsum"),
                                     src[:, 4 * i:4 * i + 4, :].rearrange("p j s -> p (j s)"), start=True, stop=True)
                return last

            def a_matrices(f, n):
                jj, g = n // 2, n % 2
                R = rows(g)
                if n >= 2:
                    f.need("amat_sb", n - 1)
                pe.matmul(PS[:, g, 0:256], bt[R, jj, :], ar[R, jj, :], start=True, stop=True)
                f.did(pe.matmul(PS[:, g, 256:512], kt[R, jj, :], ar[R, jj, :], start=True, stop=True), "amat")

            def a_ak_v(f, hf):
                for g in range(2):
                    for jj in range(4):
                        j = 4 * hf + jj
                        q = (4 * g + jj) * RW_N
                        last = pe.matmul(PS[:, 0, q:q + RW_N], amat[:, g, j, 256:384], v_tok[:, j, rows(g)],
                                         start=True, stop=True)
                f.did(last, "t1")

            def u_zero(f, hf):
                f.need("t1_sb", hf + 1)
                f.need("yt_sb", 2 * hf + 2)
                for g in range(2):
                    for jj in range(4):
                        q = (4 * g + jj) * RW_N
                        last = pe.matmul(PS[:, 1, q:q + RW_N], xt32[:, g, 4 * hf + jj, :], t1[:, g, 4 * hf + jj, :],
                                         start=True, stop=True)
                f.did(last, "u0")

            def w_tilde(f, hf):
                for g in range(2):
                    for jj in range(4):
                        j = 4 * hf + jj
                        last = pe.matmul(bank(0)[rows(g), jj, :], a_tok[:, j, rows(g)], xt32[:, g, j, :],
                                         start=True, stop=True)
                f.did(last, "wt")

            def u_state(b, ci):
                s = slice(CHUNK * ci, CHUNK * (ci + 1))
                b.settle()
                if ci == 0:
                    b.prev("m_copy")
                else:
                    b.need("m_sb", ci)
                for g in range(2):
                    for j in range(KT):
                        last = pe.matmul(PS[s, 6 + g, RW_N * j:RW_N * (j + 1)], wt[rows(g), j, s],
                                         mst[ci][rows(g), j, :], start=True, stop=True)
                b.did(last, "u")

            def m_state(b, ci):
                s = slice(CHUNK * ci, CHUNK * (ci + 1))
                b.settle()
                b.need("u_sb", ci + 1)
                for g in range(2):
                    for j in range(KT):
                        o = bank(2 + ci, RW_N)[rows(g), j, :]
                        pe.matmul(o, k_tok[s, j, rows(g)], v_tok[s, j, rows(g)], start=True, stop=False)
                        last = pe.matmul(o, b_tok[s, j, rows(g)], utok[s, g, j, :], start=False, stop=True)
                b.did(last, "m")

            def outputs(b):
                for g in range(2):
                    R = rows(g)
                    for j in range(KT):
                        o = two(4)[R, j, :]
                        pe.matmul(o, utok[:, g, j, :], amat[:, g, j, 128:256], start=True, stop=False)
                        pe.matmul(o, v_tok[:, j, R], amat[:, g, j, 384:512], start=False, stop=True)
                        for ci in range(NCH):
                            s = slice(CHUNK * ci, CHUNK * (ci + 1))
                            last = pe.matmul(o[:, s], mst[ci][R, j, :], ar[R, j, 128 + CHUNK * ci:192 + CHUNK * ci],
                                             start=False, stop=True, skip_group_check=True)
                b.did(last, "y")

            def mean(b):
                b.need("y_sb")
                b.did(head_sums(yraw, 6), "mean")

            def variance(b):
                b.need("ysq")
                b.did(sums_by_head(ysq), "var")

            def spread_inverse_std(b):
                b.need("yinv")
                b.did(spread(yinv, 6), "yspread")

            def bonus(f, b):
                f.need("rk")
                if b:
                    b.need("yn")
                for j in range(KT):
                    last = pe.matmul(two(6)[:, j, :], rkbd[:, j, :], rk[:, j, :], start=True, stop=True)
                f.did(last, "bonus")

            def inverse(f, b, hf):
                for g in range(2):
                    R = rows(g)
                    for jj in range(4):
                        last = pe.matmul(bank(XB[g])[:, jj, :], ar[R, 4 * hf + jj, 0:128], bt[R, 4 * hf + jj, :],
                                         start=True, stop=True)
                    f.did(last, "lmat")
                for l in range(6):
                    for g in range(2):
                        if l == 0:
                            continue
                        f.need("xy_sb", level(hf, l - 1, g))
                        if l == 1:
                            f.need("lt16", 2 * hf + g + 1)
                        for jj in range(4):
                            last = pe.matmul(bank(XB[g])[:, jj, :], lt16[g][:, jj, :], x16[g][:, jj, :],
                                             start=True, stop=True)
                        f.did(last, "w")
                    if hf == 0 and l == 0 and b:
                        mean(b)
                    if hf == 0 and 1 <= l < 5:
                        a_matrices(f, 8 + 2 * (l - 1))
                        a_matrices(f, 9 + 2 * (l - 1))
                    if hf == 0 and l == 3 and b:
                        variance(b)
                    if hf == 0 and l == 5 and b:
                        spread_inverse_std(b)
                    if hf == 1 and l == 0:
                        f.need("amat_sb")
                        a_ak_v(f, 0)
                    if hf == 1 and l == 1:
                        u_zero(f, 0)
                    if hf == 1 and l == 2:
                        w_tilde(f, 0)
                    if hf == 1 and l == 3:
                        bonus(f, b)
                    if hf == 1 and l == 4:
                        f.need("wt_sb", 1)
                        a_ak_v(f, 1)
                    for g in range(2):
                        f.need("w_sb", level(hf, l, g))
                        if l == 0:
                            f.need("lmat_sb", 2 * hf + g + 1)
                            if hf == 1:
                                f.need("yt_sb", g + 1)
                        for jj in range(4):
                            W = w16[g][:, jj, :]
                            X, Y = (x16[g][:, jj, :], y16[g][:, jj, :]) if l else (ident16[:], ident16[:])
                            pe.matmul(bank(XB[g])[:, jj, :], Y, W, start=True, stop=False)
                            pe.matmul(bank(XB[g])[:, jj, :], ident16[:], X, start=False, stop=True)
                            pe.matmul(bank(YB[g])[:, jj, :], W, Y, start=True, stop=False)
                            last = pe.matmul(bank(YB[g])[:, jj, :], ident16[:], Y, start=False, stop=True)
                        f.did(last, "xy")
                for g in range(2):
                    f.need("xy_sb", level(hf, 5, g))
                    f.need("l_lo", 2 * hf + g + 1)
                    for jj in range(4):
                        Y = y16[g][:, jj, :]
                        pe.matmul(bank(XB[g])[:, jj, :], l_hi[g][:, jj, :], Y, start=True, stop=False)
                        pe.matmul(bank(XB[g])[:, jj, :], l_lo[g][:, jj, :], Y, start=False, stop=False)
                        pe.matmul(bank(XB[g])[:, jj, :], negid16[:], Y, start=False, stop=False)
                        last = pe.matmul(bank(XB[g])[:, jj, :], ident16[:], ident16[:], start=False, stop=True)
                    f.did(last, "e")
                for g in range(2):
                    f.need("e_sb", 2 * hf + g + 1)
                    for jj in range(4):
                        pe.matmul(bank(YB[g])[:, jj, :], x16[g][:, jj, :], w16[g][:, jj, :], start=True, stop=False)
                        last = pe.matmul(bank(YB[g])[:, jj, :], ident16[:], y16[g][:, jj, :], start=False, stop=True)
                    f.did(last, "yt")

            def step(f, b):
                if f:
                    f.need("ksq")
                    f.prev("bv")
                    f.did(sums_by_head(tmp), "ksum")
                if b:
                    b.need("wt_sb")
                    b.need("u0_sb")
                    b.need("yt_sb")
                    b.need("bv")
                if f:
                    f.need("kroot")
                for ci in range(NCH):
                    if b:
                        u_state(b, ci)
                    if f and ci == 0:
                        f.need("kinv")
                        f.did(spread(kinv, 0), "kspread")
                    if b:
                        m_state(b, ci)
                if b:
                    outputs(b)
                if f:
                    f.need("kk")
                    for i, (src, made) in enumerate((s, m) for s, m in ((v_in, "in_v"), (bt, "bt"), (kt, "kt"),
                                                                        (ar, "at")) for _ in range(2)):
                        f.need(made)
                        if i >= 4:
                            f.need("tok", i - 3)
                        for jj in range(4):
                            last = pe.transpose(bank(TRB[i % 4])[:, jj, :], src[:, 4 * (i % 2) + jj, 0:128],
                                                const("ident"))
                        f.did(last, "trans")
                    f.need("rt")
                    f.need("tok")
                    for n in range(8):
                        a_matrices(f, n)
                    f.prev("m_add")
                    f.prev("y_sb")
                    inverse(f, b, 0)
                elif b:
                    mean(b)
                    variance(b)
                    spread_inverse_std(b)
                if f:
                    inverse(f, b, 1)
                    u_zero(f, 1)
                    w_tilde(f, 1)

            run(pe, step)



def output_projection(nc, name, src, y, w_out, residual, dst):
    per = dict(w0=16, w1=16, res0=32, res1=32, out0=32, out1=32, mm=4, sum=4)
    with ExitStack() as c:
        sems = Semaphores(nc, c)
        def sb(n, shape, dt=F32):
            return c.enter_context(nc.sbuf_tensor(f"{name}_{n}", shape, dt))

        S = {n: sems.new(f"{name}_{n}") for n in per}
        s_y = sems.new(f"{name}_y")
        w = [sb(f"w{i}", [128, KT, 128]) for i in range(2)]
        res = [sb(f"res{i}", [128, HALF]) for i in range(2)]
        out = [sb(f"out{i}", [128, HALF]) for i in range(2)]
        ps = [c.enter_context(nc.psum_tensor(f"{name}_ps{i}", [128, HALF], F32)) for i in range(2)]
        block = c.enter_context(nc.Block())
        w_cols = w_out.rearrange("(k p) n -> p k n", p=128)
        res_v = residual.rearrange("(j p) t -> j p t", p=128)
        dst_v = dst.rearrange("(j p) t -> j p t", p=128)

        def part(dram, c2, i, hv):
            return dram[ds(c2 * 2 + i, 1), :, HALF * hv:HALF * hv + HALF].rearrange("j p t -> p (j t)")

        @block.sync
        def _(sp):
            for n in per:
                sp.sem_inc(S[n], per[n])
            if src is not None:
                for k in range(KT):
                    sp.dma_start(y[:, k, :], src[128 * k:128 * k + 128, :]).then_inc(s_y, 16)
            with sp.Fori(0, KT // 2) as c2:
                at = Place(sp, S, per, c2)
                for i in range(2):
                    at.prev("mm", 2 * i + 2)
                    at.did(sp.dma_start(w[i][:], w_cols[:, :, ds(c2 * 256 + 128 * i, 128)]), f"w{i}", 16)
                    for hv in range(2):
                        if i:
                            at.need("sum", hv + 1)
                        else:
                            at.prev("sum", 3 + hv)
                        at.did(sp.dma_start(res[hv][:], part(res_v, c2, i, hv)), f"res{hv}", 16)
                at.end()

        @block.scalar
        def _(act):
            with act.Fori(0, KT // 2) as c2:
                at = Place(act, S, per, c2)
                for i in range(2):
                    for hv in range(2):
                        at.need("sum", 2 * i + hv + 1)
                        at.did(act.dma_start(part(dst_v, c2, i, hv), out[hv][:]), f"out{hv}", 16)
                at.end()
            for hv in range(2):
                act.wait_ge(S[f"out{hv}"], 32 * (KT // 2 + 1))

        @block.tensor
        def _(pe):
            if src is not None:
                pe.wait_ge(s_y, 16 * KT)
            with pe.Fori(0, KT // 2) as c2:
                at = Place(pe, S, per, c2)
                for i in range(2):
                    at.need(f"w{i}")
                    for hv in range(2):
                        if i:
                            at.need("sum", hv + 1)
                        else:
                            at.prev("sum", 3 + hv)
                        for k in range(KT):
                            for b in range(HB):
                                t0 = HALF * hv + 512 * b
                                last = pe.matmul(ps[hv][:, 512 * b:512 * b + 512], w[i][:, k, :], y[:, k, t0:t0 + 512],
                                                 start=k == 0, stop=k == KT - 1)
                        at.did(last, "mm")
                at.end()

        @block.vector
        def _(dve):
            with dve.Fori(0, KT // 2) as c2:
                at = Place(dve, S, per, c2)
                for i in range(2):
                    for hv in range(2):
                        at.need("mm", 2 * i + hv + 1)
                        at.need(f"res{hv}", 16 * (i + 1))
                        if i:
                            at.need(f"out{hv}", 16)
                        else:
                            at.prev(f"out{hv}", 32)
                        at.did(dve.tensor_tensor(out[hv][:], ps[hv][:], res[hv][:], ALU.add), "sum")
                at.end()



CW = D // 2
CB = CW // 128
HEADS = 8
DH = 64


def conv_branch(nc, h2, w_in, cvec, y2):
    order = (2, 0, 1, 3)
    per = dict(w0=32, w1=32, mm=8, gc=2, zu=2, tap0=1, tap1=1, tap2=1, gb=2, sig=2, sil=2, yc=1, out=16)
    with ExitStack() as c:
        sems = Semaphores(nc, c)
        def sb(n, shape, dt=F32):
            return c.enter_context(nc.sbuf_tensor(f"cv_{n}", shape, dt))

        S = {n: sems.new(f"cv_{n}") for n in (*per, "passed")}
        s_zero = sems.new("cv_zero")
        w = [sb(f"w{i}", [128, KT, 128]) for i in range(2)]
        gc, conv = sb("gc", [128, T]), sb("conv", [128, T])
        sig = gc
        zu = sb("zu", [128, T + 2])
        vec = sb("vec", [128, 4, CB])
        ps = [c.enter_context(nc.psum_tensor(f"cv_ps{i}", [128, HALF], F32)) for i in range(4)]
        block = c.enter_context(nc.Block())
        w_cols = w_in.rearrange("(k p) n -> p k n", p=128)

        def half(hv, shift=0):
            return slice(HALF * hv + shift, HALF * hv + HALF + shift)

        READ = {0: ("gc", 0), 1: ("zu", 0), 2: ("gb", 0), 3: ("sil", 0)}

        @block.sync
        def _(sp):
            for n in per:
                sp.sem_inc(S[n], per[n])
            with sp.Fori(0, CB) as g:
                at = Place(sp, S, per, g)
                for m in range(4):
                    at.settle()
                    if m < 2:
                        at.prev("mm", 2 * m + 6)
                    else:
                        at.need("mm", 2 * m - 2)
                    at.did(sp.dma_start(w[m % 2][:], w_cols[:, :, ds(g * 128 + order[m] * CW, 128)]), f"w{m % 2}", 16)
                at.end()

        @block.tensor
        def _(pe):
            with pe.Fori(0, CB) as g:
                at = Place(pe, S, per, g)
                for m in range(4):
                    at.need(f"w{m % 2}", 16 * (m // 2 + 1))
                    for hv in range(2):
                        if m < 2:
                            at.prev(READ[m + 2][0], hv + 1)
                        else:
                            at.need(READ[m - 2][0], hv + 1)
                        for k in range(KT):
                            for b in range(HB):
                                t0 = HALF * hv + 512 * b
                                last = pe.matmul(ps[2 * (m % 2) + hv][:, 512 * b:512 * b + 512], w[m % 2][:, k, :],
                                                 h2[:, k, t0:t0 + 512], start=k == 0, stop=k == KT - 1)
                        at.did(last, "mm")
                at.end()

        @block.scalar
        def _(act):
            act.dma_start(vec[:], cvec).then_inc(s_zero, 16)
            with act.Fori(0, CB) as g:
                at = Place(act, S, per, g)
                at.prev("yc")
                for hv in range(2):
                    at.need("mm", hv + 1)
                    at.did(act.copy(gc[:, half(hv)], ps[hv][:]), "gc")
                at.need("zu")
                for hv in range(2):
                    at.need("mm", 7 + hv)
                    at.did(act.activation(sig[:, half(hv)], ps[2 + hv][:], ACT.Sigmoid), "sig")
                at.need("yc")
                at.did(act.dma_start(y2[ds(g * 128, 128), :], conv[:]), "out", 16)
                at.end()
            act.wait_ge(S["out"], 16 * (CB + 1))

        @block.gpsimd
        def _(pool):
            pool.memset(zu[:, 0:1], 0.0).then_inc(s_zero, 1)
            pool.memset(zu[:, T + 1:T + 2], 0.0).then_inc(s_zero, 1)

        @block.vector
        def _(dve):
            dve.wait_ge(s_zero, 18)
            with dve.Fori(0, CB) as g:
                at = Place(dve, S, per, g)

                def tap(i):
                    return vec[:, i, ds(g, 1)]

                for hv in range(2):
                    at.need("mm", 3 + hv)
                    at.need("gc", hv + 1)
                    at.did(dve.tensor_tensor(zu[:, half(hv, 1)], ps[2 + hv][:], gc[:, half(hv)], ALU.mult), "zu")
                at.need("zu")
                at.prev("out")
                at.did(dve.tensor_scalar(conv[:], zu[:, 0:T], tap(0), tap(3), ALU.mult, ALU.add), "tap0")
                at.need("tap0")
                at.did(dve.scalar_tensor_tensor(conv[:], zu[:, 1:T + 1], tap(1), conv[:], ALU.mult, ALU.add), "tap1")
                at.need("tap1")
                at.did(dve.scalar_tensor_tensor(conv[:], zu[:, 2:T + 2], tap(2), conv[:], ALU.mult, ALU.add), "tap2")
                at.need("tap2")
                for hv in range(2):
                    at.need("mm", 5 + hv)
                    at.did(dve.tensor_tensor(conv[:, half(hv)], ps[hv][:], conv[:, half(hv)], ALU.mult), "gb")
                for hv in range(2):
                    at.need("sig", hv + 1)
                    at.did(dve.tensor_tensor(sig[:, half(hv)], ps[2 + hv][:], sig[:, half(hv)], ALU.mult), "sil")
                at.need("sil")
                at.need("gb")
                at.did(dve.tensor_tensor(conv[:], conv[:], sig[:], ALU.mult), "yc")
                at.end()


def attention_projections(nc, h2, w_in, qkv, gains, headsum, z_gate):
    per = dict(w0=16, w1=16, mm=4, sq=4, raw=4, ms=4, var=4, root=4, inv=4, norm=4)
    zper = dict(sig=4, out0=32, out1=32)
    with ExitStack() as c:
        sems = Semaphores(nc, c)
        def sb(n, shape, dt=F32):
            return c.enter_context(nc.sbuf_tensor(f"at_{n}", shape, dt))

        S = {n: sems.new(f"at_{n}") for n in (*per, *zper)}
        s_gain = sems.new("at_gain")
        w = [sb(f"w{i}", [128, KT, 128]) for i in range(2)]
        sq, root = ([sb(f"{n}{i}", [128, HALF]) for i in range(2)] for n in ("sq", "root"))
        gain = sb("gain", [128, 2])
        ps = [c.enter_context(nc.psum_tensor(f"at_ps{i}", [128, HALF], F32)) for i in range(2)]
        ms = [c.enter_context(nc.psum_tensor(f"at_ms{i}", [128, HALF], F32)) for i in range(2)]
        block = c.enter_context(nc.Block())
        w_cols = w_in.rearrange("(k p) n -> p k n", p=128)
        z_rows = z_gate.rearrange("(j p) t -> j p t", p=128)
        PAIRS = CB // 2

        def half(hv):
            return slice(HALF * hv, HALF * hv + HALF)

        def n_of(i, hv):
            return 2 * i + hv + 1

        def dest(kind, c2, i, hv):
            return qkv[kind][:, ds(c2 * 2 + i, 1), half(hv)].rearrange("p j t -> p (j t)")

        def pairs(eng):
            for kind in range(4):
                with eng.Fori(0, PAIRS) as c2:
                    at = Place(eng, S, per, c2 + kind * PAIRS)
                    yield kind, c2, at

        @block.sync
        def _(sp):
            for n in per:
                sp.sem_inc(S[n], per[n])
            for n in zper:
                sp.sem_inc(S[n], zper[n])
            for kind, c2, at in pairs(sp):
                for i in range(2):
                    at.prev("mm", n_of(i, 1))
                    at.did(sp.dma_start(w[i][:], w_cols[:, :, ds(c2 * 256 + ((4 + kind) * CW + 128 * i), 128)]),
                           f"w{i}", 16)
                if kind == 3:
                    zat = Place(sp, S, zper, c2)
                    for i in range(2):
                        for hv in range(2):
                            at.need("raw", n_of(i, hv))
                            zat.did(sp.dma_start(z_rows[ds(c2 * 2 + i, 1), :, half(hv)]
                                                 .rearrange("j p t -> p (j t)"), root[hv][:]), f"out{hv}", 16)
            for hv in range(2):
                sp.wait_ge(S[f"out{hv}"], 32 * (PAIRS + 1))

        @block.tensor
        def _(pe):
            for kind, c2, at in pairs(pe):
                for i in range(2):
                    at.need(f"w{i}")
                    for hv in range(2):
                        last_read = at.need if i else at.prev
                        last_read("raw", 2 * (1 - i) + hv + 1)
                        for kt in range(KT):
                            for b in range(HB):
                                t0 = HALF * hv + 512 * b
                                last = pe.matmul(ps[hv][:, 512 * b:512 * b + 512], w[i][:, kt, :],
                                                 h2[:, kt, t0:t0 + 512], start=kt == 0, stop=kt == KT - 1)
                        at.did(last, "mm")
                    if kind < 2:
                        for hv in range(2):
                            at.need("sq", n_of(i, hv))
                            (at.need if i else at.prev)("var", 2 * (1 - i) + hv + 1)
                            for b in range(HB):
                                last = pe.matmul(ms[hv][:, 512 * b:512 * b + 512], headsum,
                                                 sq[hv][:, 512 * b:512 * b + 512], start=True, stop=True)
                            at.did(last, "ms")

        @block.scalar
        def _(act):
            act.dma_start(gain[:], gains).then_inc(s_gain, 16)
            for kind, c2, at in pairs(act):
                zat = Place(act, S, zper, c2)
                for i in range(2):
                    for hv in range(2):
                        at.need("mm", n_of(i, hv))
                        if kind < 2:
                            (at.need if i else at.prev)("ms", 2 * (1 - i) + hv + 1)
                            at.did(act.activation(sq[hv][:], ps[hv][:], ACT.Square), "sq")
                        if kind < 3:
                            at.did(act.copy(dest(kind, c2, i, hv), ps[hv][:]), "raw")
                        else:
                            (at.need if i else at.prev)("raw", 2 * (1 - i) + hv + 1)
                            zat.did(act.activation(sq[hv][:], ps[hv][:], ACT.Sigmoid), "sig")
                    if kind < 2:
                        for hv in range(2):
                            at.need("var", n_of(i, hv))
                            at.did(act.activation(root[hv][:], root[hv][:], ACT.Sqrt), "root")

        @block.vector
        def _(dve):
            dve.wait_ge(s_gain, 16)
            dve.tensor_scalar(gain[:, 0:1], gain[:, 0:1], DH ** -0.5, None, ALU.mult).then_inc(s_gain, 1)
            dve.wait_ge(s_gain, 17)
            for kind, c2, at in pairs(dve):
                zat = Place(dve, S, zper, c2)
                for i in range(2):
                    for hv in range(2):
                        n = n_of(i, hv)
                        if kind < 2:
                            at.need("ms", n)
                            (at.need if i else at.prev)("norm", 2 * (1 - i) + hv + 1)
                            at.did(dve.tensor_scalar(root[hv][:], ms[hv][:], 1.0 / DH, EPS, ALU.mult, ALU.add), "var")
                        if kind == 3:
                            dve.wait_ge(S["norm"], 4 * (2 * PAIRS + 1))
                            at.need("mm", n)
                            zat.need("sig", n)
                            if i:
                                zat.need(f"out{hv}", 16)
                            else:
                                zat.prev(f"out{hv}", 32)
                            at.did(dve.tensor_tensor(root[hv][:], ps[hv][:], sq[hv][:], ALU.mult), "raw")
                    if kind < 2:
                        for hv in range(2):
                            n = n_of(i, hv)
                            at.need("root", n)
                            at.did(dve.reciprocal(root[hv][:], root[hv][:]), "inv")
                            at.need("inv", n)
                            at.need("raw", n)
                            d = dest(kind, c2, i, hv)
                            at.did(dve.scalar_tensor_tensor(d, d, gain[:, kind:kind + 1], root[hv][:],
                                                            ALU.mult, ALU.mult), "norm")
            dve.wait_ge(S["norm"], 4 * (2 * PAIRS + 1))



DILATIONS = (1, 4, 16)
WINDOW_HALF = 64
QB = 128
BUCKETS = 32
MAX_DISTANCE = 1024
NEG = -1e30
SKEW = 383
OROW = HEADS * (DH + 2)


def bucket_constants():
    half_b = BUCKETS // 2
    exact = half_b // 2
    out = np.zeros((BUCKETS + 1, len(DILATIONS), SKEW), np.float32)
    for g, dil in enumerate(DILATIONS):
        for x in range(SKEW):
            rel = x - (SKEW // 2)
            if abs(rel) > WINDOW_HALF:
                out[BUCKETS, g, x] = 1.0
                continue
            n = abs(rel) * dil
            far = exact + int(np.float32(np.log(np.float32(max(n, 1)) / np.float32(exact)))
                              / np.float32(math.log(MAX_DISTANCE / exact)) * np.float32(half_b - exact))
            out[(half_b if rel > 0 else 0) + (n if n < exact else min(far, half_b - 1)), g, x] = 1.0
    return out


def bias_tables(nc, rel_bias, onehot, skew, table):
    NG = len(DILATIONS)
    with ExitStack() as c:
        sems = Semaphores(nc, c)
        rb = c.enter_context(nc.sbuf_tensor("bt_rb", [BUCKETS + 1, HEADS], F32))
        rb_q = c.enter_context(nc.sbuf_tensor("bt_rb_q", [BUCKETS + 1, HEADS, 128], F32))
        hot = c.enter_context(nc.sbuf_tensor("bt_hot", [BUCKETS + 1, NG, SKEW], F32))
        flat = c.enter_context(nc.sbuf_tensor("bt_flat", [128, NG * HEADS, SKEW], F32))
        ps = [c.enter_context(nc.psum_tensor(f"bt_ps{i}", [128, 512], F32)) for i in range(2)]
        s_set, s_in, s_spread, s_mm, s_flat, s_skew, s_table = (
            sems.new(f"bt_{n}") for n in ("set", "in", "spread", "mm", "flat", "skew", "table"))
        block = c.enter_context(nc.Block())

        @block.gpsimd
        def _(pool):
            pool.memset(rb[:], NEG).then_inc(s_set, 1)
            pool.wait_ge(s_in, 32)
            pool.tensor_copy(rb_q[:], rb[:].unsqueeze(2).to_broadcast([BUCKETS + 1, HEADS, 128])).then_inc(s_spread, 1)

        @block.sync
        def _(sp):
            sp.dma_start(hot[:], onehot).then_inc(s_in, 16)
            sp.wait_ge(s_set, 1)
            sp.dma_start(rb[0:BUCKETS, :], rel_bias).then_inc(s_in, 16)
            for n in range(NG * HEADS):
                sp.wait_ge(s_flat, n + 1)
                sp.dma_start(skew[n].rearrange("(p x) -> p x", x=SKEW), flat[:, n, :]).then_inc(s_skew, 16)
            sp.wait_ge(s_skew, 16 * NG * HEADS)
            for n in range(NG * HEADS):
                diag = skew[n, QB - 1:QB - 1 + 128 * (SKEW - 1)].rearrange("(p x) -> p x", x=SKEW - 1)[:, 0:256]
                sp.dma_start(table[:, n // HEADS, n % HEADS, :], diag).then_inc(s_table, 16)
            sp.wait_ge(s_table, 16 * NG * HEADS)

        @block.tensor
        def _(pe):
            pe.wait_ge(s_spread, 1)
            for n in range(NG * HEADS):
                if n >= 2:
                    pe.wait_ge(s_flat, n - 1)
                pe.matmul(ps[n % 2][:, 0:SKEW], rb_q[:, n % HEADS, :], hot[:, n // HEADS, :],
                          start=True, stop=True).then_inc(s_mm, 1)

        @block.scalar
        def _(act):
            for n in range(NG * HEADS):
                act.wait_ge(s_mm, n + 1)
                act.copy(flat[:, n, :], ps[n % 2][:, 0:SKEW]).then_inc(s_flat, 1)


AT_PER = dict(stage=1, vtr=1, v_sb=1, s=4, s_red=4, neg=4, exps=4, ptr=4, p_sb=4, o=1, o_sb=1, out=16)


def window_attention(nc, qkv, table, ident, partial):
    with ExitStack() as c:
        sems = Semaphores(nc, c)
        def sb(n, shape, dt=F32):
            return c.enter_context(nc.sbuf_tensor(f"wa_{n}", shape, dt))

        S = {n: sems.new(f"wa_{n}") for n in (*AT_PER, "passed")}
        qs = [sb(f"qs{i}", [128, 4, QB]) for i in range(2)]
        ks, vs = ([sb(f"{n}{i}", [128, 4, 256]) for i in range(2)] for n in ("ks", "vs"))
        v_tok = [sb(f"v_tok{i}", [128, 2, CW]) for i in range(2)]
        sc = [sb(f"sc{i}", [128, 2, 256]) for i in range(2)]
        p = [sb(f"p{i}", [128, 2, 256]) for i in range(2)]
        pt = [sb(f"pt{i}", [128, 2, 2, 128]) for i in range(2)]
        neg = [sb(f"neg{i}", [128, HEADS]) for i in range(2)]
        ob = [sb(f"ob{i}", [128, HEADS, DH + 2]) for i in range(2)]
        V_PS = [c.enter_context(nc.psum_tensor(f"wa_vps{i}", [128, 4, 128], F32)) for i in range(2)]
        S_PS = [c.enter_context(nc.psum_tensor(f"wa_sps{i}", [128, 2, 256], F32)) for i in range(2)]
        P_PS = [c.enter_context(nc.psum_tensor(f"wa_pps{i}", [128, 2, 2, 128], F32)) for i in range(2)]
        O_PS = [c.enter_context(nc.psum_tensor(f"wa_ops{i}", [128, HEADS, DH], F32)) for i in range(2)]
        block = c.enter_context(nc.Block())
        AHEAD = 2

        def steps(eng):
            def step(t, par, g, w, col, q0, k0):
                return Place(eng, S, AT_PER, t, AHEAD), par, g, w, col, q0, k0

            yield step(0, 0, 0, 192, 64, 0, 0)
            with eng.Fori(0, 7) as i:
                for par in range(2):
                    q0 = i * 256 + (128 + 128 * par)
                    yield step(i * 2 + (1 + par), 1 - par, 0, 256, 0, q0, i * 256 + (64 + 128 * par))
            yield step(15, 1, 0, 192, 0, T - QB, T - 192)
            with eng.Fori(0, 4) as r:
                for n in range(4):
                    w, col, k0 = ((192, 64, 0), (256, 0, 64), (256, 0, 192), (192, 0, 320))[n]
                    yield step(r * 4 + (16 + n), n % 2, 1, w, col, r + 4 * QB * n, r + 4 * k0)
            with eng.Fori(0, 8) as i:
                for par in range(2):
                    yield step(i * 2 + (32 + par), par, 2, 128, 64, i * 2 + par, i * 2 + par)

        def chunks(w):
            return [(k, min(128, w - 128 * k)) for k in range(-(-w // 128))]

        def group(gi):
            return [(2 * (gi // 2) + jj, gi % 2) for jj in range(2)]

        @block.gpsimd
        def _(pool):
            for at, par, g, w, col, q0, k0 in steps(pool):
                at.settle()
                at.prev("s", 4)
                at.prev("vtr")
                pool.tensor_copy(qs[par][:], qkv[0][:, :, ds(q0, QB, step=DILATIONS[g])])
                pool.tensor_copy(ks[par][:, :, 0:w], qkv[1][:, :, ds(k0, w, step=DILATIONS[g])])
                at.did(pool.tensor_copy(vs[par][:, :, 0:w], qkv[2][:, :, ds(k0, w, step=DILATIONS[g])]), "stage")

        @block.tensor
        def _(pe):
            for at, par, g, w, col, q0, k0 in steps(pe):
                at.need("stage")
                at.prev1("v_sb")
                for k, n in chunks(w):
                    for j in range(4):
                        last = pe.transpose(V_PS[k][0:n, j, :], vs[par][:, j, 128 * k:128 * k + n], ident)
                at.did(last, "vtr")

                def scores(gi):
                    at.need("s_red", gi - 1) if gi >= 2 else at.prev1("s_red", gi + 3)
                    for jj, (j, m) in enumerate(group(gi)):
                        R = slice(DH * m, DH * m + DH)
                        last = pe.matmul(S_PS[gi % 2][:, jj, 0:w], qs[par][R, j, :], ks[par][R, j, 0:w],
                                         start=True, stop=True)
                    at.did(last, "s")

                def values(gi):
                    at.need("exps", gi + 1)
                    at.need("p_sb", gi - 1) if gi >= 2 else at.prev1("p_sb", gi + 3)
                    for jj in range(2):
                        for k, n in chunks(w):
                            last = pe.transpose(P_PS[gi % 2][0:n, jj, k, :], p[gi % 2][:, jj, 128 * k:128 * k + n],
                                                ident)
                    at.did(last, "ptr")

                def outputs(gi):
                    at.need("p_sb", gi + 1)
                    if gi == 0:
                        at.need("v_sb")
                        at.prev("o_sb")
                    for jj, (j, m) in enumerate(group(gi)):
                        for k, n in chunks(w):
                            h = 2 * j + m
                            last = pe.matmul(O_PS[par][:, h, :], pt[gi % 2][0:n, jj, k, :],
                                             v_tok[par][0:n, k, DH * h:DH * h + DH],
                                             start=k == 0, stop=k == len(chunks(w)) - 1)
                    return last

                scores(0)
                scores(1)
                for gi in range(4):
                    values(gi)
                    if gi + 2 < 4:
                        scores(gi + 2)
                    last = outputs(gi)
                at.did(last, "o")

        @block.vector
        def _(dve):
            for at, par, g, w, col, q0, k0 in steps(dve):
                def reduce(gi):
                    at.settle()
                    at.need("s", gi + 1)
                    at.need("exps", gi - 1) if gi >= 2 else at.prev1("exps", gi + 3)
                    if gi == 0:
                        at.prev("out")
                    for jj, (j, m) in enumerate(group(gi)):
                        h = 2 * j + m
                        last = dve.tensor_tensor_reduce(sc[gi % 2][:, jj, 0:w], S_PS[gi % 2][:, jj, 0:w],
                                                        table[:, g, h, col:col + w], 1.0, -3e38, ALU.add, ALU.max,
                                                        ob[par][:, h, DH:DH + 1])
                    at.did(last, "s_red")
                    at.need("s_red", gi + 1)
                    h = 2 * group(gi)[0][0] + gi % 2
                    at.did(dve.tensor_scalar(neg[par][:, h:h + 3:2], ob[par][:, h:h + 3:2, DH], -1.0, None,
                                             ALU.mult), "neg")

                def weights(gi):
                    at.need("ptr", gi + 1)
                    for k, n in chunks(w):
                        last = dve.tensor_copy(pt[gi % 2][0:n, :, k, :], P_PS[gi % 2][0:n, :, k, :])
                    at.did(last, "p_sb")

                reduce(0)
                reduce(1)
                weights(0)
                reduce(2)
                weights(1)
                reduce(3)
                weights(2)
                weights(3)

        @block.scalar
        def _(act):
            for at, par, g, w, col, q0, k0 in steps(act):
                at.need("vtr")
                for k, n in chunks(w):
                    last = act.copy(v_tok[par][0:n, k, :], V_PS[k][0:n].rearrange("p j c -> p (j c)"))
                at.did(last, "v_sb")
                for gi in range(4):
                    at.need("neg", gi + 1)
                    at.need("ptr", gi - 1) if gi >= 2 else at.prev1("ptr", gi + 3)
                    for jj, (j, m) in enumerate(group(gi)):
                        h = 2 * j + m
                        last = act.activation(p[gi % 2][:, jj, 0:w], sc[gi % 2][:, jj, 0:w], ACT.Exp,
                                              bias=neg[par][:, h:h + 1], accum_out=ob[par][:, h, DH + 1:DH + 2])
                    at.did(last, "exps")
                at.need("o")
                at.did(act.copy(ob[par][:, :, 0:DH], O_PS[par][:]), "o_sb")

        @block.sync
        def _(sp):
            for n in AT_PER:
                sp.sem_inc(S[n], AHEAD * AT_PER[n])
            for at, par, g, w, col, q0, k0 in steps(sp):
                at.need("o_sb")
                at.prev1("out")
                at.did(sp.dma_start(partial[g, ds(q0, QB, step=DILATIONS[g]), :],
                                    ob[par][:].rearrange("p h e -> p (h e)")), "out", 16)
            sp.wait_ge(S["out"], 16 * (48 + AHEAD))


MG_PER = dict(top=1, top2=1, low=1, e=1, ed=1, s1=1, s2=1, inv=1, wg=1, prod=1, o1=1, o2=1, tr=1, gated=1)


def merge_attention(nc, partial, z_gate, y2_dram, y2, ident):
    NG = len(DILATIONS)
    with ExitStack() as c:
        sems = Semaphores(nc, c)
        def sb(n, shape, dt=F32):
            return c.enter_context(nc.sbuf_tensor(f"mg_{n}", shape, dt))

        S = {n: sems.new(f"mg_{n}") for n in (*MG_PER, "passed")}
        in_per = dict(in0=16, in1=16, z0=16, z1=16)
        SI = {n: sems.new(f"mg_{n}") for n in in_per}
        SI["passed"] = S["passed"]
        s_y = sems.new("mg_y")
        part = [sb(f"part{i}", [128, NG, HEADS, DH + 2]) for i in range(2)]
        z = [sb(f"z{i}", [128, CB, 128]) for i in range(2)]
        prod = [sb(f"prod{i}", [128, NG, HEADS, DH]) for i in range(2)]
        top, tot, inv = sb("top", [128, HEADS]), sb("tot", [128, HEADS]), sb("inv", [128, HEADS])
        e, ed = sb("e", [128, NG, HEADS]), sb("ed", [128, NG, HEADS])
        ps = [c.enter_context(nc.psum_tensor(f"mg_ps{i}", [128, CB, 128], F32)) for i in range(2)]
        block = c.enter_context(nc.Block())
        z_view = z_gate.rearrange("(j p) t -> p j t", p=128)
        AHEAD = 2

        def tiles(eng):
            with eng.Fori(0, T // 256) as i:
                for par in range(2):
                    yield Place(eng, S, MG_PER, i * 2 + par, AHEAD), Place(eng, SI, in_per, i), par, i * 256 + 128 * par

        def spread(a, g=NG):
            return a.unsqueeze(1).to_broadcast([128, g, HEADS])

        @block.sync
        def _(sp):
            for n in MG_PER:
                sp.sem_inc(S[n], AHEAD * MG_PER[n])
            for n in in_per:
                sp.sem_inc(SI[n], in_per[n])
            for at, pin, par, t0 in tiles(sp):
                at.prev("prod")
                at.prev("ed")
                pin.did(sp.dma_start(part[par][:].rearrange("p g h e -> p g (h e)"),
                                     partial[:, ds(t0, 128), :].rearrange("g p e -> p g e")), f"in{par}", 16)
                at.settle()
                at.prev("gated")
                pin.did(sp.dma_start(z[par][:], z_view[:, :, ds(t0, 128)]), f"z{par}", 16)

        @block.scalar
        def _(act):
            act.dma_start(y2[:, 0:CB, :], y2_dram.rearrange("(k p) t -> p k t", p=128)).then_inc(s_y, 16)
            for at, pin, par, t0 in tiles(act):
                at.need("low")
                at.prev1("wg")
                at.did(act.activation(e[:], ed[:], ACT.Exp), "e")
            act.wait_ge(s_y, 16)

        @block.vector
        def _(dve):
            for at, pin, par, t0 in tiles(dve):
                m, d = part[par][:, :, :, DH], part[par][:, :, :, DH + 1]
                pin.need(f"in{par}")
                at.did(dve.tensor_tensor(top[:], m[:, 0, :], m[:, 1, :], ALU.max), "top")
                at.need("top")
                at.did(dve.tensor_tensor(top[:], top[:], m[:, 2, :], ALU.max), "top2")
                at.need("top2")
                at.did(dve.tensor_tensor(ed[:], m, spread(top[:]), ALU.subtract), "low")
                at.need("e")
                at.did(dve.tensor_tensor(ed[:], e[:], d, ALU.mult), "ed")
                at.need("ed")
                at.did(dve.tensor_tensor(tot[:], ed[:, 0, :], ed[:, 1, :], ALU.add), "s1")
                at.need("s1")
                at.did(dve.tensor_tensor(tot[:], tot[:], ed[:, 2, :], ALU.add), "s2")
                at.need("s2")
                at.did(dve.reciprocal(inv[:], tot[:]), "inv")
                at.need("inv")
                at.did(dve.tensor_tensor(e[:], e[:], spread(inv[:]), ALU.mult), "wg")
                at.need("wg")
                at.prev("tr")
                at.did(dve.tensor_tensor(prod[par][:], part[par][:, :, :, 0:DH],
                                         e[:].unsqueeze(3).to_broadcast([128, NG, HEADS, DH]), ALU.mult), "prod")
                at.need("tr")
                pin.need(f"z{par}")
                at.did(dve.tensor_tensor(y2[:, CB:2 * CB, ds(t0, 128)], ps[par][:], z[par][:], ALU.mult), "gated")

        @block.gpsimd
        def _(pool):
            for at, pin, par, t0 in tiles(pool):
                at.need("prod")
                at.did(pool.tensor_tensor(prod[par][:, 0], prod[par][:, 0], prod[par][:, 1], ALU.add), "o1")
                at.need("o1")
                at.did(pool.tensor_tensor(prod[par][:, 0], prod[par][:, 0], prod[par][:, 2], ALU.add), "o2")

        @block.tensor
        def _(pe):
            for at, pin, par, t0 in tiles(pe):
                at.need("o2")
                at.prev("gated")
                for j in range(CB):
                    last = pe.transpose(ps[par][:, j, :], prod[par][:, 0, 2 * j:2 * j + 2, :]
                                        .rearrange("p h d -> p (h d)"), ident)
                at.did(last, "tr")


def build(nc, xT, vecs, consts, w_in, w_up, a_up, w_out, w_in2, cvec, gains, rel_bias, onehot, w_out2, outT,
          dbg=None):
    NG = len(DILATIONS)

    def dram(n, shape):
        if dbg and n in dbg:
            return dbg[n]
        return nc.dram_tensor(n, shape, F32, kind="Internal").ap()

    proj, yT, x2T = dram("proj", (6, D, T)), dram("yT", (D, T)), dram("x2T", (D, T))
    y_conv, z_gate = dram("y_conv", (CW, T)), dram("z_gate", (CW, T))
    skew, partial = dram("skew", (NG * HEADS, 128 * SKEW)), dram("partial", (NG, T, OROW))
    with ExitStack() as c:
        sems = Semaphores(nc, c)
        vec = c.enter_context(nc.sbuf_tensor("vec", [128, NVEC], F32))
        basic = c.enter_context(nc.sbuf_tensor("basic", [128, 256], F32))
        ones = c.enter_context(nc.sbuf_tensor("ones", [128, 128], F32))
        s_const = sems.new("s_const")
        with nc.Block() as block:
            @block.sync
            def _(sp):
                sp.dma_start(vec[:], vecs).then_inc(s_const, 16)
                sp.dma_start(basic[:], consts[:, 0:256]).then_inc(s_const, 16)
                sp.wait_ge(s_const, 33)

            @block.gpsimd
            def _(pool):
                pool.memset(ones[:], 1.0).then_inc(s_const, 1)
        ident, headsum = basic[:, 0:128], basic[:, 128:256]
        with ExitStack() as c1:
            h = c1.enter_context(nc.sbuf_tensor("h", [128, KT, T + 1], F32))
            s_zero = Semaphores(nc, c1).new("s_zero")
            with nc.Block() as block:
                @block.gpsimd
                def _(pool):
                    pool.memset(h[:, :, 0:1], 0.0).then_inc(s_zero, 1)
                    pool.wait_ge(s_zero, 1)
            norm_phase(nc, "n1", xT.rearrange("(k p) t -> p k t", p=128), h[:, :, 1:T + 1],
                       vec[:, V["norm1"]:V["norm1"] + KT], ones)
            rwkv_projections(nc, h, vec, w_in, w_up, a_up, proj)
        rwkv_recurrence(nc, proj, yT, vec, consts)
        with ExitStack() as c2:
            y = c2.enter_context(nc.sbuf_tensor("y", [128, KT, T], F32))
            output_projection(nc, "o1", yT, y, w_out, xT, x2T)
        with ExitStack() as c3:
            qkv = [c3.enter_context(nc.sbuf_tensor(f"qkv{i}", [128, CB, T], F32)) for i in range(3)]
            with ExitStack() as c4:
                h2 = c4.enter_context(nc.sbuf_tensor("h2", [128, KT, T], F32))
                norm_phase(nc, "n2", x2T.rearrange("(k p) t -> p k t", p=128), h2,
                           vec[:, V["norm2"]:V["norm2"] + KT], ones)
                conv_branch(nc, h2, w_in2, cvec, y_conv)
                attention_projections(nc, h2, w_in2, qkv, gains, headsum, z_gate)
            table = c3.enter_context(nc.sbuf_tensor("table", [128, NG, HEADS, 256], F32))
            bias_tables(nc, rel_bias, onehot, skew, table)
            window_attention(nc, qkv, table, ident, partial)
        with ExitStack() as c4:
            y2 = c4.enter_context(nc.sbuf_tensor("y2", [128, KT, T], F32))
            merge_attention(nc, partial, z_gate, y_conv, y2, ident)
            output_projection(nc, "o2", None, y2, w_out2, x2T, outT)


def kernel(**inputs):
    import concourse.bacc as bacc
    from concourse.bass_utils import run_bass_kernel_spmd

    a = {k: np.asarray(v) for k, v in inputs.items()}
    order = [a["l0_norm"], *(a["l0_mu"][i] for i in (0, 2, 3, 5, 1, 4)), a["l0_w0"], a["l0_a0"], a["l0_k_k"],
             a["l0_k_a"], a["l0_r_k"].reshape(-1), a["l0_gn_w"], a["l0_gn_b"], a["norm_w_2"]]
    conv = np.concatenate([a["conv_w_2"], a["conv_b_2"][None]])
    arrays = dict(
        xT=a["x"][0].T,
        vecs=np.stack(order).reshape(-1, KT, 128).transpose(2, 0, 1).reshape(128, -1),
        consts=shape_constants(),
        w_in=a["l0_w_in"], w_up=a["l0_w_up"], a_up=a["l0_a_up"], w_out=a["l0_w_out"], w_in2=a["w_in_2"],
        cvec=conv.reshape(4, CB, 128).transpose(2, 0, 1),
        gains=np.stack([np.tile(a["q_norm_w_2"], 2), np.tile(a["k_norm_w_2"], 2)], 1),
        rel_bias=a["rel_bias_2"], onehot=bucket_constants(), w_out2=a["w_out_2"],
    )
    arrays = {k: np.ascontiguousarray(v) for k, v in arrays.items()}
    nc = bacc.Bacc("TRN2", target_bir_lowering=False, num_devices=1)
    aps = {k: nc.dram_tensor(k, v.shape, F32, kind="ExternalInput").ap() for k, v in arrays.items()}
    outT = nc.dram_tensor("outT", (D, T), F32, kind="ExternalOutput").ap()
    build(nc, **aps, outT=outT)
    r = run_bass_kernel_spmd(nc, [arrays], core_ids=[0])
    return np.ascontiguousarray(r.results[0]["outT"].T)[None]
```

```python
import math
from contextlib import ExitStack

import numpy as np
import concourse.bass as bass
from concourse import mybir

F32 = mybir.dt.float32
F16 = mybir.dt.float16
ALU = mybir.AluOpType
ACT = mybir.ActivationFunctionType
AX = mybir.AxisListType
ds = bass.ds

T = 2048
D = 1024
KT = D // 128
HALF = T // 2
HB = HALF // 512
RANK = 64
EPS = 1e-6

VEC_NAMES = ["norm1", "mu_r", "mu_k", "mu_v", "mu_g", "mu_w", "mu_a", "w0", "a0", "k_k", "k_a", "r_k",
             "gn_w", "gn_b", "norm2"]
V = {n: KT * i for i, n in enumerate(VEC_NAMES)}
NVEC = KT * len(VEC_NAMES)


class Semaphores:

    def __init__(self, nc, scope):
        self.nc, self.made = nc, []
        scope.callback(self.clear)

    def new(self, name):
        self.made.append(self.nc.alloc_semaphore(name))
        return self.made[-1]

    def clear(self):
        self.nc.clear_and_free_semaphores(self.made)
        self.nc.all_engine_barrier()


def firm_wait(eng, sem, value, passed):
    eng.wait_ge(sem, value)
    eng.sem_inc(passed, 1)


class Place:

    def __init__(self, eng, sems, per, t, ahead=1, lag=0):
        self.eng, self.sems, self.per, self.t, self.ahead, self.sent = eng, sems, per, t, ahead, {}
        self.lag = lag
        self.firm = False

    def settle(self):
        self.firm = True

    def back(self, steps, name, k):
        per = self.per[name]
        value = self.t * per + ((self.ahead - steps - self.lag) * per + (per if k is None else k))
        if self.firm and not isinstance(value, int):
            firm_wait(self.eng, self.sems[name], value, self.sems["passed"])
        else:
            self.eng.wait_ge(self.sems[name], value)

    def need(self, name, k=None):
        self.back(0, name, k)

    def prev1(self, name, k=None):
        self.back(1, name, k)

    def prev(self, name, k=None):
        self.back(self.ahead, name, k)

    def did(self, ins, name, by=1):
        ins.then_inc(self.sems[name], by)
        self.firm = False
        self.sent[name] = self.sent.get(name, 0) + by

    def end(self):
        for n, k in self.sent.items():
            assert k == self.per[n], (n, k)


F32R = mybir.dt.float32r



def product_parts(w_hi, w_lo, x_hi, x_lo):
    return ((w_hi, x_hi), (w_hi, x_lo), (w_lo, x_hi))


def norm_phase(nc, name, src, h, gain, ones):
    NB = T // 512
    with ExitStack() as c:
        sems = Semaphores(nc, c)
        sq = [c.enter_context(nc.sbuf_tensor(f"{name}_sq{i}", [128, 512], F32)) for i in range(4)]
        var = c.enter_context(nc.sbuf_tensor(f"{name}_var", [128, T], F32))
        rstd = c.enter_context(nc.sbuf_tensor(f"{name}_rstd", [128, T], F32))
        total = [c.enter_context(nc.psum_tensor(f"{name}_total{i}", [128, 512], F32)) for i in range(NB)]
        loaded = [sems.new(f"{name}_loaded{k}") for k in range(KT)]
        squared = sems.new(f"{name}_squared")
        summed = sems.new(f"{name}_summed")
        meaned = sems.new(f"{name}_meaned")
        rooted = sems.new(f"{name}_rooted")
        inverted = sems.new(f"{name}_inverted")
        block = c.enter_context(nc.Block())

        @block.sync
        def _(sp):
            for k in range(KT):
                if src is not None:
                    sp.dma_start(h[:, k, :], src[:, k, :]).then_inc(loaded[k], 16)

        @block.scalar
        def _(act):
            for b in range(NB):
                for k in range(KT):
                    n = b * KT + k
                    if src is not None:
                        act.wait_ge(loaded[k], 16)
                    if n >= 4:
                        act.wait_ge(summed, n - 3)
                    act.activation(sq[n % 4][:], h[:, k, 512 * b:512 * b + 512], ACT.Square).then_inc(squared, 1)
            for b in range(NB):
                act.wait_ge(meaned, b + 1)
                act.activation(rstd[:, 512 * b:512 * b + 512], var[:, 512 * b:512 * b + 512],
                               ACT.Sqrt).then_inc(rooted, 1)

        @block.tensor
        def _(pe):
            for b in range(NB):
                for k in range(KT):
                    pe.wait_ge(squared, b * KT + k + 1)
                    pe.matmul(total[b][:], ones[:], sq[(b * KT + k) % 4][:],
                              start=k == 0, stop=k == KT - 1).then_inc(summed, 1)

        @block.vector
        def _(dve):
            for b in range(NB):
                dve.wait_ge(summed, KT * (b + 1))
                dve.tensor_scalar(var[:, 512 * b:512 * b + 512], total[b][:], 1.0 / D, EPS,
                                  ALU.mult, ALU.add).then_inc(meaned, 1)
            for b in range(NB):
                col = slice(512 * b, 512 * b + 512)
                dve.wait_ge(rooted, b + 1)
                dve.reciprocal(var[:, col], rstd[:, col]).then_inc(inverted, 1)
                dve.wait_ge(inverted, b + 1)
                for k in range(KT):
                    dve.scalar_tensor_tensor(h[:, k, col], h[:, k, col], gain[:, k:k + 1], var[:, col],
                                             ALU.mult, ALU.mult)


def split_norm_phase(nc, name, src, h_hi, h_lo, gain, ones):
    NB = T // 512
    with ExitStack() as c:
        sems = Semaphores(nc, c)
        h = [c.enter_context(nc.sbuf_tensor(f"{name}_h{i}", [128, KT, 512], F32)) for i in range(2)]
        sq = [c.enter_context(nc.sbuf_tensor(f"{name}_sq{i}", [128, 512], F32)) for i in range(4)]
        var, rstd = (c.enter_context(nc.sbuf_tensor(f"{name}_{n}", [128, T], F32)) for n in ("var", "rstd"))
        total = [c.enter_context(nc.psum_tensor(f"{name}_total{i}", [128, 512], F32)) for i in range(NB)]
        loaded = [sems.new(f"{name}_loaded{b}") for b in range(NB)]
        squared, summed, meaned, rooted, inverted, scaled, high, low = (
            sems.new(f"{name}_{n}") for n in ("squared", "summed", "meaned", "rooted", "inverted", "scaled", "high",
                                              "low"))
        block = c.enter_context(nc.Block())

        def cols(b):
            return slice(512 * b, 512 * b + 512)

        @block.sync
        def _(sp):
            for b in range(NB):
                if b >= 2:
                    sp.wait_ge(low, KT * (b - 1))
                sp.dma_start(h[b % 2][:], src[:, :, cols(b)]).then_inc(loaded[b], 16)

        @block.scalar
        def _(act):
            def squares(b):
                act.wait_ge(loaded[b], 16)
                for k in range(KT):
                    n = b * KT + k
                    if n >= 4:
                        act.wait_ge(summed, n - 3)
                    act.activation(sq[n % 4][:], h[b % 2][:, k, :], ACT.Square).then_inc(squared, 1)

            squares(0)
            for b in range(NB):
                act.wait_ge(meaned, b + 1)
                act.activation(rstd[:, cols(b)], var[:, cols(b)], ACT.Sqrt).then_inc(rooted, 1)
                if b == 0:
                    squares(1)
                for k in range(KT):
                    act.wait_ge(scaled, b * KT + k + 1)
                    act.copy(h_hi[:, k, cols(b)], h[b % 2][:, k, :]).then_inc(high, 1)
                if 1 <= b and b + 1 < NB:
                    squares(b + 1)

        @block.tensor
        def _(pe):
            for b in range(NB):
                for k in range(KT):
                    pe.wait_ge(squared, b * KT + k + 1)
                    pe.matmul(total[b][:], ones[:], sq[(b * KT + k) % 4][:],
                              start=k == 0, stop=k == KT - 1).then_inc(summed, 1)

        @block.vector
        def _(dve):
            for b in range(NB):
                dve.wait_ge(summed, KT * (b + 1))
                dve.tensor_scalar(var[:, cols(b)], total[b][:], 1.0 / D, EPS, ALU.mult, ALU.add).then_inc(meaned, 1)
                dve.wait_ge(rooted, b + 1)
                dve.reciprocal(var[:, cols(b)], rstd[:, cols(b)]).then_inc(inverted, 1)
                dve.wait_ge(inverted, b + 1)
                for k in range(KT):
                    part = h[b % 2][:, k, :]
                    dve.scalar_tensor_tensor(part, part, gain[:, k:k + 1], var[:, cols(b)],
                                             ALU.mult, ALU.mult).then_inc(scaled, 1)
                for k in range(KT):
                    dve.wait_ge(high, b * KT + k + 1)
                    dve.tensor_tensor(h_lo[:, k, cols(b)], h[b % 2][:, k, :], h_hi[:, k, cols(b)],
                                      ALU.subtract).then_inc(low, 1)


def rwkv_projections(nc, h, vec, w_in, proj):
    with ExitStack() as c:
        sems = Semaphores(nc, c)
        def sb(n, shape, dt=F32):
            return c.enter_context(nc.sbuf_tensor(f"pj_{n}", shape, dt))

        def sem(n):
            return sems.new(f"pj_{n}")

        QT = T // 4
        x_lo = [sb(f"x_lo{i}", [128, KT, QT], F32R) for i in range(2)]
        x_hi = [sb(f"x_hi{i}", [128, KT, QT], F32R) for i in range(2)]
        x = [sb(f"x{i}", [128, QT]) for i in range(2)]
        w = sb("w", [128, KT, 128])
        w_lo = sb("w_lo", [128, KT, KT, 128], F32R)
        w_hi = sb("w_hi", [128, KT, KT, 128], F32R)
        out_sb = [sb(f"out{i}", [128, QT]) for i in range(2)]
        ps = [c.enter_context(nc.psum_tensor(f"pj_ps{i}", [128, QT], F32)) for i in range(2)]
        s_diff, s_x, s_x_hi, s_x_lo, s_w_hi, s_w_lo = (sem(n) for n in ("diff", "x", "x_hi", "x_lo", "w_hi", "w_lo"))
        s_w = sem("w")
        s_mm, s_ps_free = sem("mm"), sem("ps_free")
        s_out = [sem(f"out{i}") for i in range(2)]
        block = c.enter_context(nc.Block())
        w_cols = w_in.rearrange("(k p) n -> p k n", p=128)
        proj_rows = proj.rearrange("q (j p) t -> q p j t", p=128)
        PER = 4 * KT
        FIRST = KT // 2
        SPLITS = {25: 0, 27: 1, 29: 2, 31: 3, 1: 4, 3: 5, 5: 6, 6: 7}

        def blocks(eng, body):
            with eng.Fori(0, 3) as q:
                for r in range(PER):
                    body(q, r, False)
            for r in range(PER):
                body(3, r, True)

        def next_input(q, r, last):
            if last and r >= PER - KT:
                return None
            k, quarter = r % KT, (r // KT + 1) % 4
            return k, quarter, q * PER + (KT + r), (q + (r // KT + 1) // 4) * KT + (V["mu_r"] + k)

        def next_weights(q, r, last):
            if r not in SPLITS or (last and r >= PER // 2):
                return None
            return q + 2 * r // PER, SPLITS[r]

        @block.gpsimd
        def _(pool):
            def difference(k, quarter, n):
                t0 = quarter * QT
                pool.wait_ge(s_x_lo, n)
                pool.tensor_tensor(x[k % 2][:], h[:, k, t0:t0 + QT], h[:, k, t0 + 1:t0 + QT + 1],
                                   ALU.subtract).then_inc(s_diff, 1)

            def body(q, r, last):
                if at := next_input(q, r, last):
                    difference(at[0], at[1], at[2] + 1)

            pool.sem_inc(s_x_lo, 2)
            for k in range(KT):
                difference(k, 0, k + 1)
            blocks(pool, body)

        @block.vector
        def _(dve):
            def mix(k, quarter, n, column):
                i, t0 = quarter % 2, quarter * QT
                dve.wait_ge(s_diff, n + 1)
                dve.scalar_tensor_tensor(x[k % 2][:], x[k % 2][:], vec[:, ds(column, 1)],
                                         h[:, k, t0 + 1:t0 + QT + 1], ALU.mult, ALU.add).then_inc(s_x, 1)
                dve.wait_ge(s_x_hi, n + 1)
                dve.tensor_tensor(x_lo[i][:, k, :], x[k % 2][:], x_hi[i][:, k, :],
                                  ALU.subtract).then_inc(s_x_lo, 1)

            def weights(q, j):
                dve.wait_ge(s_w_hi, q * KT + (j + 1))
                dve.tensor_tensor(w_lo[:, j], w[:], w_hi[:, j], ALU.subtract).then_inc(s_w_lo, 1)

            def body(q, r, last):
                if at := next_input(q, r, last):
                    mix(*at)
                if at := next_weights(q, r, last):
                    weights(*at)

            weights(0, 0)
            for k in range(KT):
                mix(k, 0, k, V["mu_r"] + k)
            for j in range(1, FIRST):
                weights(0, j)
            blocks(dve, body)

        @block.sync
        def _(sp):
            sp.sem_inc(s_mm, 1)
            sp.sem_inc(s_w_lo, 1)
            with sp.Fori(0, 4) as q:
                for j in range(KT):
                    sp.wait_ge(s_w_lo, q * KT + (j + 1))
                    sp.dma_start(w[:], w_cols[:, :, ds(q * D + j * 128, 128)]).then_inc(s_w, 16)

        @block.tensor
        def _(pe):
            def body(q, r, last):
                i, j, e = r % 2, r % KT, r // KT % 2
                if j == 0:
                    pe.wait_ge(s_x_lo, q * PER + (r + KT + 2))
                if r < KT:
                    pe.wait_ge(s_w_lo, q * KT + (j + 2))
                pe.wait_ge(s_ps_free, q * PER + (r + 1))
                for k in range(KT):
                    parts = product_parts(w_hi[:, j, k, :], w_lo[:, j, k, :], x_hi[e][:, k, :], x_lo[e][:, k, :])
                    for m, (wp, xp) in enumerate(parts):
                        mm = pe.matmul(ps[i][:], wp, xp, start=k == 0 and m == 0,
                                       stop=k == KT - 1 and m == len(parts) - 1)
                mm.then_inc(s_mm, 1)

            blocks(pe, body)

        @block.scalar
        def _(act):
            def high(k, quarter, n, _):
                act.wait_ge(s_x, n + 1)
                act.copy(x_hi[quarter % 2][:, k, :], x[k % 2][:]).then_inc(s_x_hi, 1)

            def weights(q, j):
                act.wait_ge(s_w, q * (16 * KT) + (16 * j + 16))
                act.copy(w_hi[:, j], w[:]).then_inc(s_w_hi, 1)

            def body(q, r, last):
                if at := next_input(q, r, last):
                    high(*at)
                if at := next_weights(q, r, last):
                    weights(*at)
                i, n = r % 2, q * PER + r
                act.wait_ge(s_mm, n + 2)
                act.wait_ge(s_out[i], q * (8 * PER) + (16 * (r // 2) + 16))
                act.copy(out_sb[i][:], ps[i][:]).then_inc(s_ps_free, 1)
                act.wait_ge(s_ps_free, n + 3)
                t0, j = r // KT * QT, r % KT
                act.dma_start(proj_rows[ds(q, 1), :, j:j + 1, t0:t0 + QT]
                              .rearrange("q p j t -> p (q j t)"), out_sb[i][:]).then_inc(s_out[i], 16)

            act.sem_inc(s_ps_free, 2)
            act.sem_inc(s_out[0], 16)
            act.sem_inc(s_out[1], 16)
            weights(0, 0)
            for k in range(KT):
                high(k, 0, k, None)
            for j in range(1, FIRST):
                weights(0, j)
            blocks(act, body)
            for i in range(2):
                act.wait_ge(s_out[i], 8 * 4 * PER + 16)


def rwkv_low_rank(nc, h, vec, w_in, w_up, a_up, proj):
    with ExitStack() as c:
        sems = Semaphores(nc, c)
        def sb(n, shape, dt=F32):
            return c.enter_context(nc.sbuf_tensor(f"lr_{n}", shape, dt))

        def sem(n):
            return sems.new(f"lr_{n}")

        xs = [sb(f"xs{i}", [128, KT, HALF]) for i in range(2)]
        diff = [sb(f"diff{i}", [128, HALF]) for i in range(2)]
        out_sb = [sb(f"out{i}", [128, HALF]) for i in range(2)]
        lo_w = sb("lo_w", [128, KT, 2 * RANK])
        lo = [sb(f"lo{i}", [RANK, T]) for i in range(2)]
        up = [sb(f"up{i}", [RANK, D]) for i in range(2)]
        ps = [c.enter_context(nc.psum_tensor(f"lr_ps{i}", [128, HALF], F32)) for i in range(2)]
        s_diff, s_xs, s_mm, s_ps_free, s_small = (sem(n) for n in ("diff", "xs", "mm", "ps_free", "small"))
        s_out = [sem(f"out{i}") for i in range(2)]
        block = c.enter_context(nc.Block())
        w_cols = w_in.rearrange("(k p) n -> p k n", p=128)
        proj_rows = proj.rearrange("q (j p) t -> q p j t", p=128)

        @block.gpsimd
        def _(pool):
            for r in range(2):
                for hv in range(2):
                    for k in range(KT):
                        n = (2 * r + hv) * KT + k
                        if n >= 2:
                            pool.wait_ge(s_xs, n - 1)
                        pool.tensor_tensor(diff[n % 2][:], h[:, k, hv * HALF:hv * HALF + HALF],
                                           h[:, k, hv * HALF + 1:hv * HALF + HALF + 1],
                                           ALU.subtract).then_inc(s_diff, 1)

        @block.vector
        def _(dve):
            for r in range(2):
                for hv in range(2):
                    if r > 0:
                        dve.wait_ge(s_mm, hv + 1)
                    for k in range(KT):
                        n = (2 * r + hv) * KT + k
                        m = V["mu_w"] + r * KT + k
                        dve.wait_ge(s_diff, n + 1)
                        dve.scalar_tensor_tensor(xs[hv][:, k, :], diff[n % 2][:], vec[:, m:m + 1],
                                                 h[:, k, hv * HALF + 1:hv * HALF + HALF + 1],
                                                 ALU.mult, ALU.add).then_inc(s_xs, 1)

        @block.sync
        def _(sp):
            sp.dma_start(lo_w[:], w_cols[:, :, 4 * D:4 * D + 2 * RANK]).then_inc(s_small, 16)
            sp.dma_start(up[0][:], w_up).then_inc(s_small, 16)
            sp.dma_start(up[1][:], a_up).then_inc(s_small, 16)

        @block.tensor
        def _(pe):
            pe.wait_ge(s_small, 48)
            n = 0
            for r in range(2):
                for hv in range(2):
                    pe.wait_ge(s_ps_free, n + 1)
                    for k in range(KT):
                        pe.wait_ge(s_xs, (2 * r + hv) * KT + k + 1)
                        for b in range(HB):
                            last = pe.matmul(ps[n % 2][0:RANK, 512 * b:512 * b + 512],
                                             lo_w[:, k, r * RANK:(r + 1) * RANK],
                                             xs[hv][:, k, 512 * b:512 * b + 512],
                                             start=k == 0, stop=k == KT - 1)
                    last.then_inc(s_mm, 1)
                    n += 1
            for r in range(2):
                for j in range(KT):
                    for hv in range(2):
                        pe.wait_ge(s_ps_free, 2 * r + hv + 3)
                        pe.wait_ge(s_ps_free, n + 1)
                        for b in range(HB):
                            t0 = hv * HALF + 512 * b
                            last = pe.matmul(ps[n % 2][:, 512 * b:512 * b + 512], up[r][:, 128 * j:128 * j + 128],
                                             lo[r][:, t0:t0 + 512], start=True, stop=True)
                        last.then_inc(s_mm, 1)
                        n += 1

        @block.scalar
        def _(act):
            act.sem_inc(s_ps_free, 2)
            act.sem_inc(s_out[0], 16)
            act.sem_inc(s_out[1], 16)
            n = 0
            for r in range(2):
                for hv in range(2):
                    act.wait_ge(s_mm, n + 1)
                    act.activation(lo[r][:, hv * HALF:(hv + 1) * HALF], ps[n % 2][0:RANK, :],
                                   ACT.Tanh if r == 0 else ACT.Copy).then_inc(s_ps_free, 1)
                    n += 1
            use = 0
            for r in range(2):
                for j in range(KT):
                    for hv in range(2):
                        v = V["w0" if r == 0 else "a0"] + j
                        act.wait_ge(s_mm, n + 1)
                        act.wait_ge(s_out[n % 2], use * 16 + 16)
                        act.activation(out_sb[n % 2][:], ps[n % 2][:], ACT.Sigmoid,
                                       bias=vec[:, v:v + 1]).then_inc(s_ps_free, 1)
                        act.wait_ge(s_ps_free, n + 3)
                        act.dma_start(proj_rows[4 + r, :, j, hv * HALF:(hv + 1) * HALF],
                                      out_sb[n % 2][:]).then_inc(s_out[n % 2], 16)
                        n += 1
                        use += hv
            for i in range(2):
                act.wait_ge(s_out[i], (use + 1) * 16)



CHUNK = 64
NCH = 128 // CHUNK
RW_HEADS = 16
RW_N = 64
DECAY = math.exp(-0.5)
GN_EPS = 64e-5
LEVELS = [1, 2, 4, 8, 16, 32]

C_WIDTHS = {"ident": 128, "headsum": 128, "maskA": 512, "maskL": 128, "merge": 128 * len(LEVELS),
            "select": 32 * KT, "selectT": 128 * KT, "restart": 1024}
C_AT, _at = {}, 0
for _n, _w in C_WIDTHS.items():
    C_AT[_n] = _at
    _at += _w
C_TOTAL = _at


def shape_constants():
    s = np.arange(128)[:, None]
    t = np.arange(128)[None, :]
    same = s // CHUNK == t // CHUNK
    strict, incl = same & (s < t), same & (s <= t)
    out = np.zeros((128, C_TOTAL), np.float32)

    def put(name, a):
        out[:, C_AT[name]:C_AT[name] + C_WIDTHS[name]] = a

    put("maskA", np.concatenate([strict, incl, strict, incl], 1))
    put("maskL", same & (s > t))
    merge = [(s // (2 * b) == t // (2 * b)) & (s // b % 2 == 1) & (t // b % 2 == 0) for b in LEVELS]
    put("merge", np.concatenate(merge, 1))
    put("ident", s == t)
    put("headsum", s // RW_N == t // RW_N)
    pairs = np.arange(KT)
    put("select", (np.arange(32) == 2 * pairs[:, None] + s[:, :, None] // RW_N).reshape(128, KT * 32))
    head = np.arange(32)[:, None]
    spread = np.concatenate([head == 2 * j + t // RW_N for j in range(KT)], 1)
    put("selectT", np.concatenate([spread, np.zeros((96, 128 * KT))]))
    put("restart", np.broadcast_to(np.arange(1024)[None, :] % CHUNK != 0, (128, 1024)))
    return out


RW_PER = dict(
    in_r=16, in_k=16, in_v=16, in_g=16, in_sw=16, in_a=16,
    scan=1, exps=2, dec=1, kkr=1, ksq=1, ksum=1, kroot=1, kclamp=1, kinv=1, kspread=1, kk=1, am=1, kp=1, at=1, rt=1, b=1, bt=1, kt=1,
    rk=1, trans=8, tok=8, amat=16, amat_sb=16, lmat=4, lmat_sb=4, l_hi=4, l_lo=4, lt16=4,
    w=20, w_sb=24, xy=24, xy_sb=24, e=4, e_sb=4, yt=4, yt_sb=4,
    t1=2, t1_sb=2, u0=2, u0_sb=2, wt=2, wt_sb=2, u=2, u_sb=2, m=2, m_add=2, m_sb=2, m_copy=1,
    y=1, y_sb=1, mean=1, yc=1, ysq=1, var=1, ystd=1, yinv=1, yspread=1, yn=1, yw=1, yb=1, bonus=1, bv=1, ysum=1,
    gsig=1, gs=1, yout=1, stored=16,
)


def rwkv_recurrence(nc, proj, yT, vec, consts):
    with ExitStack() as c:
        sems = Semaphores(nc, c)
        def sb(n, shape, dt=F32):
            return c.enter_context(nc.sbuf_tensor(f"rw_{n}", shape, dt))

        S = {n: sems.new(f"rw_{n}") for n in (*RW_PER, "passed")}
        s_init, s_const = sems.new("rw_init"), sems.new("rw_const")
        cst = sb("cst", [128, C_TOTAL])
        tile = [128, KT, 128]
        r_in, k_in, v_in, g_in, sw_in, a_in = (sb(n, tile) for n in ("r", "k", "v", "g", "sw", "a"))
        inputs = dict(r=r_in, k=k_in, v=v_in, g=g_in, sw=sw_in, a=a_in)
        csum = sb("csum", tile)
        pe1 = sb("pe1", [128, KT, NCH, CHUNK + 1])
        dec = sb("dec", [128, KT, NCH])
        pinv = sb("pinv", tile)
        kkr, tmp, am = (sb(n, tile) for n in ("kkr", "tmp", "am"))
        yraw, yn, ysq, bv = (sb(n, tile) for n in ("yraw", "yn", "ysq", "bv"))
        ar = sb("ar", [128, KT, 256])
        bt, kt, rk, ybuf = (sb(n, tile) for n in ("bt", "kt", "rk", "ybuf"))
        tok = [sb(f"tok{i}", tile) for i in range(4)]
        v_tok, b_tok, k_tok, a_tok = tok
        amat = sb("amat", [128, 2, KT, 512])
        four = [128, 4, 128]
        lmat = [sb(f"lmat{g}", four) for g in range(2)]
        l_hi, l_lo, lt16, x16, y16, w16 = ([sb(f"{n}{g}", four, F16) for g in range(2)]
                                           for n in ("l_hi", "l_lo", "lt16", "x16", "y16", "w16"))
        ident16, negid16 = sb("ident16", [128, 128], F16), sb("negid16", [128, 128], F16)
        xt32 = sb("xt32", [128, 2, KT, 128])
        t1, u0, utok = (sb(n, [128, 2, KT, RW_N]) for n in ("t1", "u0", "utok"))
        wt = sb("wt", tile)
        mst = [sb(f"m{i}", [128, KT, RW_N]) for i in range(NCH + 1)]
        mtmp = sb("mtmp", [128, KT, RW_N])
        rkbd = sb("rkbd", tile)
        gneps = sb("gneps", [32, 1])
        kinv, yinv = (sb(n, [32, 128]) for n in ("kinv", "yinv"))
        PS = c.enter_context(nc.psum_tensor("rw_ps", [128, 8, 512], F32))

        def bc(v):
            return vec[:, V[v]:V[v] + KT].unsqueeze(2).to_broadcast(tile)

        def const(name, i=0):
            at = C_AT[name] + 128 * i
            return cst[:, at:at + 128]

        def sel(j):
            at = C_AT["select"] + 32 * j
            return cst[:, at:at + 32]

        def sel_t(j):
            at = C_AT["selectT"] + 128 * j
            return cst[0:32, at:at + 128]

        def four_of(a):
            return a.unsqueeze(1).to_broadcast(four)

        def rows(g):
            return slice(RW_N * g, RW_N * (g + 1))

        def bank(b, w=128):
            return PS[:, b, :].rearrange("p (j w) -> p j w", w=w)

        def two(b, w=128):
            return PS[:, b:b + 2, :].rearrange("p b (j w) -> p (b j) w", w=w)

        XB, YB = (2, 4), (3, 5)
        TRB = (0, 1, 6, 7)

        def level(hf, l, g):
            return hf * 12 + l * 2 + g + 1

        def product(hf, l, g):
            return hf * 10 + (l - 1) * 2 + g + 1

        block = c.enter_context(nc.Block())
        p_view = proj.rearrange("q (j p) t -> q p j t", p=128)
        y_view = yT.rearrange("(j p) t -> p j t", p=128)
        TILES = T // 128

        def run(eng, step):
            def place(t, lag=0):
                return Place(eng, S, RW_PER, t, lag=lag)

            step(place(0), None, None)
            step(place(1), place(0), None)
            with eng.Fori(1, TILES - 1) as t:
                n, f, b = place(t, -1), place(t), place(t, 1)
                step(n, f, b)
                sent = {}
                for at in (n, f, b):
                    for name, k in at.sent.items():
                        sent[name] = sent.get(name, 0) + k
                assert all(RW_PER[name] == k for name, k in sent.items()), sent
            step(None, place(TILES - 1), place(TILES - 2))
            step(None, None, place(TILES - 1))

        def tokens(at):
            return ds(at.t * 128 - 128 * at.lag, 128)

        @block.sync
        def _(sp):
            def load(f, name, q, freed):
                f.settle()
                for reader in freed:
                    f.prev(reader)
                f.did(sp.dma_start(inputs[name][:], p_view[q, :, :, tokens(f)]), f"in_{name}", 16)

            def step(n, f, b):
                if f:
                    load(f, "r", 0, ["rt", "rk"])
                    load(f, "v", 2, ["bv", "trans"])
                if n:
                    load(n, "k", 1, ["kkr", "kp"])
                    load(n, "sw", 4, ["scan"])
                    load(n, "a", 5, ["am", "b"])
                if f:
                    load(f, "g", 3, ["gs"])
                if b:
                    b.need("yout")
                    b.did(sp.dma_start(y_view[:, :, tokens(b)], ybuf[:]), "stored", 16)

            sp.dma_start(cst[:], consts).then_inc(s_const, 16)
            for n in RW_PER:
                sp.sem_inc(S[n], RW_PER[n])
            run(sp, step)
            sp.wait_ge(S["stored"], 16 * (TILES + 1))

        @block.gpsimd
        def _(pool):
            pool.wait_ge(s_const, 16)
            pool.memset(pe1[:, :, :, 0:1], 1.0).then_inc(s_init, 1)
            pool.memset(mst[0][:], 0.0).then_inc(s_init, 1)
            pool.memset(gneps[:], GN_EPS).then_inc(s_init, 1)
            pool.tensor_copy(ident16[:], const("ident")).then_inc(s_init, 1)
            pool.tensor_scalar(negid16[:], const("ident"), -1.0, None, ALU.mult).then_inc(s_init, 1)
            for j in range(KT):
                pool.tensor_scalar(rkbd[:, j, :], const("headsum"), vec[:, V["r_k"] + j:V["r_k"] + j + 1], None,
                                   ALU.mult).then_inc(s_init, 1)

            def split_l(f, hf):
                for g in range(2):
                    G = 2 * hf + g + 1
                    f.settle()
                    f.need("lmat_sb", G)
                    f.did(pool.tensor_copy(l_hi[g][:], lmat[g][:]), "l_hi")
                    f.need("l_hi", G)
                    f.did(pool.tensor_tensor(l_lo[g][:], lmat[g][:], l_hi[g][:], ALU.subtract), "l_lo")

            def step(n, f, b):
                if f:
                    f.need("kk")
                    f.need("in_a")
                    f.prev("lmat")
                    f.did(pool.tensor_tensor(bt[:], kkr[:], a_in[:], ALU.mult), "b")
                    split_l(f, 0)
                    f.need("kp")
                    f.need("in_r")
                    f.prev("bonus")
                    f.did(pool.tensor_tensor(rk[:], r_in[:], am[:], ALU.mult), "rk")
                if b:
                    b.need("gsig")
                    b.did(pool.tensor_tensor(ybuf[:], g_in[:], ybuf[:], ALU.mult), "gs")
                    b.need("yn")
                    b.did(pool.tensor_tensor(yn[:], yn[:], bc("gn_w"), ALU.mult), "yw")
                    b.need("yw")
                    b.did(pool.tensor_tensor(yn[:], yn[:], bc("gn_b"), ALU.add), "yb")
                if n:
                    n.need("in_k")
                    n.prev("at")
                    n.prev("b")
                    n.did(pool.tensor_tensor(kkr[:], k_in[:], bc("k_k"), ALU.mult), "kkr")
                if f:
                    split_l(f, 1)

            run(pool, step)

        @block.scalar
        def _(act):
            act.wait_ge(s_const, 16)
            act.wait_ge(s_init, 5 + KT)
            heads_of = "p (g j w) -> p g j w"

            def decays(n, i):
                flat = csum[:].rearrange("p j (c s) -> p j c s", s=CHUNK)
                if i == 0:
                    n.need("scan")
                    n.prev("at")
                    n.prev("rt")
                    n.prev("bt")
                    n.prev("dec")
                    n.did(act.activation(pe1[:, :, :, 1:CHUNK + 1], flat, ACT.Exp, scale=-DECAY), "exps")
                else:
                    n.did(act.activation(pinv[:], csum[:], ACT.Exp, scale=DECAY), "exps")

            def key_squares(n):
                n.need("kkr")
                n.did(act.activation(tmp[:], kkr[:], ACT.Square), "ksq")

            def key_root(n):
                n.need("ksum")
                n.prev("kspread")
                n.did(act.activation(kinv[:], PS[0:32, 6, 0:128], ACT.Sqrt), "kroot")

            def inverse(n, f, b, hf):
                for g in range(2):
                    f.need("amat_sb", 8 * hf + 8)
                    f.did(act.copy(lt16[g][:], amat[:, g, 4 * hf:4 * hf + 4, 0:128]), "lt16")
                for l in range(6):
                    for g in range(2):
                        f.need("xy", level(hf, l, g))
                        act.copy(x16[g][:], bank(XB[g]))
                        f.did(act.copy(y16[g][:], bank(YB[g])), "xy_sb")
                    if hf == 0 and l == 1 and b:
                        b.need("yc")
                        b.did(act.activation(ysq[:], yn[:], ACT.Square), "ysq")
                    if hf == 0 and l == 3 and b:
                        std(b)
                    if hf == 1 and l == 0:
                        t1_copy(f, 0)
                    if hf == 1 and l == 1:
                        u0_copy(f, 0)
                    if hf == 1 and l == 2:
                        wt_copy(f, 0)
                    if hf == 1 and l == 4:
                        t1_copy(f, 1)
                    if hf == 1 and n:
                        if l == 1:
                            key_squares(n)
                        if l == 3:
                            decays(n, 0)
                        if l == 4:
                            decays(n, 1)
                        if l == 5:
                            key_root(n)
                for g in range(2):
                    f.need("yt", 2 * hf + g + 1)
                    f.did(act.copy(xt32[:, g, 4 * hf:4 * hf + 4, :], bank(YB[g])), "yt_sb")

            def std(b):
                b.need("var")
                b.prev("yspread")
                b.did(act.activation(yinv[:], PS[0:32, 6, 0:128], ACT.Sqrt, bias=gneps[:], scale=1.0 / RW_N), "ystd")

            def t1_copy(f, hf):
                f.need("t1", hf + 1)
                f.did(act.copy(t1[:, :, 4 * hf:4 * hf + 4, :], PS[:, 0, :].rearrange(heads_of, g=2, w=RW_N)), "t1_sb")

            def u0_copy(f, hf):
                f.need("u0", hf + 1)
                f.did(act.copy(u0[:, :, 4 * hf:4 * hf + 4, :], PS[:, 1, :].rearrange(heads_of, g=2, w=RW_N)), "u0_sb")

            def wt_copy(f, hf):
                f.need("wt", hf + 1)
                f.did(act.copy(wt[:, 4 * hf:4 * hf + 4, :], bank(0)), "wt_sb")

            def step(n, f, b):
                if n and not f:
                    decays(n, 0)
                    decays(n, 1)
                    key_squares(n)
                    key_root(n)
                if b:
                    b.need("y")
                    b.prev("mean")
                    b.prev("yc")
                    b.did(act.copy(yraw[:], two(4)), "y_sb")
                    b.need("m_sb")
                    b.did(act.copy(mst[0][:], mst[2][:]), "m_copy")
                if f:
                    for i in range(8):
                        f.need("trans", i + 1)
                        f.did(act.copy(tok[i // 2][:, 4 * (i % 2):4 * (i % 2) + 4, :], bank(TRB[i % 4])), "tok")
                    f.need("exps")
                    f.prev("m_sb")
                    f.did(act.copy(dec[:], pe1[:, :, :, CHUNK]), "dec")
                    inverse(n, f, b, 0)
                elif b:
                    b.need("yc")
                    b.did(act.activation(ysq[:], yn[:], ACT.Square), "ysq")
                    std(b)
                if b:
                    b.need("in_g")
                    b.prev("stored")
                    b.did(act.activation(ybuf[:], g_in[:], ACT.Sigmoid), "gsig")
                if f:
                    inverse(n, f, b, 1)
                    u0_copy(f, 1)
                    wt_copy(f, 1)

            run(act, step)

        @block.vector
        def _(dve):
            dve.wait_ge(s_const, 16)
            dve.wait_ge(s_init, 5 + KT)
            split = "p j (c s) -> p j c s"

            def masked(f, n):
                f.need("amat", n + 1)
                f.did(dve.tensor_tensor(amat[:, n % 2, n // 2, :], PS[:, n % 2, :],
                                        cst[:, C_AT["maskA"]:C_AT["maskA"] + 512], ALU.mult), "amat_sb")

            def u_sum(b, ci):
                s = slice(CHUNK * ci, CHUNK * (ci + 1))
                b.need("u0_sb")
                b.need("u", ci + 1)
                b.did(dve.tensor_tensor(utok[s].rearrange("p g j v -> p g (j v)"), PS[s, 6:8, :],
                                        u0[s].rearrange("p g j v -> p g (j v)"), ALU.add), "u_sb")

            def m_next(b, ci):
                if ci == 0:
                    b.prev("m_copy")
                else:
                    b.need("m_sb", ci)
                b.need("m", ci + 1)
                b.did(dve.tensor_tensor(mtmp[:], bank(2 + ci, RW_N), mst[ci][:], ALU.add), "m_add")
                b.need("m_add", ci + 1)
                b.need("dec")
                b.did(dve.tensor_tensor(mst[ci + 1][:], mtmp[:], dec[:, :, ci:ci + 1].to_broadcast([128, KT, RW_N]),
                                        ALU.mult), "m_sb")

            def centre(b):
                b.need("mean")
                b.need("y_sb")
                b.prev("yout")
                b.did(dve.scalar_tensor_tensor(yn[:], two(6), -1.0 / RW_N, yraw[:], ALU.mult, ALU.add), "yc")

            def inverse_std(b):
                b.need("ystd")
                b.did(dve.reciprocal(yinv[:], yinv[:]), "yinv")

            def scale(b):
                b.need("yspread")
                b.did(dve.tensor_tensor(yn[:], yn[:], two(6), ALU.mult), "yn")

            def finish(b):
                b.need("yb")
                b.need("bv")
                b.did(dve.tensor_tensor(yn[:], yn[:], bv[:], ALU.add), "ysum")
                b.need("ysum")
                b.need("gs")
                b.did(dve.tensor_tensor(ybuf[:], yn[:], ybuf[:], ALU.mult), "yout")

            def decay_sums(n):
                n.need("in_sw")
                n.prev("exps")
                at = C_AT["restart"]
                n.did(dve.tensor_tensor_scan(csum[:].rearrange("p j s -> p (j s)"), cst[:, at:at + 1024],
                                             sw_in[:].rearrange("p j s -> p (j s)"), 0.0, ALU.mult, ALU.add),
                      "scan")

            def key_factor(n):
                n.need("in_a")
                n.prev("kt")
                n.prev("rk")
                n.did(dve.scalar_tensor_tensor(am[:], a_in[:], -1.0, bc("k_a"), ALU.add, ALU.mult), "am")

            def keys(n):
                n.need("am")
                n.need("in_k")
                n.did(dve.scalar_tensor_tensor(am[:], am[:], 1.0, k_in[:], ALU.add, ALU.mult), "kp")

            def inverse_norm(n):
                n.need("kroot")
                n.did(dve.tensor_scalar(kinv[:], kinv[:], 1e-12, None, ALU.max), "kclamp")
                n.need("kclamp")
                n.did(dve.reciprocal(kinv[:], kinv[:]), "kinv")
                n.need("exps")
                n.need("kp")
                n.prev("amat")
                n.did(dve.tensor_tensor(kt[:], am[:], pinv[:], ALU.mult), "kt")

            def inverse(n, f, b, hf):
                for g in range(2):
                    f.need("lmat", 2 * hf + g + 1)
                    f.did(dve.tensor_tensor(w16[g][:], bank(XB[g]), four_of(const("merge")), ALU.mult), "w_sb")
                    f.did(dve.tensor_tensor(lmat[g][:], bank(XB[g]), four_of(const("maskL")), ALU.mult), "lmat_sb")
                for l in range(1, 6):
                    for g in range(2):
                        f.need("w", product(hf, l, g))
                        f.did(dve.tensor_tensor(w16[g][:], bank(XB[g]), four_of(const("merge", l)), ALU.mult), "w_sb")
                    if hf == 0 and l == 1 and b:
                        centre(b)
                    if hf == 0 and l < 5:
                        masked(f, 8 + 2 * (l - 1))
                        masked(f, 9 + 2 * (l - 1))
                    if hf == 0 and l == 4 and b:
                        inverse_std(b)
                    if hf == 1 and l == 3 and b:
                        finish(b)
                    if hf == 1 and l == 4:
                        f.need("bonus")
                        f.prev("ysum")
                        f.did(dve.tensor_tensor(bv[:], two(6), v_in[:], ALU.mult), "bv")
                    if hf == 1 and n:
                        if l == 1:
                            decay_sums(n)
                        if l == 2:
                            key_factor(n)
                        if l == 5:
                            keys(n)
                for g in range(2):
                    f.need("e", 2 * hf + g + 1)
                    f.did(dve.tensor_copy(w16[g][:], bank(XB[g])), "e_sb")

            def step(n, f, b):
                if n and not f:
                    decay_sums(n)
                    key_factor(n)
                    keys(n)
                    inverse_norm(n)
                if f:
                    f.need("kspread")
                    f.did(dve.tensor_tensor(kkr[:], kkr[:], two(2), ALU.mult), "kk")
                if b:
                    b.prev("y")
                    u_sum(b, 0)
                    m_next(b, 0)
                if f:
                    f.need("b")
                    f.need("exps")
                    f.prev("lmat")
                    f.did(dve.tensor_tensor(bt[:], bt[:], pinv[:], ALU.mult), "bt")
                if b:
                    u_sum(b, 1)
                if f:
                    f.need("kk")
                    f.did(dve.scalar_tensor_tensor(ar[:, :, 0:128].rearrange(split, s=CHUNK),
                                                   kkr[:].rearrange(split, s=CHUNK), -1.0, pe1[:, :, :, 0:CHUNK],
                                                   ALU.mult, ALU.mult), "at")
                if b:
                    m_next(b, 1)
                if f:
                    f.need("in_r")
                    f.prev("y")
                    f.did(dve.tensor_tensor(ar[:, :, 128:256].rearrange(split, s=CHUNK),
                                            r_in[:].rearrange(split, s=CHUNK), pe1[:, :, :, 1:CHUNK + 1],
                                            ALU.mult), "rt")
                    for i in range(8):
                        masked(f, i)
                    inverse(n, f, b, 0)
                elif b:
                    centre(b)
                    inverse_std(b)
                if b:
                    scale(b)
                if f:
                    inverse(n, f, b, 1)
                    if n:
                        inverse_norm(n)
                elif b:
                    finish(b)

            run(dve, step)

        @block.tensor
        def _(pe):
            pe.wait_ge(s_const, 16)
            pe.wait_ge(s_init, 5 + KT)

            def sums_by_head(src):
                for j in range(KT):
                    last = pe.matmul(PS[0:32, 6, 0:128], sel(j), src[:, j, :], start=j == 0, stop=j == KT - 1)
                return last

            def spread(src, at):
                for j in range(KT):
                    last = pe.matmul(two(at)[:, j, :], sel_t(j), src[:], start=True, stop=True)
                return last

            def head_sums(src, at):
                for i in range(2):
                    last = pe.matmul(PS[:, at + i, :], const("headsum"),
                                     src[:, 4 * i:4 * i + 4, :].rearrange("p j s -> p (j s)"), start=True, stop=True)
                return last

            def a_matrices(f, n):
                jj, g = n // 2, n % 2
                R = rows(g)
                if n >= 2:
                    f.need("amat_sb", n - 1)
                pe.matmul(PS[:, g, 0:256], bt[R, jj, :], ar[R, jj, :], start=True, stop=True)
                f.did(pe.matmul(PS[:, g, 256:512], kt[R, jj, :], ar[R, jj, :], start=True, stop=True), "amat")

            def a_ak_v(f, hf):
                for g in range(2):
                    for jj in range(4):
                        j = 4 * hf + jj
                        q = (4 * g + jj) * RW_N
                        last = pe.matmul(PS[:, 0, q:q + RW_N], amat[:, g, j, 256:384], v_tok[:, j, rows(g)],
                                         start=True, stop=True)
                f.did(last, "t1")

            def u_zero(f, hf):
                f.need("t1_sb", hf + 1)
                f.need("yt_sb", 2 * hf + 2)
                for g in range(2):
                    for jj in range(4):
                        q = (4 * g + jj) * RW_N
                        last = pe.matmul(PS[:, 1, q:q + RW_N], xt32[:, g, 4 * hf + jj, :], t1[:, g, 4 * hf + jj, :],
                                         start=True, stop=True)
                f.did(last, "u0")

            def w_tilde(f, hf):
                for g in range(2):
                    for jj in range(4):
                        j = 4 * hf + jj
                        last = pe.matmul(bank(0)[rows(g), jj, :], a_tok[:, j, rows(g)], xt32[:, g, j, :],
                                         start=True, stop=True)
                f.did(last, "wt")

            def u_state(b, ci):
                s = slice(CHUNK * ci, CHUNK * (ci + 1))
                b.settle()
                if ci == 0:
                    b.prev("m_copy")
                else:
                    b.need("m_sb", ci)
                for g in range(2):
                    for j in range(KT):
                        last = pe.matmul(PS[s, 6 + g, RW_N * j:RW_N * (j + 1)], wt[rows(g), j, s],
                                         mst[ci][rows(g), j, :], start=True, stop=True)
                b.did(last, "u")

            def m_from_v(ci):
                s = slice(CHUNK * ci, CHUNK * (ci + 1))
                for g in range(2):
                    for j in range(KT):
                        pe.matmul(bank(2 + ci, RW_N)[rows(g), j, :], k_tok[s, j, rows(g)], v_tok[s, j, rows(g)],
                                  start=j == 0, stop=True, skip_group_check=True)

            def m_from_u(b, ci):
                s = slice(CHUNK * ci, CHUNK * (ci + 1))
                b.settle()
                b.need("u_sb", ci + 1)
                for g in range(2):
                    for j in range(KT):
                        last = pe.matmul(bank(2 + ci, RW_N)[rows(g), j, :], b_tok[s, j, rows(g)], utok[s, g, j, :],
                                         start=False, stop=True, skip_group_check=True)
                b.did(last, "m")

            def y_from_v():
                for g in range(2):
                    for j in range(KT):
                        pe.matmul(two(4)[rows(g), j, :], v_tok[:, j, rows(g)], amat[:, g, j, 384:512],
                                  start=j % 4 == 0, stop=True, skip_group_check=True)

            def y_from_u(b):
                for g in range(2):
                    R = rows(g)
                    for j in range(KT):
                        o = two(4)[R, j, :]
                        pe.matmul(o, utok[:, g, j, :], amat[:, g, j, 128:256], start=False, stop=True,
                                  skip_group_check=True)
                        for ci in range(NCH):
                            s = slice(CHUNK * ci, CHUNK * (ci + 1))
                            last = pe.matmul(o[:, s], mst[ci][R, j, :], ar[R, j, 128 + CHUNK * ci:192 + CHUNK * ci],
                                             start=False, stop=True, skip_group_check=True)
                b.did(last, "y")

            def mean(b):
                b.need("y_sb")
                b.did(head_sums(yraw, 6), "mean")

            def variance(b):
                b.need("ysq")
                b.did(sums_by_head(ysq), "var")

            def spread_inverse_std(b):
                b.need("yinv")
                b.did(spread(yinv, 6), "yspread")

            def key_sums(n):
                n.need("ksq")
                n.prev("bv")
                n.did(sums_by_head(tmp), "ksum")

            def key_spread(n):
                n.need("kinv")
                n.did(spread(kinv, 2), "kspread")

            def bonus(f, b):
                f.need("rk")
                if b:
                    b.need("yn")
                for j in range(KT):
                    last = pe.matmul(two(6)[:, j, :], rkbd[:, j, :], rk[:, j, :], start=True, stop=True)
                f.did(last, "bonus")

            def inverse(n, f, b, hf):
                for g in range(2):
                    R = rows(g)
                    for jj in range(4):
                        last = pe.matmul(bank(XB[g])[:, jj, :], ar[R, 4 * hf + jj, 0:128], bt[R, 4 * hf + jj, :],
                                         start=True, stop=True)
                    f.did(last, "lmat")
                for l in range(6):
                    for g in range(2):
                        if l == 0:
                            continue
                        f.need("xy_sb", level(hf, l - 1, g))
                        if l == 1:
                            f.need("lt16", 2 * hf + g + 1)
                        for jj in range(4):
                            last = pe.matmul(bank(XB[g])[:, jj, :], lt16[g][:, jj, :], x16[g][:, jj, :],
                                             start=True, stop=True)
                        f.did(last, "w")
                    if hf == 0 and l == 0 and b:
                        mean(b)
                    if hf == 0 and 1 <= l < 5:
                        a_matrices(f, 8 + 2 * (l - 1))
                        a_matrices(f, 9 + 2 * (l - 1))
                    if hf == 0 and l == 3 and b:
                        variance(b)
                    if hf == 0 and l == 5 and b:
                        spread_inverse_std(b)
                    if hf == 1 and l == 0:
                        f.need("amat_sb")
                        a_ak_v(f, 0)
                    if hf == 1 and l == 1:
                        u_zero(f, 0)
                    if hf == 1 and l == 2:
                        w_tilde(f, 0)
                    if hf == 1 and l == 3:
                        bonus(f, b)
                    if hf == 1 and l == 4:
                        f.need("wt_sb", 1)
                        a_ak_v(f, 1)
                    if hf == 1 and l == 5 and n:
                        key_sums(n)
                    for g in range(2):
                        f.need("w_sb", level(hf, l, g))
                        if l == 0:
                            f.need("lmat_sb", 2 * hf + g + 1)
                            if hf == 1:
                                f.need("yt_sb", g + 1)
                        for jj in range(4):
                            W = w16[g][:, jj, :]
                            X, Y = (x16[g][:, jj, :], y16[g][:, jj, :]) if l else (ident16[:], ident16[:])
                            pe.matmul(bank(XB[g])[:, jj, :], Y, W, start=True, stop=False)
                            pe.matmul(bank(XB[g])[:, jj, :], ident16[:], X, start=False, stop=True)
                            pe.matmul(bank(YB[g])[:, jj, :], W, Y, start=True, stop=False)
                            last = pe.matmul(bank(YB[g])[:, jj, :], ident16[:], Y, start=False, stop=True)
                        f.did(last, "xy")
                for g in range(2):
                    f.need("xy_sb", level(hf, 5, g))
                    f.need("l_lo", 2 * hf + g + 1)
                    for jj in range(4):
                        Y = y16[g][:, jj, :]
                        pe.matmul(bank(XB[g])[:, jj, :], l_hi[g][:, jj, :], Y, start=True, stop=False)
                        pe.matmul(bank(XB[g])[:, jj, :], l_lo[g][:, jj, :], Y, start=False, stop=False)
                        pe.matmul(bank(XB[g])[:, jj, :], negid16[:], Y, start=False, stop=False)
                        last = pe.matmul(bank(XB[g])[:, jj, :], ident16[:], ident16[:], start=False, stop=True)
                    f.did(last, "e")
                for g in range(2):
                    f.need("e_sb", 2 * hf + g + 1)
                    for jj in range(4):
                        pe.matmul(bank(YB[g])[:, jj, :], x16[g][:, jj, :], w16[g][:, jj, :], start=True, stop=False)
                        last = pe.matmul(bank(YB[g])[:, jj, :], ident16[:], y16[g][:, jj, :], start=False, stop=True)
                    f.did(last, "yt")

            def step(n, f, b):
                if n and not f:
                    key_sums(n)
                    key_spread(n)
                if b:
                    b.need("wt_sb")
                    b.need("u0_sb")
                    b.need("yt_sb")
                    b.need("bv")
                    if f:
                        f.need("kroot")
                    u_state(b, 0)
                    if f:
                        f.settle()
                        f.need("kk")
                    m_from_v(0)
                    m_from_u(b, 0)
                    m_from_v(1)
                    u_state(b, 1)
                    y_from_v()
                    m_from_u(b, 1)
                    y_from_u(b)
                if f:
                    for i, (src, made) in enumerate((s, m) for s, m in ((v_in, "in_v"), (bt, "bt"), (kt, "kt"),
                                                                        (ar, "at")) for _ in range(2)):
                        f.need(made)
                        if i >= 4:
                            f.need("tok", i - 3)
                        for jj in range(4):
                            last = pe.transpose(bank(TRB[i % 4])[:, jj, :], src[:, 4 * (i % 2) + jj, 0:128],
                                                const("ident"))
                        f.did(last, "trans")
                    f.need("rt")
                    f.need("tok", 6)
                    for i in range(8):
                        a_matrices(f, i)
                    f.need("tok")
                    f.prev("m_add")
                    f.prev("y_sb")
                    inverse(n, f, b, 0)
                elif b:
                    mean(b)
                    variance(b)
                    spread_inverse_std(b)
                if f:
                    inverse(n, f, b, 1)
                    u_zero(f, 1)
                    if n:
                        key_spread(n)
                    w_tilde(f, 1)

            run(pe, step)



def output_projection(nc, name, src, y, w_out, residual, dst):
    per = dict(w0=16, w1=16, w_hi=2, w_lo=2, res0=32, res1=32, out0=32, out1=32, mm=4, sum=4)
    with ExitStack() as c:
        sems = Semaphores(nc, c)
        def sb(n, shape, dt=F32):
            return c.enter_context(nc.sbuf_tensor(f"{name}_{n}", shape, dt))

        S = {n: sems.new(f"{name}_{n}") for n in per}
        s_y = [sems.new(f"{name}_y{k}") for k in range(4)]
        s_y_hi, s_y_lo = sems.new(f"{name}_y_hi"), sems.new(f"{name}_y_lo")
        y_hi, y_lo = (sb(n, [128, KT, T], F32R) for n in ("y_hi", "y_lo"))
        w = [sb(f"w{i}", [128, KT, 128]) for i in range(2)]
        w_hi = [sb(f"w_hi{i}", [128, KT, 128], F32R) for i in range(2)]
        w_lo = [sb(f"w_lo{i}", [128, KT, 128], F32R) for i in range(2)]
        res = [sb(f"res{i}", [128, HALF]) for i in range(2)]
        out = [sb(f"out{i}", [128, HALF]) for i in range(2)]
        ps = [c.enter_context(nc.psum_tensor(f"{name}_ps{i}", [128, HALF], F32)) for i in range(2)]
        block = c.enter_context(nc.Block())
        w_cols = w_out.rearrange("(k p) n -> p k n", p=128)
        res_v = residual.rearrange("(j p) t -> j p t", p=128)
        dst_v = dst.rearrange("(j p) t -> j p t", p=128)
        PAIRS = KT // 2
        stage = [*out, *res]
        LOADED = 2 * (KT if y is None else KT - y.shape[1])

        def value(n):
            return stage[n % 4][:] if n < LOADED else y[:, (n - LOADED) // 2, HALF * (n % 2):HALF * (n % 2) + HALF]

        def at_half(a, n):
            return a[:, n // 2, HALF * (n % 2):HALF * (n % 2) + HALF]

        def part(dram, c2, i, hv):
            return dram[ds(c2 * 2 + i, 1), :, HALF * hv:HALF * hv + HALF].rearrange("j p t -> p (j t)")

        def pairs(eng, split, use):
            split(Place(eng, S, per, 0), 0)
            with eng.Fori(0, PAIRS - 1) as c2:
                at = Place(eng, S, per, c2)
                split(at, 1)
                use(at, c2, 0)
                split(Place(eng, S, per, c2, lag=-1), 0)
                use(at, c2, 1)
            at = Place(eng, S, per, PAIRS - 1)
            split(at, 1)
            use(at, PAIRS - 1, 0)
            use(at, PAIRS - 1, 1)

        @block.sync
        def _(sp):
            for n in per:
                sp.sem_inc(S[n], per[n])
            def load(at, column, i):
                at.did(sp.dma_start(w[i][:], w_cols[:, :, ds(column, 128)]), f"w{i}", 16)

            def step(at, after, c2):
                for i in range(2):
                    for hv in range(2):
                        if i:
                            at.need("sum", hv + 1)
                        else:
                            at.prev("sum", 3 + hv)
                        at.did(sp.dma_start(res[hv][:], part(res_v, c2, i, hv)), f"res{hv}", 16)
                    if after:
                        at.need("mm", 2 * i + 2)
                        load(after, c2 * 256 + (256 + 128 * i), i)

            for i in range(2):
                load(Place(sp, S, per, 0), 128 * i, i)
            for n in range(LOADED):
                if n >= 4:
                    sp.wait_ge(s_y_lo, n - 3)
                sp.dma_start(stage[n % 4][:], src[128 * (n // 2):128 * (n // 2) + 128,
                                                  HALF * (n % 2):HALF * (n % 2) + HALF]).then_inc(s_y[n % 4], 16)
            sp.wait_ge(s_y_lo, LOADED)
            with sp.Fori(0, PAIRS - 1) as c2:
                step(Place(sp, S, per, c2), Place(sp, S, per, c2, lag=-1), c2)
            step(Place(sp, S, per, PAIRS - 1), None, PAIRS - 1)

        @block.scalar
        def _(act):
            def split(at, i):
                at.need(f"w{i}")
                at.did(act.copy(w_hi[i][:], w[i][:]), "w_hi")

            def store(at, c2, i):
                for hv in range(2):
                    at.need("sum", 2 * i + hv + 1)
                    at.did(act.dma_start(part(dst_v, c2, i, hv), out[hv][:]), f"out{hv}", 16)

            for n in range(2 * KT):
                if n < LOADED:
                    act.wait_ge(s_y[n % 4], 16 * (n // 4 + 1))
                act.copy(at_half(y_hi, n), value(n)).then_inc(s_y_hi, 1)
            pairs(act, split, store)
            for hv in range(2):
                act.wait_ge(S[f"out{hv}"], 32 * (PAIRS + 1))

        @block.tensor
        def _(pe):
            with pe.Fori(0, PAIRS) as c2:
                at = Place(pe, S, per, c2)
                for i in range(2):
                    at.need("w_lo", i + 1)
                    for hv in range(2):
                        if i:
                            at.need("sum", hv + 1)
                        else:
                            at.prev("sum", 3 + hv)
                        for k in range(KT):
                            if i == 0 and hv == 0:
                                pe.wait_ge(s_y_lo, 2 * k + 2)
                            parts = product_parts(w_hi[i], w_lo[i], y_hi, y_lo)
                            for m, (wp, yp) in enumerate(parts):
                                for b in range(HB):
                                    t0 = HALF * hv + 512 * b
                                    last = pe.matmul(ps[hv][:, 512 * b:512 * b + 512], wp[:, k, :],
                                                     yp[:, k, t0:t0 + 512], start=k == 0 and m == 0,
                                                     stop=k == KT - 1 and m == len(parts) - 1)
                        at.did(last, "mm")
                at.end()

        @block.vector
        def _(dve):
            def split(at, i):
                at.need("w_hi", i + 1)
                at.did(dve.tensor_tensor(w_lo[i][:], w[i][:], w_hi[i][:], ALU.subtract), "w_lo")

            def add(at, c2, i):
                for hv in range(2):
                    at.need("mm", 2 * i + hv + 1)
                    at.need(f"res{hv}", 16 * (i + 1))
                    if i:
                        at.need(f"out{hv}", 16)
                    else:
                        at.prev(f"out{hv}", 32)
                    at.did(dve.tensor_tensor(out[hv][:], ps[hv][:], res[hv][:], ALU.add), "sum")

            for n in range(2 * KT):
                dve.wait_ge(s_y_hi, n + 1)
                dve.tensor_tensor(at_half(y_lo, n), value(n), at_half(y_hi, n), ALU.subtract).then_inc(s_y_lo, 1)
            pairs(dve, split, add)



CW = D // 2
CB = CW // 128
HEADS = 8
DH = 64


def conv_branch(nc, h2_hi, h2_lo, w_in, cvec, y2):
    order = (2, 0, 1, 3)
    per = dict(w0=32, w1=32, w_hi=4, w_lo=4, mm=8, gc=2, zu=2, tap0=1, tap1=1, tap2=1, gb=2, sig=2, sil=2, yc=1,
               out=16)
    with ExitStack() as c:
        sems = Semaphores(nc, c)
        def sb(n, shape, dt=F32):
            return c.enter_context(nc.sbuf_tensor(f"cv_{n}", shape, dt))

        S = {n: sems.new(f"cv_{n}") for n in (*per, "passed")}
        s_zero = sems.new("cv_zero")
        w = [sb(f"w{i}", [128, KT, 128]) for i in range(2)]
        w_hi = [sb(f"w_hi{i}", [128, KT, 128], F32R) for i in range(2)]
        w_lo = [sb(f"w_lo{i}", [128, KT, 128], F32R) for i in range(2)]
        gc, conv = sb("gc", [128, T]), sb("conv", [128, T])
        sig = gc
        zu = sb("zu", [128, T + 2])
        vec = sb("vec", [128, 4, CB])
        ps = [c.enter_context(nc.psum_tensor(f"cv_ps{i}", [128, HALF], F32)) for i in range(4)]
        block = c.enter_context(nc.Block())
        w_cols = w_in.rearrange("(k p) n -> p k n", p=128)

        def half(hv, shift=0):
            return slice(HALF * hv + shift, HALF * hv + HALF + shift)

        READ = {0: "gc", 1: "zu", 2: "gb", 3: "sil"}

        def groups(eng, split, step):
            first = Place(eng, S, per, 0)
            split(first, 0)
            split(first, 1)
            with eng.Fori(0, CB - 1) as g:
                step(Place(eng, S, per, g), Place(eng, S, per, g, lag=-1), g)
            step(Place(eng, S, per, CB - 1), None, CB - 1)

        @block.sync
        def _(sp):
            for n in per:
                sp.sem_inc(S[n], per[n])
            with sp.Fori(0, CB) as g:
                at = Place(sp, S, per, g)
                for m in range(4):
                    at.settle()
                    if m < 2:
                        at.prev("mm", 2 * m + 6)
                    else:
                        at.need("mm", 2 * m - 2)
                    at.did(sp.dma_start(w[m % 2][:], w_cols[:, :, ds(g * 128 + order[m] * CW, 128)]), f"w{m % 2}", 16)
                at.end()

        @block.tensor
        def _(pe):
            with pe.Fori(0, CB) as g:
                at = Place(pe, S, per, g)
                for m in range(4):
                    at.need("w_lo", m + 1)
                    for hv in range(2):
                        if m < 2:
                            at.prev(READ[m + 2], hv + 1)
                        else:
                            at.need(READ[m - 2], hv + 1)
                        for k in range(KT):
                            parts = product_parts(w_hi[m % 2], w_lo[m % 2], h2_hi, h2_lo)
                            for n, (wp, hp) in enumerate(parts):
                                for b in range(HB):
                                    t0 = HALF * hv + 512 * b
                                    last = pe.matmul(ps[2 * (m % 2) + hv][:, 512 * b:512 * b + 512], wp[:, k, :],
                                                     hp[:, k, t0:t0 + 512], start=k == 0 and n == 0,
                                                     stop=k == KT - 1 and n == len(parts) - 1)
                        at.did(last, "mm")
                at.end()

        @block.scalar
        def _(act):
            def split(at, m):
                at.need(f"w{m % 2}", 16 * (m // 2 + 1))
                at.did(act.copy(w_hi[m % 2][:], w[m % 2][:]), "w_hi")

            def step(at, after, g):
                at.prev("yc")
                for hv in range(2):
                    at.need("mm", hv + 1)
                    at.did(act.copy(gc[:, half(hv)], ps[hv][:]), "gc")
                split(at, 2)
                split(at, 3)
                at.need("zu")
                if after:
                    split(after, 0)
                for hv in range(2):
                    at.need("mm", 7 + hv)
                    at.did(act.activation(sig[:, half(hv)], ps[2 + hv][:], ACT.Sigmoid), "sig")
                if after:
                    split(after, 1)
                at.need("yc")
                at.did(act.dma_start(y2[ds(g * 128, 128), :], conv[:]), "out", 16)

            act.dma_start(vec[:], cvec).then_inc(s_zero, 16)
            groups(act, split, step)
            act.wait_ge(S["out"], 16 * (CB + 1))

        @block.gpsimd
        def _(pool):
            pool.memset(zu[:, 0:1], 0.0).then_inc(s_zero, 1)
            pool.memset(zu[:, T + 1:T + 2], 0.0).then_inc(s_zero, 1)

        @block.vector
        def _(dve):
            def split(at, m):
                at.need("w_hi", m + 1)
                at.did(dve.tensor_tensor(w_lo[m % 2][:], w[m % 2][:], w_hi[m % 2][:], ALU.subtract), "w_lo")

            def step(at, after, g):
                def tap(i):
                    return vec[:, i, ds(g, 1)]

                split(at, 2)
                for hv in range(2):
                    at.need("mm", 3 + hv)
                    at.need("gc", hv + 1)
                    at.did(dve.tensor_tensor(zu[:, half(hv, 1)], ps[2 + hv][:], gc[:, half(hv)], ALU.mult), "zu")
                split(at, 3)
                at.need("zu")
                at.prev("out")
                at.did(dve.tensor_scalar(conv[:], zu[:, 0:T], tap(0), tap(3), ALU.mult, ALU.add), "tap0")
                at.need("tap0")
                at.did(dve.scalar_tensor_tensor(conv[:], zu[:, 1:T + 1], tap(1), conv[:], ALU.mult, ALU.add), "tap1")
                at.need("tap1")
                at.did(dve.scalar_tensor_tensor(conv[:], zu[:, 2:T + 2], tap(2), conv[:], ALU.mult, ALU.add), "tap2")
                at.need("tap2")
                for hv in range(2):
                    at.need("mm", 5 + hv)
                    at.did(dve.tensor_tensor(conv[:, half(hv)], ps[hv][:], conv[:, half(hv)], ALU.mult), "gb")
                if after:
                    split(after, 0)
                for hv in range(2):
                    at.need("sig", hv + 1)
                    at.did(dve.tensor_tensor(sig[:, half(hv)], ps[2 + hv][:], sig[:, half(hv)], ALU.mult), "sil")
                if after:
                    split(after, 1)
                at.need("sil")
                at.need("gb")
                at.did(dve.tensor_tensor(conv[:], conv[:], sig[:], ALU.mult), "yc")

            dve.wait_ge(s_zero, 18)
            groups(dve, split, step)


def attention_projections(nc, h2_hi, h2_lo, w_in, qkv, gains, headsum, z_gate):
    per = dict(w0=16, w1=16, w_hi=2, w_lo=2, mm=4, sq=4, raw=4, ms=4, var=4, root=4, inv=4, norm=4)
    oper = {f"out{i}{hv}": 16 for i in range(2) for hv in range(2)}
    zper = dict(sig=4)
    with ExitStack() as c:
        sems = Semaphores(nc, c)
        def sb(n, shape, dt=F32):
            return c.enter_context(nc.sbuf_tensor(f"at_{n}", shape, dt))

        S = {n: sems.new(f"at_{n}") for n in (*per, *oper, *zper)}
        s_gain = sems.new("at_gain")
        w = [sb(f"w{i}", [128, KT, 128]) for i in range(2)]
        w_hi = [sb(f"w_hi{i}", [128, KT, 128], F32R) for i in range(2)]
        w_lo = [sb(f"w_lo{i}", [128, KT, 128], F32R) for i in range(2)]
        sq, root = ([sb(f"{n}{i}", [128, HALF]) for i in range(2)] for n in ("sq", "root"))
        out = [[sb(f"out{i}{hv}", [128, HALF]) for hv in range(2)] for i in range(2)]
        gain = sb("gain", [128, 2])
        ps = [c.enter_context(nc.psum_tensor(f"at_ps{i}", [128, HALF], F32)) for i in range(2)]
        ms = [c.enter_context(nc.psum_tensor(f"at_ms{i}", [128, HALF], F32)) for i in range(2)]
        block = c.enter_context(nc.Block())
        w_cols = w_in.rearrange("(k p) n -> p k n", p=128)
        rows = [qkv[n].rearrange("(j p) t -> j p t", p=128) for n in range(3)]
        rows.append(z_gate.rearrange("(j p) t -> j p t", p=128))
        PAIRS = CB // 2

        def half(hv):
            return slice(HALF * hv, HALF * hv + HALF)

        def n_of(i, hv):
            return 2 * i + hv + 1

        def pairs(eng):
            for kind in range(3):
                with eng.Fori(0, PAIRS) as c2:
                    t = c2 + kind * PAIRS
                    yield kind, c2, Place(eng, S, {**per, **oper}, t), Place(eng, S, per, t, lag=-1)
            for c2 in range(PAIRS):
                t = c2 + 3 * PAIRS
                yield (3, c2, Place(eng, S, {**per, **oper}, t),
                       Place(eng, S, per, t, lag=-1) if c2 + 1 < PAIRS else None)

        @block.sync
        def _(sp):
            def load(at, column, i):
                at.did(sp.dma_start(w[i][:], w_cols[:, :, ds(column, 128)]), f"w{i}", 16)

            for n in {**per, **oper, **zper}:
                sp.sem_inc(S[n], {**per, **oper, **zper}[n])
            for i in range(2):
                load(Place(sp, S, per, 0), 4 * CW + 128 * i, i)
            for kind, c2, at, after in pairs(sp):
                for i in range(2):
                    if after:
                        at.need("mm", n_of(i, 1))
                        load(after, c2 * 256 + ((4 + kind) * CW + 256 + 128 * i), i)
                    for hv in range(2):
                        at.need("norm" if kind < 2 else "raw", n_of(i, hv))
                        at.did(sp.dma_start(rows[kind][ds(c2 * 2 + i, 1), :, half(hv)]
                                            .rearrange("j p t -> p (j t)"), out[i][hv][:]), f"out{i}{hv}", 16)
            for n in oper:
                sp.wait_ge(S[n], 16 * (4 * PAIRS + 1))

        @block.tensor
        def _(pe):
            for kind, c2, at, after in pairs(pe):
                for i in range(2):
                    at.need("w_lo", i + 1)
                    for hv in range(2):
                        last_read = at.need if i else at.prev
                        last_read("raw", 2 * (1 - i) + hv + 1)
                        for k in range(KT):
                            parts = product_parts(w_hi[i], w_lo[i], h2_hi, h2_lo)
                            for n, (wp, hp) in enumerate(parts):
                                for b in range(HB):
                                    t0 = HALF * hv + 512 * b
                                    last = pe.matmul(ps[hv][:, 512 * b:512 * b + 512], wp[:, k, :],
                                                     hp[:, k, t0:t0 + 512], start=k == 0 and n == 0,
                                                     stop=k == KT - 1 and n == len(parts) - 1)
                        at.did(last, "mm")
                    if kind < 2:
                        for hv in range(2):
                            at.need("sq", n_of(i, hv))
                            (at.need if i else at.prev)("var", 2 * (1 - i) + hv + 1)
                            for b in range(HB):
                                last = pe.matmul(ms[hv][:, 512 * b:512 * b + 512], headsum,
                                                 sq[hv][:, 512 * b:512 * b + 512], start=True, stop=True)
                            at.did(last, "ms")

        @block.scalar
        def _(act):
            def split(at, i):
                at.need(f"w{i}")
                at.did(act.copy(w_hi[i][:], w[i][:]), "w_hi")

            act.dma_start(gain[:], gains).then_inc(s_gain, 16)
            split(Place(act, S, per, 0), 0)
            for kind, c2, at, after in pairs(act):
                zat = Place(act, S, zper, c2)
                for i in range(2):
                    if i == 0:
                        split(at, 1)
                    elif after:
                        split(after, 0)
                    for hv in range(2):
                        at.need("mm", n_of(i, hv))
                        if kind < 2:
                            (at.need if i else at.prev)("ms", 2 * (1 - i) + hv + 1)
                            at.did(act.activation(sq[hv][:], ps[hv][:], ACT.Square), "sq")
                        if kind < 3:
                            at.prev(f"out{i}{hv}")
                            at.did(act.copy(out[i][hv][:], ps[hv][:]), "raw")
                        else:
                            (at.need if i else at.prev)("raw", 2 * (1 - i) + hv + 1)
                            act.wait_ge(S["ms"], 4 * (2 * PAIRS + 1))
                            zat.did(act.activation(sq[hv][:], ps[hv][:], ACT.Sigmoid), "sig")
                    if kind < 2:
                        for hv in range(2):
                            at.need("var", n_of(i, hv))
                            at.did(act.activation(root[hv][:], root[hv][:], ACT.Sqrt), "root")

        @block.vector
        def _(dve):
            def split(at, i):
                at.need("w_hi", i + 1)
                at.did(dve.tensor_tensor(w_lo[i][:], w[i][:], w_hi[i][:], ALU.subtract), "w_lo")

            split(Place(dve, S, per, 0), 0)
            dve.wait_ge(s_gain, 16)
            dve.tensor_scalar(gain[:, 0:1], gain[:, 0:1], DH ** -0.5, None, ALU.mult).then_inc(s_gain, 1)
            dve.wait_ge(s_gain, 17)
            for kind, c2, at, after in pairs(dve):
                zat = Place(dve, S, zper, c2)
                for i in range(2):
                    if i == 0:
                        split(at, 1)
                    elif after:
                        split(after, 0)
                    for hv in range(2):
                        n = n_of(i, hv)
                        if kind < 2:
                            at.need("ms", n)
                            (at.need if i else at.prev)("norm", 2 * (1 - i) + hv + 1)
                            at.did(dve.tensor_scalar(root[hv][:], ms[hv][:], 1.0 / DH, EPS, ALU.mult, ALU.add), "var")
                        if kind == 3:
                            at.need("mm", n)
                            zat.need("sig", n)
                            at.prev(f"out{i}{hv}")
                            at.did(dve.tensor_tensor(out[i][hv][:], ps[hv][:], sq[hv][:], ALU.mult), "raw")
                    if kind < 2:
                        for hv in range(2):
                            n = n_of(i, hv)
                            at.need("root", n)
                            at.did(dve.reciprocal(root[hv][:], root[hv][:]), "inv")
                            at.need("inv", n)
                            at.need("raw", n)
                            d = out[i][hv][:]
                            at.did(dve.scalar_tensor_tensor(d, d, gain[:, kind:kind + 1], root[hv][:],
                                                            ALU.mult, ALU.mult), "norm")
            dve.wait_ge(S["norm"], 4 * (2 * PAIRS + 1))



DILATIONS = (1, 4, 16)
WINDOW_HALF = 64
QB = 128
BUCKETS = 32
MAX_DISTANCE = 1024
NEG = -1e30
SKEW = 383
OROW = HEADS * (DH + 2)


def bucket_constants():
    half_b = BUCKETS // 2
    exact = half_b // 2
    out = np.zeros((BUCKETS + 1, len(DILATIONS), SKEW), np.float32)
    for g, dil in enumerate(DILATIONS):
        for x in range(SKEW):
            rel = x - (SKEW // 2)
            if abs(rel) > WINDOW_HALF:
                out[BUCKETS, g, x] = 1.0
                continue
            n = abs(rel) * dil
            far = exact + int(np.float32(np.log(np.float32(max(n, 1)) / np.float32(exact)))
                              / np.float32(math.log(MAX_DISTANCE / exact)) * np.float32(half_b - exact))
            out[(half_b if rel > 0 else 0) + (n if n < exact else min(far, half_b - 1)), g, x] = 1.0
    return out


def bias_tables(nc, rel_bias, onehot, skew, table, qkv_dram, qkv):
    NG = len(DILATIONS)
    with ExitStack() as c:
        sems = Semaphores(nc, c)
        rb = c.enter_context(nc.sbuf_tensor("bt_rb", [BUCKETS + 1, HEADS], F32))
        rb_q = c.enter_context(nc.sbuf_tensor("bt_rb_q", [BUCKETS + 1, HEADS, 128], F32))
        hot = c.enter_context(nc.sbuf_tensor("bt_hot", [BUCKETS + 1, NG, SKEW], F32))
        flat = c.enter_context(nc.sbuf_tensor("bt_flat", [128, NG * HEADS, SKEW], F32))
        ps = [c.enter_context(nc.psum_tensor(f"bt_ps{i}", [128, 512], F32)) for i in range(2)]
        s_set, s_in, s_spread, s_mm, s_flat, s_table, s_qkv = (
            sems.new(f"bt_{n}") for n in ("set", "in", "spread", "mm", "flat", "table", "qkv"))
        s_skew = [sems.new(f"bt_skew{g}") for g in range(NG)]
        block = c.enter_context(nc.Block())

        @block.gpsimd
        def _(pool):
            pool.memset(rb[:], NEG).then_inc(s_set, 1)
            pool.wait_ge(s_in, 32)
            pool.tensor_copy(rb_q[:], rb[:].unsqueeze(2).to_broadcast([BUCKETS + 1, HEADS, 128])).then_inc(s_spread, 1)

        @block.sync
        def _(sp):
            sp.dma_start(hot[:], onehot).then_inc(s_in, 16)
            sp.wait_ge(s_set, 1)
            sp.dma_start(rb[0:BUCKETS, :], rel_bias).then_inc(s_in, 16)
            for g in range(NG):
                heads = slice(g * HEADS, (g + 1) * HEADS)
                sp.wait_ge(s_flat, (g + 1) * HEADS)
                rows = skew[heads].rearrange("n (p x) -> p n x", x=SKEW)
                sp.dma_start(rows, flat[:, heads, :]).then_inc(s_skew[g], 16)
            for g in range(NG):
                heads = slice(g * HEADS, (g + 1) * HEADS)
                sp.wait_ge(s_skew[g], 16)
                diag = skew[heads, QB - 1:QB - 1 + 128 * (SKEW - 1)].rearrange("n (p x) -> p n x", x=SKEW - 1)
                sp.dma_start(table[:, g, :, :], diag[:, :, 0:256]).then_inc(s_table, 16)
            sp.wait_ge(s_table, 16 * NG)

        @block.tensor
        def _(pe):
            pe.wait_ge(s_spread, 1)
            for n in range(NG * HEADS):
                if n >= 2:
                    pe.wait_ge(s_flat, n - 1)
                pe.matmul(ps[n % 2][:, 0:SKEW], rb_q[:, n % HEADS, :], hot[:, n // HEADS, :],
                          start=True, stop=True).then_inc(s_mm, 1)

        @block.scalar
        def _(act):
            for n in range(3):
                act.dma_start(qkv[n][:], qkv_dram[n].rearrange("(j p) t -> p j t", p=128)).then_inc(s_qkv, 16)
            for n in range(NG * HEADS):
                act.wait_ge(s_mm, n + 1)
                act.copy(flat[:, n, :], ps[n % 2][:, 0:SKEW]).then_inc(s_flat, 1)
            act.wait_ge(s_qkv, 48)


AT_PER = dict(stage=1, vtr=1, v_sb=1, s=4, s_red=4, neg=4, exps=4, ptr=4, p_sb=4, o=1, o_sb=1, out=16)


def window_attention(nc, qkv, table, ident, partial):
    with ExitStack() as c:
        sems = Semaphores(nc, c)
        def sb(n, shape, dt=F32):
            return c.enter_context(nc.sbuf_tensor(f"wa_{n}", shape, dt))

        S = {n: sems.new(f"wa_{n}") for n in (*AT_PER, "passed")}
        qs = [sb(f"qs{i}", [128, 4, QB]) for i in range(2)]
        ks, vs = ([sb(f"{n}{i}", [128, 4, 256]) for i in range(2)] for n in ("ks", "vs"))
        v_tok = [sb(f"v_tok{i}", [128, 2, CW]) for i in range(2)]
        sc = [sb(f"sc{i}", [128, 2, 256]) for i in range(2)]
        p = [sb(f"p{i}", [128, 2, 256]) for i in range(2)]
        pt = [sb(f"pt{i}", [128, 2, 2, 128]) for i in range(2)]
        neg = [sb(f"neg{i}", [128, HEADS]) for i in range(2)]
        ob = [sb(f"ob{i}", [128, HEADS, DH + 2]) for i in range(2)]
        V_PS = [c.enter_context(nc.psum_tensor(f"wa_vps{i}", [128, 4, 128], F32)) for i in range(2)]
        S_PS = [c.enter_context(nc.psum_tensor(f"wa_sps{i}", [128, 2, 256], F32)) for i in range(2)]
        P_PS = [c.enter_context(nc.psum_tensor(f"wa_pps{i}", [128, 2, 2, 128], F32)) for i in range(2)]
        O_PS = [c.enter_context(nc.psum_tensor(f"wa_ops{i}", [128, HEADS, DH], F32)) for i in range(2)]
        block = c.enter_context(nc.Block())
        AHEAD = 2

        def steps(eng):
            def step(t, par, g, w, col, q0, k0):
                return Place(eng, S, AT_PER, t, AHEAD), par, g, w, col, q0, k0

            yield step(0, 0, 0, 192, 64, 0, 0)
            with eng.Fori(0, 7) as i:
                for par in range(2):
                    q0 = i * 256 + (128 + 128 * par)
                    yield step(i * 2 + (1 + par), 1 - par, 0, 256, 0, q0, i * 256 + (64 + 128 * par))
            yield step(15, 1, 0, 192, 0, T - QB, T - 192)
            with eng.Fori(0, 4) as r:
                for n in range(4):
                    w, col, k0 = ((192, 64, 0), (256, 0, 64), (256, 0, 192), (192, 0, 320))[n]
                    yield step(r * 4 + (16 + n), n % 2, 1, w, col, r + 4 * QB * n, r + 4 * k0)
            with eng.Fori(0, 8) as i:
                for par in range(2):
                    yield step(i * 2 + (32 + par), par, 2, 128, 64, i * 2 + par, i * 2 + par)

        def chunks(w):
            return [(k, min(128, w - 128 * k)) for k in range(-(-w // 128))]

        def group(gi):
            return [(2 * (gi // 2) + jj, gi % 2) for jj in range(2)]

        @block.gpsimd
        def _(pool):
            for at, par, g, w, col, q0, k0 in steps(pool):
                at.settle()
                at.prev("s", 4)
                at.prev("vtr")
                pool.tensor_copy(qs[par][:], qkv[0][:, :, ds(q0, QB, step=DILATIONS[g])])
                pool.tensor_copy(ks[par][:, :, 0:w], qkv[1][:, :, ds(k0, w, step=DILATIONS[g])])
                at.did(pool.tensor_copy(vs[par][:, :, 0:w], qkv[2][:, :, ds(k0, w, step=DILATIONS[g])]), "stage")

        @block.tensor
        def _(pe):
            for at, par, g, w, col, q0, k0 in steps(pe):
                at.need("stage")
                at.prev1("v_sb")
                for k, n in chunks(w):
                    for j in range(4):
                        last = pe.transpose(V_PS[k][0:n, j, :], vs[par][:, j, 128 * k:128 * k + n], ident)
                at.did(last, "vtr")

                def scores(gi):
                    at.need("s_red", gi - 1) if gi >= 2 else at.prev1("s_red", gi + 3)
                    for jj, (j, m) in enumerate(group(gi)):
                        R = slice(DH * m, DH * m + DH)
                        last = pe.matmul(S_PS[gi % 2][:, jj, 0:w], qs[par][R, j, :], ks[par][R, j, 0:w],
                                         start=True, stop=True)
                    at.did(last, "s")

                def values(gi):
                    at.need("exps", gi + 1)
                    at.need("p_sb", gi - 1) if gi >= 2 else at.prev1("p_sb", gi + 3)
                    for jj in range(2):
                        for k, n in chunks(w):
                            last = pe.transpose(P_PS[gi % 2][0:n, jj, k, :], p[gi % 2][:, jj, 128 * k:128 * k + n],
                                                ident)
                    at.did(last, "ptr")

                def outputs(gi):
                    at.need("p_sb", gi + 1)
                    if gi == 0:
                        at.need("v_sb")
                        at.prev("o_sb")
                    for jj, (j, m) in enumerate(group(gi)):
                        for k, n in chunks(w):
                            h = 2 * j + m
                            last = pe.matmul(O_PS[par][:, h, :], pt[gi % 2][0:n, jj, k, :],
                                             v_tok[par][0:n, k, DH * h:DH * h + DH],
                                             start=k == 0, stop=k == len(chunks(w)) - 1)
                    return last

                scores(0)
                scores(1)
                for gi in range(4):
                    values(gi)
                    if gi + 2 < 4:
                        scores(gi + 2)
                    last = outputs(gi)
                at.did(last, "o")

        @block.vector
        def _(dve):
            for at, par, g, w, col, q0, k0 in steps(dve):
                def reduce(gi):
                    at.settle()
                    at.need("s", gi + 1)
                    at.need("exps", gi - 1) if gi >= 2 else at.prev1("exps", gi + 3)
                    if gi == 0:
                        at.prev("out")
                    for jj, (j, m) in enumerate(group(gi)):
                        h = 2 * j + m
                        last = dve.tensor_tensor_reduce(sc[gi % 2][:, jj, 0:w], S_PS[gi % 2][:, jj, 0:w],
                                                        table[:, g, h, col:col + w], 1.0, -3e38, ALU.add, ALU.max,
                                                        ob[par][:, h, DH:DH + 1])
                    at.did(last, "s_red")
                    at.need("s_red", gi + 1)
                    h = 2 * group(gi)[0][0] + gi % 2
                    at.did(dve.tensor_scalar(neg[par][:, h:h + 3:2], ob[par][:, h:h + 3:2, DH], -1.0, None,
                                             ALU.mult), "neg")

                def weights(gi):
                    at.need("ptr", gi + 1)
                    for k, n in chunks(w):
                        last = dve.tensor_copy(pt[gi % 2][0:n, :, k, :], P_PS[gi % 2][0:n, :, k, :])
                    at.did(last, "p_sb")

                reduce(0)
                reduce(1)
                weights(0)
                reduce(2)
                weights(1)
                reduce(3)
                weights(2)
                weights(3)

        @block.scalar
        def _(act):
            for at, par, g, w, col, q0, k0 in steps(act):
                at.need("vtr")
                for k, n in chunks(w):
                    last = act.copy(v_tok[par][0:n, k, :], V_PS[k][0:n].rearrange("p j c -> p (j c)"))
                at.did(last, "v_sb")
                for gi in range(4):
                    at.need("neg", gi + 1)
                    at.need("ptr", gi - 1) if gi >= 2 else at.prev1("ptr", gi + 3)
                    for jj, (j, m) in enumerate(group(gi)):
                        h = 2 * j + m
                        last = act.activation(p[gi % 2][:, jj, 0:w], sc[gi % 2][:, jj, 0:w], ACT.Exp,
                                              bias=neg[par][:, h:h + 1], accum_out=ob[par][:, h, DH + 1:DH + 2])
                    at.did(last, "exps")
                at.need("o")
                at.did(act.copy(ob[par][:, :, 0:DH], O_PS[par][:]), "o_sb")

        @block.sync
        def _(sp):
            for n in AT_PER:
                sp.sem_inc(S[n], AHEAD * AT_PER[n])
            for at, par, g, w, col, q0, k0 in steps(sp):
                at.need("o_sb")
                at.prev1("out")
                at.did(sp.dma_start(partial[g, ds(q0, QB, step=DILATIONS[g]), :],
                                    ob[par][:].rearrange("p h e -> p (h e)")), "out", 16)
            sp.wait_ge(S["out"], 16 * (48 + AHEAD))


MG_PER = dict(top=1, top2=1, low=1, e=1, ed=1, s1=1, s2=1, inv=1, wg=1, prod=1, o1=1, o2=1, tr=1, gated=1)


def merge_attention(nc, partial, z_gate, y2, ident):
    NG = len(DILATIONS)
    with ExitStack() as c:
        sems = Semaphores(nc, c)
        def sb(n, shape, dt=F32):
            return c.enter_context(nc.sbuf_tensor(f"mg_{n}", shape, dt))

        S = {n: sems.new(f"mg_{n}") for n in (*MG_PER, "passed")}
        in_per = dict(in0=16, in1=16, z0=16, z1=16)
        SI = {n: sems.new(f"mg_{n}") for n in in_per}
        SI["passed"] = S["passed"]
        part = [sb(f"part{i}", [128, NG, HEADS, DH + 2]) for i in range(2)]
        z = [sb(f"z{i}", [128, CB, 128]) for i in range(2)]
        prod = [sb(f"prod{i}", [128, NG, HEADS, DH]) for i in range(2)]
        top, tot, inv = sb("top", [128, HEADS]), sb("tot", [128, HEADS]), sb("inv", [128, HEADS])
        e, ed = sb("e", [128, NG, HEADS]), sb("ed", [128, NG, HEADS])
        ps = [c.enter_context(nc.psum_tensor(f"mg_ps{i}", [128, CB, 128], F32)) for i in range(2)]
        block = c.enter_context(nc.Block())
        z_view = z_gate.rearrange("(j p) t -> p j t", p=128)
        AHEAD = 2

        def tiles(eng):
            with eng.Fori(0, T // 256) as i:
                for par in range(2):
                    yield Place(eng, S, MG_PER, i * 2 + par, AHEAD), Place(eng, SI, in_per, i), par, i * 256 + 128 * par

        def spread(a, g=NG):
            return a.unsqueeze(1).to_broadcast([128, g, HEADS])

        @block.sync
        def _(sp):
            for n in MG_PER:
                sp.sem_inc(S[n], AHEAD * MG_PER[n])
            for n in in_per:
                sp.sem_inc(SI[n], in_per[n])
            for at, pin, par, t0 in tiles(sp):
                at.prev("prod")
                at.prev("ed")
                pin.did(sp.dma_start(part[par][:].rearrange("p g h e -> p g (h e)"),
                                     partial[:, ds(t0, 128), :].rearrange("g p e -> p g e")), f"in{par}", 16)
                at.settle()
                at.prev("gated")
                pin.did(sp.dma_start(z[par][:], z_view[:, :, ds(t0, 128)]), f"z{par}", 16)

        @block.scalar
        def _(act):
            for at, pin, par, t0 in tiles(act):
                at.need("low")
                at.prev1("wg")
                at.did(act.activation(e[:], ed[:], ACT.Exp), "e")

        @block.vector
        def _(dve):
            for at, pin, par, t0 in tiles(dve):
                m, d = part[par][:, :, :, DH], part[par][:, :, :, DH + 1]
                pin.need(f"in{par}")
                at.did(dve.tensor_tensor(top[:], m[:, 0, :], m[:, 1, :], ALU.max), "top")
                at.need("top")
                at.did(dve.tensor_tensor(top[:], top[:], m[:, 2, :], ALU.max), "top2")
                at.need("top2")
                at.did(dve.tensor_tensor(ed[:], m, spread(top[:]), ALU.subtract), "low")
                at.need("e")
                at.did(dve.tensor_tensor(ed[:], e[:], d, ALU.mult), "ed")
                at.need("ed")
                at.did(dve.tensor_tensor(tot[:], ed[:, 0, :], ed[:, 1, :], ALU.add), "s1")
                at.need("s1")
                at.did(dve.tensor_tensor(tot[:], tot[:], ed[:, 2, :], ALU.add), "s2")
                at.need("s2")
                at.did(dve.reciprocal(inv[:], tot[:]), "inv")
                at.need("inv")
                at.did(dve.tensor_tensor(e[:], e[:], spread(inv[:]), ALU.mult), "wg")
                at.need("wg")
                at.prev("tr")
                at.did(dve.tensor_tensor(prod[par][:], part[par][:, :, :, 0:DH],
                                         e[:].unsqueeze(3).to_broadcast([128, NG, HEADS, DH]), ALU.mult), "prod")
                at.need("tr")
                pin.need(f"z{par}")
                at.did(dve.tensor_tensor(y2[:, :, ds(t0, 128)], ps[par][:], z[par][:], ALU.mult), "gated")

        @block.gpsimd
        def _(pool):
            for at, pin, par, t0 in tiles(pool):
                at.need("prod")
                at.did(pool.tensor_tensor(prod[par][:, 0], prod[par][:, 0], prod[par][:, 1], ALU.add), "o1")
                at.need("o1")
                at.did(pool.tensor_tensor(prod[par][:, 0], prod[par][:, 0], prod[par][:, 2], ALU.add), "o2")

        @block.tensor
        def _(pe):
            for at, pin, par, t0 in tiles(pe):
                at.need("o2")
                at.prev("gated")
                for j in range(CB):
                    last = pe.transpose(ps[par][:, j, :], prod[par][:, 0, 2 * j:2 * j + 2, :]
                                        .rearrange("p h d -> p (h d)"), ident)
                at.did(last, "tr")


def build(nc, xT, vecs, consts, w_in, w_up, a_up, w_out, w_in2, cvec, gains, rel_bias, onehot, w_out2, outT,
          dbg=None):
    NG = len(DILATIONS)

    def dram(n, shape):
        if dbg and n in dbg:
            return dbg[n]
        return nc.dram_tensor(n, shape, F32, kind="Internal").ap()

    proj, yT, x2T = dram("proj", (6, D, T)), dram("yT", (D, T)), dram("x2T", (D, T))
    y_conv, z_gate = dram("y_conv", (CW, T)), dram("z_gate", (CW, T))
    qkv_dram = dram("qkv_dram", (3, CW, T))
    skew, partial = dram("skew", (NG * HEADS, 128 * SKEW)), dram("partial", (NG, T, OROW))
    with ExitStack() as c:
        sems = Semaphores(nc, c)
        vec = c.enter_context(nc.sbuf_tensor("vec", [128, NVEC], F32))
        basic = c.enter_context(nc.sbuf_tensor("basic", [128, 256], F32))
        ones = c.enter_context(nc.sbuf_tensor("ones", [128, 128], F32))
        s_const = sems.new("s_const")
        with nc.Block() as block:
            @block.sync
            def _(sp):
                sp.dma_start(vec[:], vecs).then_inc(s_const, 16)
                sp.dma_start(basic[:], consts[:, 0:256]).then_inc(s_const, 16)
                sp.wait_ge(s_const, 33)

            @block.gpsimd
            def _(pool):
                pool.memset(ones[:], 1.0).then_inc(s_const, 1)
        ident, headsum = basic[:, 0:128], basic[:, 128:256]
        with ExitStack() as c1:
            h = c1.enter_context(nc.sbuf_tensor("h", [128, KT, T + 1], F32))
            s_zero = Semaphores(nc, c1).new("s_zero")
            with nc.Block() as block:
                @block.gpsimd
                def _(pool):
                    pool.memset(h[:, :, 0:1], 0.0).then_inc(s_zero, 1)
                    pool.wait_ge(s_zero, 1)
            norm_phase(nc, "n1", xT.rearrange("(k p) t -> p k t", p=128), h[:, :, 1:T + 1],
                       vec[:, V["norm1"]:V["norm1"] + KT], ones)
            rwkv_projections(nc, h, vec, w_in, proj)
            rwkv_low_rank(nc, h, vec, w_in, w_up, a_up, proj)
        rwkv_recurrence(nc, proj, yT, vec, consts)
        output_projection(nc, "o1", yT, None, w_out, xT, x2T)
        with ExitStack() as c3:
            with ExitStack() as c4:
                h2_hi, h2_lo = (c4.enter_context(nc.sbuf_tensor(n, [128, KT, T], F32R)) for n in ("h2_hi", "h2_lo"))
                split_norm_phase(nc, "n2", x2T.rearrange("(k p) t -> p k t", p=128), h2_hi, h2_lo,
                                 vec[:, V["norm2"]:V["norm2"] + KT], ones)
                conv_branch(nc, h2_hi, h2_lo, w_in2, cvec, y_conv)
                attention_projections(nc, h2_hi, h2_lo, w_in2, qkv_dram, gains, headsum, z_gate)
            table = c3.enter_context(nc.sbuf_tensor("table", [128, NG, HEADS, 256], F32))
            qkv = [c3.enter_context(nc.sbuf_tensor(f"qkv{i}", [128, CB, T], F32)) for i in range(3)]
            bias_tables(nc, rel_bias, onehot, skew, table, qkv_dram, qkv)
            window_attention(nc, qkv, table, ident, partial)
        with ExitStack() as c4:
            y2 = c4.enter_context(nc.sbuf_tensor("y2", [128, CB, T], F32))
            merge_attention(nc, partial, z_gate, y2, ident)
            output_projection(nc, "o2", y_conv, y2, w_out2, x2T, outT)


def kernel(**inputs):
    import concourse.bacc as bacc
    from concourse.bass_utils import run_bass_kernel_spmd

    a = {k: np.asarray(v) for k, v in inputs.items()}
    order = [a["l0_norm"], *(a["l0_mu"][i] for i in (0, 2, 3, 5, 1, 4)), a["l0_w0"], a["l0_a0"], a["l0_k_k"],
             a["l0_k_a"], a["l0_r_k"].reshape(-1), a["l0_gn_w"], a["l0_gn_b"], a["norm_w_2"]]
    conv = np.concatenate([a["conv_w_2"], a["conv_b_2"][None]])
    arrays = dict(
        xT=a["x"][0].T,
        vecs=np.stack(order).reshape(-1, KT, 128).transpose(2, 0, 1).reshape(128, -1),
        consts=shape_constants(),
        w_in=a["l0_w_in"], w_up=a["l0_w_up"], a_up=a["l0_a_up"], w_out=a["l0_w_out"], w_in2=a["w_in_2"],
        cvec=conv.reshape(4, CB, 128).transpose(2, 0, 1),
        gains=np.stack([np.tile(a["q_norm_w_2"], 2), np.tile(a["k_norm_w_2"], 2)], 1),
        rel_bias=a["rel_bias_2"], onehot=bucket_constants(), w_out2=a["w_out_2"],
    )
    arrays = {k: np.ascontiguousarray(v) for k, v in arrays.items()}
    nc = bacc.Bacc("TRN2", target_bir_lowering=False, num_devices=1)
    aps = {k: nc.dram_tensor(k, v.shape, F32, kind="ExternalInput").ap() for k, v in arrays.items()}
    outT = nc.dram_tensor("outT", (D, T), F32, kind="ExternalOutput").ap()
    build(nc, **aps, outT=outT)
    r = run_bass_kernel_spmd(nc, [arrays], core_ids=[0])
    return np.ascontiguousarray(r.results[0]["outT"].T)[None]
```
